# Optimizing a Trainium2 kernel written in Bass

```python
import jax, jax.numpy as jnp
from jax import lax
import numpy as np
import math

D_MODEL = 2048
BATCH = 1
SEQ = 256
DEPTH = 2

HEAD_DIM = 128
EPS = 1e-6
DN_QK_HEADS = 8
DN_V_HEADS = 16
DN_DK = 128
DN_DV = 128
DN_CONV = 4
DN_CHUNK = 64
SW_HEADS = 8
SW_PATTERNS = ((128, 1), (512, 4), (2048, 16))
SW_GROUPS = 3
SW_BLOCK = 128
ROPE_THETA = 500000.0
ROPE_DIM = HEAD_DIM // 4
SC_WIDTH = 3072
SC_CONV = 3

A_Q = DN_QK_HEADS * DN_DK
A_K = DN_QK_HEADS * DN_DK
A_V = DN_V_HEADS * DN_DV
A_Z = A_V
B_Q = SW_GROUPS * SW_HEADS * HEAD_DIM
B_K = SW_HEADS * HEAD_DIM
B_V = SW_HEADS * HEAD_DIM
B_Z = B_V
HYB_IN = A_Q + A_K + A_V + A_Z + 2 * DN_V_HEADS + B_Q + B_K + B_V + B_Z
HYB_MIX = A_V + B_V
N_EVEN = (DEPTH + 1) // 2
N_ODD = DEPTH // 2


def rmsnorm(x, w):
    xf = x.astype(jnp.float32)
    y = xf * lax.rsqrt(jnp.mean(xf * xf, axis=-1, keepdims=True) + EPS)
    return (y * w.astype(jnp.float32)).astype(x.dtype)

def causal_depthwise_conv(x, w):
    k = w.shape[1]
    rhs = jnp.transpose(w)[:, None, :].astype(x.dtype)
    return lax.conv_general_dilated(x, rhs, window_strides=(1,), padding=[(k - 1, 0)],
                                    dimension_numbers=('NWC', 'WIO', 'NWC'),
                                    feature_group_count=x.shape[-1])

def partial_rope(x, pos):
    half = ROPE_DIM // 2
    inv = jnp.power(jnp.float32(ROPE_THETA), -jnp.arange(half, dtype=jnp.float32) * 2.0 / ROPE_DIM)
    ang = pos.astype(jnp.float32)[:, None] * inv[None, :]
    cos = jnp.cos(ang)[None, :, None, :]
    sin = jnp.sin(ang)[None, :, None, :]
    x1 = x[..., :half]
    x2 = x[..., half:ROPE_DIM]
    return jnp.concatenate([x1 * cos - x2 * sin, x2 * cos + x1 * sin, x[..., ROPE_DIM:]], axis=-1)

def l2norm(x):
    return x * lax.rsqrt(jnp.sum(x * x, axis=-1, keepdims=True) + EPS)

def gated_delta_chunked(q, k, v, beta, g):
    b, s, h, dk = q.shape
    dv = v.shape[-1]
    n = s // DN_CHUNK
    c = DN_CHUNK

    def chunks(t):
        return t.reshape(b, n, c, h, t.shape[-1]).transpose(0, 1, 3, 2, 4)

    q, k, v = chunks(q), chunks(k), chunks(v)
    beta = beta.reshape(b, n, c, h).transpose(0, 1, 3, 2)
    g = jnp.cumsum(g.reshape(b, n, c, h).transpose(0, 1, 3, 2), axis=-1)
    idx = jnp.arange(c)
    causal = idx[:, None] >= idx[None, :]
    strict = idx[:, None] > idx[None, :]
    diff = g[..., :, None] - g[..., None, :]
    decay = jnp.exp(jnp.where(causal, diff, -jnp.inf))
    kk = jnp.einsum('bnhik,bnhjk->bnhij', k, k)
    a_strict = jnp.where(strict, beta[..., :, None] * kk * decay, 0.0)
    rhs = jnp.concatenate([v * beta[..., None], k * (beta * jnp.exp(g))[..., None]], axis=-1)
    sol = lax.linalg.triangular_solve(a_strict, rhs, left_side=True, lower=True, unit_diagonal=True)
    u = sol[..., :dv]
    w = sol[..., dv:]
    qk = jnp.einsum('bnhik,bnhjk->bnhij', q, k) * decay

    def step(state, inp):
        q_c, k_c, u_c, w_c, g_c, qk_c = inp
        v_new = u_c - jnp.einsum('bhck,bhkv->bhcv', w_c, state)
        o = jnp.einsum('bhck,bhkv->bhcv', q_c * jnp.exp(g_c)[..., None], state) + \
            jnp.einsum('bhij,bhjv->bhiv', qk_c, v_new)
        g_last = g_c[..., -1]
        state = state * jnp.exp(g_last)[..., None, None] + jnp.einsum(
            'bhck,bhcv->bhkv', k_c * jnp.exp(g_last[..., None] - g_c)[..., None], v_new)
        return state, o

    xs = tuple(jnp.moveaxis(t, 1, 0) for t in (q, k, u, w, g, qk))
    state0 = jnp.zeros((b, h, dk, dv), jnp.float32)
    _, o = lax.scan(step, state0, xs)
    return o.transpose(1, 0, 3, 2, 4).reshape(b, s, h, dv)

def dilated_window_group(q, k, v, dil):
    b, s, h, dh = q.shape
    wb = SW_BLOCK
    ln = s // dil
    nb = -(-ln // wb)
    lp = nb * wb

    def strided(t):
        t = t.reshape(b, ln, dil, h, dh).transpose(0, 2, 3, 1, 4)
        t = jnp.pad(t, ((0, 0), (0, 0), (0, 0), (0, lp - ln), (0, 0)))
        return t.reshape(b, dil, h, nb, wb, dh)

    def with_prev(t):
        prev = jnp.concatenate([jnp.zeros_like(t[:, :, :, :1]), t[:, :, :, :-1]], axis=3)
        return jnp.concatenate([prev, t], axis=4)

    qs = strided(q)
    kb = with_prev(strided(k))
    vb = with_prev(strided(v))
    sc = jnp.einsum('brhnqc,brhnkc->brhnqk', qs, kb) * (dh ** -0.5)
    i = jnp.arange(wb)[:, None]
    j = jnp.arange(2 * wb)[None, :]
    dist = i + wb - j
    blk = jnp.arange(nb)[:, None, None]
    valid = (dist >= 0) & (dist <= wb) & (blk * wb - wb + j >= 0)
    sc = jnp.where(valid, sc, -jnp.inf)
    m = jnp.max(sc, axis=-1, keepdims=True)
    p = jnp.exp(sc - m)
    den = jnp.sum(p, axis=-1)
    num = jnp.einsum('brhnqk,brhnkc->brhnqc', p, vb)

    def unstride(t):
        rest = t.shape[5:]
        t = t.reshape((b, dil, h, lp) + rest)[:, :, :, :ln]
        return jnp.moveaxis(t, 3, 1).reshape((b, s, h) + rest)

    return unstride(num), unstride(den), unstride(m[..., 0])

def dilated_attention(q, k, v):
    nums, dens, maxs = [], [], []
    for gi, (window, dil) in enumerate(SW_PATTERNS):
        n_, d_, m_ = dilated_window_group(q[:, :, gi], k, v, dil)
        nums.append(n_)
        dens.append(d_)
        maxs.append(m_)
    mx = jnp.max(jnp.stack(maxs), axis=0)
    wts = [jnp.exp(m_ - mx) for m_ in maxs]
    num = sum(w_[..., None] * n_ for w_, n_ in zip(wts, nums))
    den = sum(w_ * d_ for w_, d_ in zip(wts, dens))
    return num / den[..., None]

def hybrid_layer(h, w_in, conv_w, a_log, dt_bias, dn_norm_w, w_out, pos):
    b, s, _ = h.shape
    f32 = jnp.float32
    proj = h @ w_in
    sizes = [A_Q, A_K, A_V, A_Z, DN_V_HEADS, DN_V_HEADS, B_Q, B_K, B_V, B_Z]
    offs = []
    acc = 0
    for sz in sizes[:-1]:
        acc += sz
        offs.append(acc)
    aq, ak, av, az, ab, aa, bq, bk, bv, bz = jnp.split(proj, offs, axis=-1)

    qkv = jax.nn.silu(causal_depthwise_conv(jnp.concatenate([aq, ak, av], axis=-1), conv_w)).astype(f32)
    q_a = l2norm(qkv[..., :A_Q].reshape(b, s, DN_QK_HEADS, DN_DK)) * (DN_DK ** -0.5)
    k_a = l2norm(qkv[..., A_Q:A_Q + A_K].reshape(b, s, DN_QK_HEADS, DN_DK))
    v_a = qkv[..., A_Q + A_K:].reshape(b, s, DN_V_HEADS, DN_DV)
    rep = DN_V_HEADS // DN_QK_HEADS
    q_a = jnp.repeat(q_a, rep, axis=2)
    k_a = jnp.repeat(k_a, rep, axis=2)
    beta = jax.nn.sigmoid(ab.astype(f32))
    g = -jnp.exp(a_log.astype(f32)) * jax.nn.softplus(aa.astype(f32) + dt_bias.astype(f32))
    o_a = gated_delta_chunked(q_a, k_a, v_a, beta, g)
    o_a = o_a * lax.rsqrt(jnp.mean(o_a * o_a, axis=-1, keepdims=True) + EPS) * dn_norm_w.astype(f32)
    y_a = (o_a.reshape(b, s, A_V) * jax.nn.silu(az.astype(f32))).astype(h.dtype)

    q_b = partial_rope(bq.astype(f32).reshape(b, s, SW_GROUPS * SW_HEADS, HEAD_DIM), pos)
    q_b = q_b.reshape(b, s, SW_GROUPS, SW_HEADS, HEAD_DIM)
    k_b = partial_rope(bk.astype(f32).reshape(b, s, SW_HEADS, HEAD_DIM), pos)
    v_b = bv.astype(f32).reshape(b, s, SW_HEADS, HEAD_DIM)
    o_b = dilated_attention(q_b, k_b, v_b)
    y_b = (o_b.reshape(b, s, B_V) * jax.nn.silu(bz.astype(f32))).astype(h.dtype)

    return jnp.concatenate([y_a, y_b], axis=-1) @ w_out

def shortconv_layer(h, w_in, conv_w, w_out):
    gate_b, gate_c, u, z = jnp.split(h @ w_in, 4, axis=-1)
    y = gate_b * causal_depthwise_conv(gate_c * u, conv_w)
    return (y * jax.nn.silu(z)) @ w_out

def first_inputs(seed: int = 0) -> dict:
    key = jax.random.key(seed)
    ks = jax.random.split(key, 14)
    f32 = jnp.float32

    def nrm(k, shape, scale):
        return jax.random.normal(k, shape, f32) * scale

    x = nrm(ks[0], (BATCH, SEQ, D_MODEL), 1.0)
    norm_w = 1.0 + nrm(ks[1], (DEPTH, D_MODEL), 0.05)
    hyb_w_in = nrm(ks[2], (N_EVEN, D_MODEL, HYB_IN), D_MODEL ** -0.5)
    dn_conv_w = nrm(ks[3], (N_EVEN, A_Q + A_K + A_V, DN_CONV), DN_CONV ** -0.5)
    dn_a_log = jnp.log(jax.random.uniform(ks[4], (N_EVEN, DN_V_HEADS), f32, 1.0, 16.0))
    dt = jnp.exp(jax.random.uniform(ks[5], (N_EVEN, DN_V_HEADS), f32, jnp.log(1e-3), jnp.log(1e-1)))
    dn_dt_bias = dt + jnp.log(-jnp.expm1(-dt))
    dn_norm_w = 1.0 + nrm(ks[6], (N_EVEN, DN_DV), 0.05)
    hyb_w_out = nrm(ks[7], (N_EVEN, HYB_MIX, D_MODEL), HYB_MIX ** -0.5)
    sc_w_in = nrm(ks[8], (N_ODD, D_MODEL, 4 * SC_WIDTH), D_MODEL ** -0.5)
    sc_conv_w = nrm(ks[9], (N_ODD, SC_WIDTH, SC_CONV), SC_CONV ** -0.5)
    sc_w_out = nrm(ks[10], (N_ODD, SC_WIDTH, D_MODEL), SC_WIDTH ** -0.5)
    final_norm_w = 1.0 + nrm(ks[11], (D_MODEL,), 0.05)
    return {"x": x, "norm_w": norm_w, "hyb_w_in": hyb_w_in, "dn_conv_w": dn_conv_w,
            "dn_a_log": dn_a_log, "dn_dt_bias": dn_dt_bias, "dn_norm_w": dn_norm_w,
            "hyb_w_out": hyb_w_out, "sc_w_in": sc_w_in, "sc_conv_w": sc_conv_w,
            "sc_w_out": sc_w_out, "final_norm_w": final_norm_w}

def first_block(x, norm_w, hyb_w_in, dn_conv_w, dn_a_log, dn_dt_bias, dn_norm_w, hyb_w_out,
              sc_w_in, sc_conv_w, sc_w_out, final_norm_w):
    pos = jnp.arange(x.shape[1], dtype=jnp.int32)
    h = x
    for layer in range(DEPTH):
        hn = rmsnorm(h, norm_w[layer])
        li = layer // 2
        if layer % 2 == 0:
            h = h + hybrid_layer(hn, hyb_w_in[li], dn_conv_w[li], dn_a_log[li], dn_dt_bias[li],
                                 dn_norm_w[li], hyb_w_out[li], pos)
        else:
            h = h + shortconv_layer(hn, sc_w_in[li], sc_conv_w[li], sc_w_out[li])
    return rmsnorm(h, final_norm_w)


DEPTH_2 = 1

SSM_WIDTH = D_MODEL // 2
SSM_GROUP = 16
SSM_GROUPS = SSM_WIDTH // SSM_GROUP
SSM_STATE = 64
DT_MIN = 0.001
DT_MAX = 0.1
ATTN_HEADS = 8
ATTN_WIDTH = ATTN_HEADS * HEAD_DIM
MOBA_BLOCK = 256
MOBA_TOPK = 3
Q_BLOCK = 128
REL_BUCKETS = 32
REL_MAX_DIST = 128
D_FF = 4 * D_MODEL
N_MOD = 6
NEG_INF = -1e30
IN_WIDTH = SSM_WIDTH + 3 * ATTN_WIDTH + 2 * D_MODEL


def rms_norm(x, g):
    x32 = x.astype(jnp.float32)
    y = x32 * lax.rsqrt(jnp.mean(x32 * x32, axis=-1, keepdims=True) + EPS)
    return (y * g.astype(jnp.float32)).astype(x.dtype)

def _ssm_combine(lhs, rhs):
    a_re1, a_im1, b_re1, b_im1 = lhs
    a_re2, a_im2, b_re2, b_im2 = rhs
    a_re = a_re2 * a_re1 - a_im2 * a_im1
    a_im = a_re2 * a_im1 + a_im2 * a_re1
    b_re = a_re2 * b_re1 - a_im2 * b_im1 + b_re2
    b_im = a_re2 * b_im1 + a_im2 * b_re1 + b_im2
    return (a_re, a_im, b_re, b_im)

def s5_branch(u, a_re, a_im, log_dt, b_re, b_im, c_re, c_im, d_skip, w_glu, b_glu):
    bsz, seq_len, _ = u.shape
    f32 = jnp.float32
    u32 = u.astype(f32).reshape(bsz, seq_len, SSM_GROUPS, SSM_GROUP)
    a_re = a_re.astype(f32)
    a_im = a_im.astype(f32)
    dt = jnp.exp(log_dt.astype(f32))[:, None]
    mag = jnp.exp(dt * a_re)
    abar_re = mag * jnp.cos(dt * a_im)
    abar_im = mag * jnp.sin(dt * a_im)
    den = a_re * a_re + a_im * a_im
    p_re = abar_re - 1.0
    f_re = (p_re * a_re + abar_im * a_im) / den
    f_im = (abar_im * a_re - p_re * a_im) / den
    b_re = b_re.astype(f32)
    b_im = b_im.astype(f32)
    bbar_re = f_re[..., None] * b_re - f_im[..., None] * b_im
    bbar_im = f_re[..., None] * b_im + f_im[..., None] * b_re
    bu_re = jnp.einsum('blgp,gnp->blgn', u32, bbar_re)
    bu_im = jnp.einsum('blgp,gnp->blgn', u32, bbar_im)
    a_seq_re = jnp.broadcast_to(abar_re, bu_re.shape)
    a_seq_im = jnp.broadcast_to(abar_im, bu_im.shape)
    _, _, s_re, s_im = lax.associative_scan(
        _ssm_combine, (a_seq_re, a_seq_im, bu_re, bu_im), axis=1)
    y = (jnp.einsum('blgn,gpn->blgp', s_re, c_re.astype(f32))
         - jnp.einsum('blgn,gpn->blgp', s_im, c_im.astype(f32)))
    y = y.reshape(bsz, seq_len, SSM_WIDTH) + d_skip.astype(f32) * u32.reshape(bsz, seq_len, SSM_WIDTH)
    y = jax.nn.gelu(y).astype(u.dtype)
    return y * jax.nn.sigmoid(y @ w_glu + b_glu)

def t5_bucket(rel):
    n = jnp.maximum(rel, 0)
    max_exact = REL_BUCKETS // 2
    nf = jnp.maximum(n, 1).astype(jnp.float32)
    large = max_exact + (jnp.log(nf / max_exact) / math.log(REL_MAX_DIST / max_exact)
                         * (REL_BUCKETS - max_exact)).astype(jnp.int32)
    large = jnp.minimum(large, REL_BUCKETS - 1)
    return jnp.where(n < max_exact, n, large)

def moba_attention(q, k, v, rel_bias):
    bsz, seq_len = q.shape[0], q.shape[1]
    n_blk = -(-seq_len // MOBA_BLOCK)
    pad = n_blk * MOBA_BLOCK - seq_len
    n_sel = min(MOBA_TOPK, n_blk - 1)
    q = q.transpose(0, 2, 1, 3)
    k = jnp.pad(k.transpose(0, 2, 1, 3), ((0, 0), (0, 0), (0, pad), (0, 0)))
    v = jnp.pad(v.transpose(0, 2, 1, 3), ((0, 0), (0, 0), (0, pad), (0, 0)))
    kb = k.reshape(bsz, ATTN_HEADS, n_blk, MOBA_BLOCK, HEAD_DIM)
    vb = v.reshape(bsz, ATTN_HEADS, n_blk, MOBA_BLOCK, HEAD_DIM)
    kmean = jnp.mean(kb.astype(jnp.float32), axis=3).astype(k.dtype)
    bias_table = rel_bias.T
    head_ix = jnp.arange(ATTN_HEADS)
    n_qblk = seq_len // Q_BLOCK
    scale = HEAD_DIM ** -0.5
    blk_off = jnp.arange(MOBA_BLOCK)

    def one_block(i):
        b = i // n_qblk
        q0 = (i % n_qblk) * Q_BLOCK
        own = q0 // MOBA_BLOCK
        qc = lax.dynamic_slice_in_dim(lax.dynamic_index_in_dim(q, b, 0, keepdims=False),
                                      q0, Q_BLOCK, axis=1)
        kb_b = lax.dynamic_index_in_dim(kb, b, 0, keepdims=False)
        vb_b = lax.dynamic_index_in_dim(vb, b, 0, keepdims=False)
        q_pos = q0 + jnp.arange(Q_BLOCK)
        k_own = lax.dynamic_index_in_dim(kb_b, own, 1, keepdims=False)
        v_own = lax.dynamic_index_in_dim(vb_b, own, 1, keepdims=False)
        rel_own = q_pos[:, None] - (own * MOBA_BLOCK + blk_off)[None, :]
        s_own = (jnp.einsum('hqd,hsd->hqs', qc, k_own).astype(jnp.float32) * scale
                 + bias_table[:, t5_bucket(rel_own)].astype(jnp.float32))
        s_own = jnp.where(rel_own[None] >= 0, s_own, NEG_INF)
        if n_sel == 0:
            p = jax.nn.softmax(s_own, axis=-1).astype(v.dtype)
            return jnp.einsum('hqs,hsd->hqd', p, v_own)
        gate = jnp.einsum('hqd,hnd->hqn', qc, kmean[b]).astype(jnp.float32)
        gate = jnp.where(jnp.arange(n_blk) < own, gate, NEG_INF)
        _, sel = lax.top_k(gate, n_sel)
        valid = jnp.arange(n_sel) < own
        kg = kb_b[head_ix[:, None, None], sel]
        vg = vb_b[head_ix[:, None, None], sel]
        rel_sel = q_pos[None, :, None, None] - (sel[..., None] * MOBA_BLOCK + blk_off)
        s_sel = (jnp.einsum('hqd,hqksd->hqks', qc, kg).astype(jnp.float32) * scale
                 + bias_table[head_ix[:, None, None, None], t5_bucket(rel_sel)].astype(jnp.float32))
        s_sel = jnp.where(valid[None, None, :, None], s_sel, NEG_INF)
        s = jnp.concatenate([s_sel.reshape(ATTN_HEADS, Q_BLOCK, n_sel * MOBA_BLOCK), s_own], axis=-1)
        p = jax.nn.softmax(s, axis=-1).astype(v.dtype)
        p_sel = p[..., :n_sel * MOBA_BLOCK].reshape(ATTN_HEADS, Q_BLOCK, n_sel, MOBA_BLOCK)
        return (jnp.einsum('hqks,hqksd->hqd', p_sel, vg)
                + jnp.einsum('hqs,hsd->hqd', p[..., n_sel * MOBA_BLOCK:], v_own))

    o = lax.map(one_block, jnp.arange(bsz * n_qblk))
    o = o.reshape(bsz, n_qblk, ATTN_HEADS, Q_BLOCK, HEAD_DIM).transpose(0, 1, 3, 2, 4)
    return o.reshape(bsz, seq_len, ATTN_WIDTH)

def second_inputs(seed: int = 0) -> dict:
    key = jax.random.key(seed)
    ks = jax.random.split(key, 24)
    f32 = jnp.float32
    nrm = lambda k, shape, s: jax.random.normal(k, shape, f32) * s
    n_idx = jnp.arange(SSM_STATE, dtype=f32)
    a_re = -0.5 + nrm(ks[4], (DEPTH_2, SSM_GROUPS, SSM_STATE), 0.01)
    a_im = math.pi * n_idx + nrm(ks[5], (DEPTH_2, SSM_GROUPS, SSM_STATE), 0.01)
    log_dt = jax.random.uniform(ks[6], (DEPTH_2, SSM_GROUPS), f32,
                                math.log(DT_MIN), math.log(DT_MAX))
    return {
        "x": nrm(ks[0], (BATCH, SEQ, D_MODEL), 1.0),
        "c": nrm(ks[1], (BATCH, D_MODEL), 1.0),
        "rel_bias": nrm(ks[2], (REL_BUCKETS, ATTN_HEADS), 0.5),
        "w_ada": nrm(ks[3], (DEPTH_2, D_MODEL, N_MOD * D_MODEL), 0.5 * D_MODEL ** -0.5),
        "b_ada": nrm(ks[7], (DEPTH_2, N_MOD * D_MODEL), 0.02),
        "norm_mix_g": 1.0 + nrm(ks[8], (DEPTH_2, D_MODEL), 0.02),
        "w_in": nrm(ks[9], (DEPTH_2, D_MODEL, IN_WIDTH), D_MODEL ** -0.5),
        "ssm_a_re": a_re,
        "ssm_a_im": a_im,
        "ssm_log_dt": log_dt,
        "ssm_b_re": nrm(ks[10], (DEPTH_2, SSM_GROUPS, SSM_STATE, SSM_GROUP), (2 * SSM_GROUP) ** -0.5),
        "ssm_b_im": nrm(ks[11], (DEPTH_2, SSM_GROUPS, SSM_STATE, SSM_GROUP), (2 * SSM_GROUP) ** -0.5),
        "ssm_c_re": nrm(ks[12], (DEPTH_2, SSM_GROUPS, SSM_GROUP, SSM_STATE), (2 * SSM_STATE) ** -0.5),
        "ssm_c_im": nrm(ks[13], (DEPTH_2, SSM_GROUPS, SSM_GROUP, SSM_STATE), (2 * SSM_STATE) ** -0.5),
        "ssm_d": nrm(ks[14], (DEPTH_2, SSM_WIDTH), 1.0),
        "w_glu": nrm(ks[15], (DEPTH_2, SSM_WIDTH, SSM_WIDTH), SSM_WIDTH ** -0.5),
        "b_glu": nrm(ks[16], (DEPTH_2, SSM_WIDTH), 0.02),
        "w_proj_ssm": nrm(ks[17], (DEPTH_2, SSM_WIDTH, D_MODEL), SSM_WIDTH ** -0.5),
        "w_proj_attn": nrm(ks[18], (DEPTH_2, ATTN_WIDTH, D_MODEL), ATTN_WIDTH ** -0.5),
        "w_out": nrm(ks[19], (DEPTH_2, D_MODEL, D_MODEL), D_MODEL ** -0.5),
        "norm_mlp_g": 1.0 + nrm(ks[20], (DEPTH_2, D_MODEL), 0.02),
        "w_ff1": nrm(ks[21], (DEPTH_2, D_MODEL, D_FF), D_MODEL ** -0.5),
        "w_ff2": nrm(ks[22], (DEPTH_2, D_FF, D_MODEL), D_FF ** -0.5),
        "norm_final_g": 1.0 + nrm(ks[23], (D_MODEL,), 0.02),
    }

def second_block(x, c, rel_bias, w_ada, b_ada, norm_mix_g, w_in, ssm_a_re, ssm_a_im, ssm_log_dt,
              ssm_b_re, ssm_b_im, ssm_c_re, ssm_c_im, ssm_d, w_glu, b_glu, w_proj_ssm,
              w_proj_attn, w_out, norm_mlp_g, w_ff1, w_ff2, norm_final_g):
    bsz, seq_len, _ = x.shape
    split_at = [SSM_WIDTH, SSM_WIDTH + ATTN_WIDTH, SSM_WIDTH + 2 * ATTN_WIDTH,
                SSM_WIDTH + 3 * ATTN_WIDTH, SSM_WIDTH + 3 * ATTN_WIDTH + D_MODEL]
    c_act = jax.nn.silu(c)
    for l in range(DEPTH_2):
        mod = c_act @ w_ada[l] + b_ada[l]
        sh1, sc1, g1, sh2, sc2, g2 = [m[:, None, :] for m in jnp.split(mod, N_MOD, axis=-1)]
        h = rms_norm(x, norm_mix_g[l]) * (1.0 + sc1) + sh1
        proj = h @ w_in[l]
        u, q, k, v, ga, gb = jnp.split(proj, split_at, axis=-1)
        y_ssm = s5_branch(u, ssm_a_re[l], ssm_a_im[l], ssm_log_dt[l], ssm_b_re[l], ssm_b_im[l],
                          ssm_c_re[l], ssm_c_im[l], ssm_d[l], w_glu[l], b_glu[l])
        shp = (bsz, seq_len, ATTN_HEADS, HEAD_DIM)
        y_att = moba_attention(q.reshape(shp), k.reshape(shp), v.reshape(shp), rel_bias)
        merged = (jax.nn.sigmoid(ga) * (y_ssm @ w_proj_ssm[l])
                  + jax.nn.sigmoid(gb) * (y_att @ w_proj_attn[l]))
        x = x + g1 * (merged @ w_out[l])
        h2 = rms_norm(x, norm_mlp_g[l]) * (1.0 + sc2) + sh2
        x = x + g2 * (jnp.square(jax.nn.relu(h2 @ w_ff1[l])) @ w_ff2[l])
    return rms_norm(x, norm_final_g)


def setup_inputs(seed=0):
    out = dict(first_inputs(seed))
    for name, value in second_inputs(seed + 1).items():
        if name != "x":
            out[name + "_2"] = value
    return out


def reference(
    x, norm_w, hyb_w_in, dn_conv_w, dn_a_log, dn_dt_bias, dn_norm_w, hyb_w_out, sc_w_in,
    sc_conv_w, sc_w_out, final_norm_w, c_2, rel_bias_2, w_ada_2, b_ada_2, norm_mix_g_2, w_in_2,
    ssm_a_re_2, ssm_a_im_2, ssm_log_dt_2, ssm_b_re_2, ssm_b_im_2, ssm_c_re_2, ssm_c_im_2,
    ssm_d_2, w_glu_2, b_glu_2, w_proj_ssm_2, w_proj_attn_2, w_out_2, norm_mlp_g_2, w_ff1_2,
    w_ff2_2, norm_final_g_2,
):
    x = first_block(
        x, norm_w, hyb_w_in, dn_conv_w, dn_a_log, dn_dt_bias, dn_norm_w, hyb_w_out, sc_w_in,
        sc_conv_w, sc_w_out, final_norm_w,
    )
    return second_block(
        x, c_2, rel_bias_2, w_ada_2, b_ada_2, norm_mix_g_2, w_in_2, ssm_a_re_2, ssm_a_im_2,
        ssm_log_dt_2, ssm_b_re_2, ssm_b_im_2, ssm_c_re_2, ssm_c_im_2, ssm_d_2, w_glu_2, b_glu_2,
        w_proj_ssm_2, w_proj_attn_2, w_out_2, norm_mlp_g_2, w_ff1_2, w_ff2_2, norm_final_g_2,
    )


_drawn_inputs = setup_inputs


def setup_inputs(seed=0):
    import zlib

    import numpy as np

    out = dict(_drawn_inputs(seed))
    spreads = {}
    factors = {'rel_bias_2': 3.609,
     'norm_mix_g_2': 8.0,
     'ssm_a_re_2': 64.0,
     'ssm_a_im_2': 64.0,
     'ssm_log_dt_2': 64.0,
     'ssm_b_re_2': 64.0,
     'ssm_b_im_2': 64.0,
     'ssm_c_re_2': 64.0,
     'ssm_c_im_2': 64.0,
     'w_glu_2': 2.712,
     'b_glu_2': 61.92,
     'norm_mlp_g_2': 6.132,
     'norm_final_g_2': 7.811}
    for name, (base, spread) in spreads.items():
        noise = np.random.default_rng([zlib.crc32(name.encode()), seed]).standard_normal(out[name].shape)
        drawn = base * np.exp(spread * noise) if base else spread * noise
        out[name] = __import__('jax').numpy.asarray(drawn.astype(out[name].dtype))
    for name, factor in factors.items():
        out[name] = (out[name] * factor).astype(out[name].dtype)
    return out
```

```python
import math

import numpy as np

import concourse.bass as bass
from concourse import mybir

P = 128
T = 256
D = 2048
KC = D // P
EPS = 1e-6
NEG = -1e30

F32 = mybir.dt.float32
F32R = mybir.dt.float32r
ALU = mybir.AluOpType
ACT = mybir.ActivationFunctionType
AX = mybir.AxisListType

QK_HEADS = 8
V_HEADS = 16
B_HEADS = 8
PATTERNS = 3
SC_CHUNKS = 3072 // P
SSM_GROUPS = 64
SSM_P = 16
SSM_CHUNKS = SSM_GROUPS * SSM_P // P
FF_QUARTERS = 4
DK_SCALE = float(P) ** -0.5

SLAB_K = 2
SLAB_N = 4
SLAB = SLAB_K * SLAB_N * P
RING = 4
AHEAD = 3
POOL_SLOTS = (1, 3)
KSLABS = KC // SLAB_K

HYB_GROUPS_PER_HEAD = 3
N_HYB = QK_HEADS * HYB_GROUPS_PER_HEAD
OUT_A_K, OUT_B_K = 16, 8
SC_GROUPS = 4
N_SC_ITER = SC_CHUNKS // SLAB_N
ADA_GROUPS = 24


VEC_WIDTHS = [
    ("norm0", 16), ("norm1", 16), ("final1", 16), ("mix", 16), ("mlp", 16), ("final2", 16),
    ("dn_conv", 8 * 4 * 4), ("sc_conv", 24 * 3), ("dn_norm", 1), ("ssm_d", 8), ("b_glu", 8),
    ("c", 16), ("b_ada", 96), ("a_log", 32), ("dt_bias", 32),
    ("a_re", 64), ("a_im", 64), ("log_dt", 64),
]
CONST_WIDTHS = [
    ("ident", 128), ("upper", 128), ("ones", 128),
]
HYB_CONST_WIDTHS = [
    ("mask_t", 128), ("mask_s", 128), ("nm0", 128), ("nm0t", 128), ("levels", 6 * 64),
    ("att_mask", 3 * 384), ("cos", 256), ("sin", 256), ("rot", 32),
]
LATE_CONST_WIDTHS = [("flip", 128), ("onehot", 512), ("negrow", 512), ("emask", 8), ("sgn", 1), ("nsgn", 1)]


def offsets(widths):
    at, out = 0, {}
    for name, w in widths:
        out[name] = (at, w)
        at += w
    return out, at


VEC, VEC_N = offsets(VEC_WIDTHS)
CST, CST_N = offsets(CONST_WIDTHS)
HYC, HYC_N = offsets(HYB_CONST_WIDTHS)
LTC, LTC_N = offsets(LATE_CONST_WIDTHS)


def wait(eng, sem, value):
    if isinstance(value, int) and value <= 0:
        return
    eng.wait_ge(sem, value)


def program(nc, stack, ins, out_d):
    base0 = 16512
    top = [base0]
    named = [0]

    def place(name, shape, dt=F32):
        n = 4
        for s in shape[1:]:
            n *= s
        n = (n + 31) // 32 * 32
        t = nc.alloc_sbuf_tensor_at(name, list(shape), dt, offset=top[0])
        top[0] += n
        assert top[0] <= 229368, (name, top[0])
        return t

    raw = place("raw", [P, RING, SLAB])
    wh = place("wh", [P, RING, SLAB], F32R)
    wl = place("wl", [P, RING, SLAB], F32R)
    xs_at = top[0]
    xs = place("xs", [P, KC, 2 * T], F32R)
    tmp = place("tmp", [P, 4, T])
    vec = place("vec", [P, VEC_N])
    cst = place("cst", [P, CST_N])
    mod = place("mod", [P, 96])
    nrm = place("nrm", [P, 8])
    rn = place("rn", [P, 8])
    mhalf = place("mhalf", [P, 8])
    dnh = place("dnh", [P, 8])
    hid_at = top[0]
    hid = place("hid", [P, 24, 2 * T], F32R)
    arena = top[0]
    hid2 = nc.alloc_sbuf_tensor_at("hid2", [P, 32, 2 * T], F32R, offset=hid_at)
    arena2 = hid_at + 32 * 2 * T * 4
    x_at = 229344 - KC * T * 4
    x_at -= x_at % 32
    x = nc.alloc_sbuf_tensor_at("x", [P, KC, T], F32, offset=x_at)
    xacc = nc.alloc_sbuf_tensor_at("xacc", [P, KC, T], F32, offset=xs_at)

    def V(name, a=0, n=None):
        at, w = VEC[name]
        n = w - a if n is None else n
        if isinstance(a, int):
            return vec[:, at + a:at + a + n]
        return vec[:, bass.ds(at + a, n)]

    def C(name):
        at, w = CST[name]
        return cst[:, at:at + w]

    ident, upper, ones = C("ident"), C("upper"), C("ones")

    top[0] = arena + 32768
    nsq0 = place("nsq0", [P, 4, T])
    nyb0 = place("nyb0", [P, 4, T])
    assert top[0] <= x_at

    top[0] = arena
    hyc = place("hyc", [P, HYC_N])

    def H(name):
        at, w = HYC[name]
        return hyc[:, at:at + w]

    cb = place("cb", [P, 4, 4 + T])
    qkv = place("qkv", [P, 4, T])
    th = place("th", [P, 4, T])
    sqq = th
    zz = place("zz", [P, 2, T])
    zs = place("zs", [P, 2, T])
    gA = place("gA", [P, 4, P])
    gB = place("gB", [P, 4, P])
    eg = place("eg", [P, 2, P])
    kb = place("kb", [P, 4, P])
    kd = place("kd", [P, 2, P])
    rhsv = place("rhsv", [P, 4, P])
    AT = place("AT", [P, 4, P])
    Dm = place("Dm", [P, 4, P])
    Em = place("Em", [P, 4, P])
    Xm = place("Xm", [P, 4, 64])
    vn0 = place("vn0", [P, 2, P])
    wTn = place("wTn", [P, 2, P])
    Sst = place("Sst", [P, 2, P])
    vn1 = place("vn1", [P, 2, P])
    qe = place("qe", [P, 2, P])
    gsel = place("gsel", [P, 4])
    gcum = place("gcum", [P, V_HEADS, 2])
    gnat = place("gnat", [P, V_HEADS, 2])
    ngcum = place("ngcum", [P, V_HEADS, 2])
    beta = place("beta", [P, V_HEADS, 2])
    bhalf = place("bhalf", [P, V_HEADS, 2])
    bexp = place("bexp", [P, V_HEADS, 2])
    kdecf = place("kdecf", [P, V_HEADS, 2])
    gt = place("gt", [P, 6, 2 * V_HEADS])
    bb = place("bb", [P, 6, T])
    rb = place("rb", [32, 2, T])
    Sb = place("Sb", [P, PATTERNS, 384])
    Pb = place("Pb", [P, 384])
    PT = place("PT", [P, 384])
    vnat = place("vnat", [P, T])
    bzs = place("bzs", [P, T])
    bth = place("bth", [P, T])
    yb = place("yb", [P, T])
    smx = place("smx", [P, 8])
    osb, sqo = AT, Dm
    yh = kb
    wab_at = nc.alloc_sbuf_tensor_at("wab", [P, KC, 32], F32, offset=arena + 4 * HYC_N + 64)
    wabh = nc.alloc_sbuf_tensor_at("wabh", [P, KC, 32], F32R, offset=arena + 4 * HYC_N + 64 + 2048)
    wabl = nc.alloc_sbuf_tensor_at("wabl", [P, KC, 32], F32R, offset=arena + 4 * HYC_N + 64 + 4096)

    top[0] = arena
    nsq = place("nsq", [P, 4, T])
    nyb = place("nyb", [P, 4, T])
    cc = place("cc", [P, 4, T])
    uu = place("uu", [P, 4, T])
    pc = place("pc", [P, 4, 2 + T])
    yv = place("yv", [P, 4, T])
    sth = place("sth", [P, 4, T])
    araw = place("araw", [P, 2, SLAB])
    aacc = place("aacc", [P, 512])
    cact = place("cact", [P, KC])
    cth = place("cth", [P, KC])
    assert top[0] <= x_at, top[0]

    top[0] = arena2
    norm_g = place("norm_g", [P, KC])
    ltc = place("ltc", [P, LTC_N])
    rel_sb = place("rel_sb", [32, 8])
    bgh = place("bgh", [P, 8])

    def L(name):
        at, w = LTC[name]
        return ltc[:, at:at + w]
    second = top[0]
    nsq2 = place("nsq2", [P, 4, T])
    nyb2 = place("nyb2", [P, 4, T])
    top[0] = second
    uT = place("uT", [P, SSM_CHUNKS, T])
    cB = place("cB", [P, SSM_GROUPS, 16])
    sB = place("sB", [P, SSM_GROUPS, 16])
    bb1 = place("bb1", [P, SSM_GROUPS * SSM_P])
    bb2 = place("bb2", [P, SSM_GROUPS * SSM_P])
    sC = place("sC", [P, 2, SSM_GROUPS, SSM_P])
    assert top[0] <= x_at, (top[0], x_at)
    top[0] = hid_at
    cA = place("cA", [P, SSM_GROUPS, 16])
    sA = place("sA", [P, SSM_GROUPS, 16])
    lb = place("lb", [P, 2, 8, P])
    cpad = place("cpad", [P, 2, 8 * 144])
    assert top[0] <= hid_at + 16 * 2 * T * 4, (top[0] - hid_at)
    top[0] = hid_at + 24 * 2 * T * 4
    Ct = place("Ct", [P, T])
    St = place("St", [P, T])
    t1 = place("t1", [P, 2, T])
    t2 = place("t2", [P, 2, T])
    xr = place("xr", [P, T])
    rr = place("rr", [P, T])
    crs = place("crs", [P, 2, T])
    bs = place("bs", [P, 2, P])
    yt = place("yt", [P, T])
    yg = place("yg", [P, T])
    trg = place("trg", [P, 8, SSM_GROUPS])
    mag = place("mag", [P, SSM_GROUPS])
    assert top[0] <= hid_at + 32 * 2 * T * 4, (top[0] - hid_at)

    fxg = nc.alloc_sbuf_tensor_at("fxg", [P, 4, T], F32, offset=second + 8 * T * 4)
    top[0] = second
    att = place("att", [P, 24, T])
    btab = place("btab", [P, 8, 256])
    assert top[0] <= x_at, (top[0], x_at)
    top[0] = hid_at + 24 * 2 * T * 4
    bvec = nc.alloc_sbuf_tensor_at("bvec", [8, 512], F32, offset=top[0])
    qvs = place("qvs", [P, 2, T])
    mSb = place("mSb", [P, 384])
    mPT = place("mPT", [P, 384])
    mvn = place("mvn", [P, T])
    my = place("my", [P, T])
    msm = place("msm", [P, 8])
    toep = place("toep", [P, 8, 256])
    assert top[0] <= hid_at + 32 * 2 * T * 4

    top[0] = second
    sg = place("sg", [P, 4, T])
    mt = place("mt", [P, 4, T])
    macc = place("macc", [P, 4, T])
    fx = place("fx", [P, 4, T])
    assert top[0] <= x_at

    def sem(name):
        return stack.enter_context(nc.semaphore(name))

    G = [stack.enter_context(nc.psum_tensor(f"gemm{n}", [P, 512], F32)) for n in range(4)]
    ps0, ps1, ps2, ps3 = [stack.enter_context(nc.psum_tensor(f"side{n}", [P, 512], F32)) for n in range(4)]
    bias_dram = nc.dram_tensor("bias_scratch", (8, 512), F32).ap()

    raw_in = [sem(f"raw_in{n}") for n in range(RING)]
    ada_in = [sem(f"ada_in{n}") for n in range(2)]
    hi_ready = sem("hi_ready")
    lo_dve, lo_pool = sem("lo_dve"), sem("lo_pool")
    slab_used = sem("slab_used")
    bank_ready, bank_freed = sem("bank_ready"), sem("bank_freed")
    tmp_ready = sem("tmp_ready")
    loads = {n: sem("in_" + n) for n in ("first", "second", "xback", "toep", "bias")}
    x_ready = sem("x_ready")
    norm_sq, norm_sum, norm_var, norm_rn, norm_bc = (sem("norm_" + n) for n in ("sq", "sum", "var", "rn", "bc"))
    norm_y, norm_hi, xs_ready = sem("norm_y"), sem("norm_hi"), sem("xs_ready")
    dve_step, act_step, pool_step = sem("dve_step"), sem("act_step"), sem("pool_step")
    setup = sem("setup")
    Z = {}

    def S(name):
        if name not in Z:
            Z[name] = sem(name)
        return Z[name]

    NP = len(POOL_SLOTS)
    DVE_SLOTS = [n for n in range(RING) if n not in POOL_SLOTS]

    def wait_lo(eng, q, slot):
        if slot in POOL_SLOTS:
            wait(eng, lo_pool, q * NP + POOL_SLOTS.index(slot) + 1)
        else:
            wait(eng, lo_dve, q * (RING - NP) + DVE_SLOTS.index(slot) + 1)

    def walk(q0, nslabs, split, hook=None, slot0=0):
        for sl in range(nslabs):
            nxt = sl + AHEAD
            split(q0 + nxt // RING, nxt % RING)
            if hook is not None:
                hook(slot0 + 2 * sl)
                hook(slot0 + 2 * sl + 1)

    Q_OUTA = N_HYB * 2
    Q_OUTB = Q_OUTA + 4 * OUT_A_K // 8
    Q_SC = Q_OUTB + 4 * OUT_B_K // 8
    Q_SCOUT = Q_SC + 24 * 2
    Q_U = Q_SCOUT + 4 * 3
    Q_GLU = Q_U + 2 * 2
    Q_QKV = Q_GLU + 2 * 1
    Q_MRG = Q_QKV + 6 * 2
    Q_WO = Q_MRG + 4 * 6
    Q_FF = Q_WO + 4 * 2
    Q_END = Q_FF + 4 * 16
    G_OUTA = N_HYB
    G_OUTB, G_SC = G_OUTA + 4, G_OUTA + 8
    G_SCOUT = G_SC + 24
    G_U = G_SCOUT + 4
    G_GLU, G_QKV = G_U + 2, G_U + 4
    G_MRG = G_QKV + 6
    G_WO = G_MRG + 16
    G_FF = G_WO + 4
    assert Q_END * 4 == ins["stream"].shape[0] - RING

    DELTA_AT = {1 + int(s * 1.55): s for s in range(29)}
    ATTN_AT = {3 + 4 * k: k for k in range(8)}
    outa_chunks = list(range(0, 12)) + list(range(16, 20))
    outb_chunks = list(range(12, 16)) + list(range(20, 24))

    X_READY = {0: 0, 1: 4, 2: 8, 3: 12, 4: 16, 5: 32}
    norm_bufs = {0: (nsq0, nyb0), 1: (nsq, nyb), 2: (nsq, nyb), 3: (nsq, nyb), 4: (nsq2, nyb2), 5: (nsq2, nyb2)}

    def shift_of(n):
        return {3: mod[:, 0:16], 4: mod[:, 48:64]}.get(n)

    def four(ap):
        return ap.unsqueeze(1).to_broadcast([P, 4, ap.shape[1]])

    block = stack.enter_context(nc.Block())

    @block.sync
    def _(sp):
        sp.dma_start(x[:], ins["x"]).then_inc(loads["first"], 16)
        sp.dma_start(vec[:], ins["vec"]).then_inc(loads["first"], 16)
        sp.dma_start(cst[:], ins["cst"]).then_inc(loads["first"], 16)
        sp.dma_start(hyc[:], ins["hyc"]).then_inc(loads["first"], 16)
        sp.dma_start(wab_at[:], ins["wab"]).then_inc(loads["first"], 16)

        def slab(q, slot):
            if not (isinstance(q, int) and q == 0):
                wait_lo(sp, q - 1, slot)
            sp.dma_start(raw[:, slot, :], ins["stream"][4 * q + slot]).then_inc(raw_in[slot], 16)

        for slot in range(RING):
            slab(0, slot)
        with sp.Fori(1, Q_SC) as q:
            for slot in range(RING):
                slab(q, slot)
        def ada(a, n):
            if not (isinstance(a, int) and a < 2):
                sp.wait_ge(S("ada_used"), a - 1)
            sp.dma_start(araw[:, n, :], ins["ada"][a]).then_inc(ada_in[n], 16)

        sp.wait_ge(S("first_done"), 1)
        for slot in range(RING):
            slab(Q_SC, slot)
        ada(0, 0)
        ada(1, 1)
        with sp.Fori(1, 48) as i:
            for slot in range(RING):
                slab(Q_SC + i, slot)
                ada(4 * i + slot - 2, slot % 2)
        for slot in range(RING):
            slab(Q_SCOUT, slot)
            if slot < 2:
                ada(8 * ADA_GROUPS - 2 + slot, slot)
        with sp.Fori(Q_SCOUT + 1, Q_END + 1) as q:
            for slot in range(RING):
                slab(q, slot)
        for slot in range(RING):
            sp.wait_ge(raw_in[slot], 16 * (Q_END + 1))
        sp.wait_ge(S("out_ready"), 4)
        sp.dma_start(out_d, x[:]).then_inc(S("out_stored"), 16)
        sp.wait_ge(S("out_stored"), 16)

    @block.tensor
    def _(pe):
        mm = nc.tensor.matmul

        def group(g, q0, nslabs, rhs, ready, hook=None, slot0=0):
            for sl in range(nslabs):
                q, slot = q0 + sl // RING, sl % RING
                wait(pe, hi_ready, 4 * q + slot + 1)
                wait_lo(pe, q, slot)
                ready(sl)
                for n in range(SLAB_N):
                    if sl == 0:
                        wait(pe, bank_freed, 4 * g + n - 3)
                    for k in range(SLAB_K):
                        xk = rhs(sl * SLAB_K + k)
                        at = (k * SLAB_N + n) * P
                        first = sl == 0 and k == 0
                        last = sl == nslabs - 1 and k == SLAB_K - 1
                        mm(G[n][:, :], wh[:, slot, at:at + P], xk, start=first, stop=False,
                           skip_group_check=True)
                        op = mm(G[n][:, T:2 * T], wl[:, slot, at:at + P], xk[:, 0:T], start=False, stop=last,
                                skip_group_check=True)
                    if n == SLAB_N - 1:
                        op.then_inc(slab_used, 1)
                    elif sl == nslabs - 1:
                        op.then_inc(bank_ready, 1)
                    if hook is not None and n % 2 == 1:
                        hook(slot0 + 2 * sl + n // 2)

        def xs_of(k):
            return xs[:, k, :]

        def xs_wait(m):
            def ready(sl):
                if sl % 2 == 0:
                    wait(pe, xs_ready, 4 * m + sl // 2 + 1)
            return ready

        def norm(n):
            for q in range(4):
                wait(pe, norm_sq, 4 * n + q + 1)
                b = norm_bufs[n][0]
                for j in range(4):
                    for c in range(2):
                        op = mm(ps0[:, c:c + 1], b[:, j, c * P:(c + 1) * P], ones[:, 0:1],
                                start=(q == 0 and j == 0 and c == 0), stop=(q == 3 and j == 3),
                                skip_group_check=True)
                op.then_inc(norm_sum, 1)
            wait(pe, norm_rn, n + 1)
            for c in range(2):
                op = mm(ps1[:, c * P:(c + 1) * P], rn[:, c:c + 1].to_broadcast([P, P]), ident, start=True, stop=True)
            op.then_inc(norm_bc, 1)

        def gates():
            pe.wait_ge(S("gate_dve"), 1)
            pe.wait_ge(xs_ready, 4)
            for c in range(2):
                for k in range(KC):
                    lh = xs[:, k, c * P:(c + 1) * P]
                    ll = xs[:, k, T + c * P:T + (c + 1) * P]
                    o = ps0[:, 32 * c:32 * c + 32]
                    mm(o, lh, wabh[:, k, :], start=(k == 0), stop=False, skip_group_check=True)
                    mm(o, lh, wabl[:, k, :], start=False, stop=False, skip_group_check=True)
                    op = mm(o, ll, wabh[:, k, :], start=False, stop=(k == KC - 1), skip_group_check=True)
            op.then_inc(S("gate_pe"), 1)
            pe.wait_ge(S("gate_dve"), 4)
            for c in range(2):
                mm(ps1[:, 16 * c:16 * c + 16], upper, gnat[:, :, c], start=True, stop=True)
                op = mm(ps1[:, 32 + 16 * c:48 + 16 * c], ones, gnat[:, :, c], start=True, stop=True)
            op.then_inc(S("gate_pe"), 1)

        def delta(s, it):
            if s == 0:
                pe.wait_ge(S("d_sq"), it + 1)
                for a in range(2):
                    for c in range(2):
                        op = mm(ps0[:, 2 * a + c:2 * a + c + 1], sqq[:, a, c * P:(c + 1) * P], ones[:, 0:1],
                                start=True, stop=True)
                op.then_inc(S("p_norm"), 1)
            elif s == 1:
                pe.wait_ge(S("l_rn"), it + 1)
                for j in range(4):
                    mm(ps0[:, j * P:(j + 1) * P], rn[:, j:j + 1].to_broadcast([P, P]), ident, start=True, stop=True)
                for j in range(4):
                    op = mm(ps1[:, j * P:(j + 1) * P], gsel[:, j:j + 1].to_broadcast([P, P]), upper,
                            start=True, stop=True)
                op.then_inc(S("p_bc"), 1)
            elif s == 2:
                pe.wait_ge(S("d_qk"), it + 1)
                for c in range(2):
                    kc_ = qkv[:, 1, c * P:(c + 1) * P]
                    mm(ps2[:, c * P:(c + 1) * P], kc_, kc_, start=True, stop=True)
                    op = mm(ps2[:, (2 + c) * P:(3 + c) * P], kc_, qkv[:, 0, c * P:(c + 1) * P], start=True, stop=True)
                op.then_inc(S("p_kk"), 1)
            elif s == 3:
                pe.wait_ge(S("d_gm"), it + 1)
                pe.wait_ge(S("a_eg"), it + 1)
                for c in range(2):
                    nc.tensor.transpose(ps0[:, c * P:(c + 1) * P], qkv[:, 1, c * P:(c + 1) * P], ident)
                for j in range(4):
                    op = nc.tensor.transpose(ps1[:, j * P:(j + 1) * P],
                                             qkv[:, 2 + j // 2, (j % 2) * P:(j % 2 + 1) * P], ident)
                op.then_inc(S("p_nat"), 1)
            elif s == 4:
                pe.wait_ge(S("d_A"), it + 1)
                for j in range(4):
                    op = nc.tensor.transpose(ps2[:, j * P:(j + 1) * P], gB[:, j, :], ident)
                op.then_inc(S("p_AT"), 1)
            elif s < 23:
                lv, part = (s - 5) // 3 + 1, (s - 5) % 3
                b = 1 << lv
                if part == 0:
                    wait(pe, S("d_D"), 7 * it + lv)
                    if lv == 1:
                        pe.wait_ge(S("a_nat"), it + 1)
                    for j in range(4):
                        left = Dm[:, j, :].rearrange("p (m two b) -> p m two b", two=2, b=b)[:, :, 0, :]
                        op = mm(ps0[:, j * 64:(j + 1) * 64], AT[:, j, :], left, start=True, stop=True)
                    op.then_inc(S("p_X"), 1)
                elif part == 1:
                    wait(pe, S("d_X"), 6 * it + lv)
                    if lv > 1:
                        wait(pe, S("a_E"), 6 * it + lv - 1)
                    for j in range(4):
                        op = mm(ps0[:, 256 + j * 64:256 + (j + 1) * 64], Em[:, j, :], Xm[:, j, :], start=True, stop=True)
                    op.then_inc(S("p_DX"), 1)
                else:
                    wait(pe, S("d_D"), 7 * it + lv + 1)
                    for j in range(4):
                        op = nc.tensor.transpose(ps1[:, j * P:(j + 1) * P], Dm[:, j, :], ident)
                    op.then_inc(S("p_E"), 1)
            elif s == 23:
                wait(pe, S("a_E"), 6 * it + 6)
                for v in range(2):
                    mm(ps2[:, v * P:(v + 1) * P], Em[:, 2 * v, :], rhsv[:, 2 * v, :], start=True, stop=True)
                    op = mm(ps2[:, (2 + v) * P:(3 + v) * P], kb[:, 2 * v + 1, :], Em[:, 2 * v + 1, :],
                            start=True, stop=True)
                op.then_inc(S("p_v0"), 1)
            elif s == 24:
                pe.wait_ge(S("a_v0"), it + 1)
                for v in range(2):
                    op = mm(ps0[:, v * P:(v + 1) * P], kd[:, v, :], vn0[:, v, :], start=True, stop=True)
                op.then_inc(S("p_S"), 1)
            elif s == 25:
                pe.wait_ge(S("d_S"), it + 1)
                for v in range(2):
                    o = ps0[:, (2 + v) * P:(3 + v) * P]
                    mm(o, Em[:, 2 * v + 1, :], rhsv[:, 2 * v + 1, :], start=True, stop=False)
                    op = mm(o, wTn[:, v, :], Sst[:, v, :], start=False, stop=True)
                op.then_inc(S("p_v1"), 1)
            elif s == 26:
                pe.wait_ge(S("d_v1"), it + 1)
                for v in range(2):
                    mm(ps1[:, 2 * v * P:(2 * v + 1) * P], vn0[:, v, :], gA[:, 2 * v, :], start=True, stop=True)
                    o = ps1[:, (2 * v + 1) * P:(2 * v + 2) * P]
                    mm(o, Sst[:, v, :], qe[:, v, :], start=True, stop=False)
                    op = mm(o, vn1[:, v, :], gA[:, 2 * v + 1, :], start=False, stop=True)
                op.then_inc(S("p_o"), 1)
            elif s == 27:
                pe.wait_ge(S("a_o"), it + 1)
                for j in range(4):
                    op = mm(ps2[:, j:j + 1], sqo[:, j, :], ones[:, 0:1], start=True, stop=True)
                op.then_inc(S("p_osum"), 1)
            elif s == 28:
                pe.wait_ge(S("l_orn"), it + 1)
                for j in range(4):
                    op = mm(ps2[:, j * P:(j + 1) * P], rn[:, 4 + j:5 + j].to_broadcast([P, P]), ident,
                            start=True, stop=True)
                op.then_inc(S("p_obc"), 1)

        def attn(k, it):
            if k < 2:
                pe.wait_ge(bank_freed, 12 * it + 12)
                if k == 1:
                    pe.wait_ge(S("b_rope"), 2 * it + 1)
                mm(ps3[0:32, :], H("rot"), bb[:, 2 * k:2 * k + 2, :], start=True, stop=True
                   ).then_inc(S("bp_rope"), 1)
            elif k == 2:
                pe.wait_ge(S("b_rope"), 2 * it + 2)
                for c in range(2):
                    op = nc.tensor.transpose(ps3[:, c * P:(c + 1) * P], bb[:, 4, c * P:(c + 1) * P], ident)
                op.then_inc(S("bp_vn"), 1)
            elif k == 3:
                pe.wait_ge(S("b_vn"), it + 1)
                for a in range(PATTERNS):
                    op = mm(ps3[:, a * P:(a + 1) * P], bb[:, a, 0:P], bb[:, 3, 0:P], start=True, stop=True)
                op.then_inc(S("bp_s"), 1)
            elif k == 4:
                pe.wait_ge(S("b_s"), 3 * it + 1)
                for a in range(2):
                    op = mm(ps3[:, a * T:(a + 1) * T], bb[:, a, P:T], bb[:, 3, :], start=True, stop=True)
                op.then_inc(S("bp_s"), 1)
            elif k == 5:
                pe.wait_ge(S("b_s"), 3 * it + 2)
                mm(ps3[:, 0:T], bb[:, 2, P:T], bb[:, 3, :], start=True, stop=True).then_inc(S("bp_s"), 1)
            elif k == 6:
                pe.wait_ge(S("b_p"), it + 1)
                for j in range(3):
                    op = nc.tensor.transpose(ps3[:, j * P:(j + 1) * P], Pb[:, j * P:(j + 1) * P], ident)
                op.then_inc(S("bp_pt"), 1)
            elif k == 7:
                pe.wait_ge(S("b_pt"), it + 1)
                mm(ps3[:, 0:T], vnat[:, 0:P], PT[:, 0:T], start=True, stop=False, skip_group_check=True)
                mm(ps3[:, P:T], vnat[:, P:T], PT[:, T:T + P], start=False, stop=True,
                   skip_group_check=True).then_inc(S("bp_o"), 1)

        def heads(it):
            def hook(slot):
                if slot in DELTA_AT:
                    delta(DELTA_AT[slot], it)
                if slot in ATTN_AT:
                    attn(ATTN_AT[slot], it)
            return hook

        pe.wait_ge(loads["first"], 80)
        pe.wait_ge(setup, 1)
        norm(0)
        gates()
        for gi in range(3):
            group(gi, 2 * gi, 8, xs_of, xs_wait(0))
        with pe.Fori(1, QK_HEADS) as h:
            for gi in range(3):
                group(3 * h + gi, 6 * h + 2 * gi, 8, xs_of, lambda sl: None, heads(h - 1), 16 * gi)

        def hid_of(chunks):
            return lambda k: hid[:, chunks[k], :]

        def outa_ready(sl):
            wait(pe, S("ya_lo"), 6)
            wait(pe, S("yb_lo"), 4)

        for gi in range(3):
            group(G_OUTA + gi, Q_OUTA + 2 * gi, 8, hid_of(outa_chunks), outa_ready, heads(7), 16 * gi)
        group(G_OUTA + 3, Q_OUTA + 6, 8, hid_of(outa_chunks), outa_ready)

        def outb_ready(sl):
            wait(pe, S("ya_lo"), 8)
            wait(pe, S("yb_lo"), 8)

        with pe.Fori(0, 4) as i:
            group(G_OUTB + i, Q_OUTB + i, 4, hid_of(outb_chunks), outb_ready)
        norm(1)

        def ada_sum(g):
            pe.wait_ge(S("ada_used"), 8 * g + 8)
            for n in range(4):
                op = mm(ps2[:, n:n + 1], aacc[:, n * P:(n + 1) * P], ones[:, 0:1], start=True, stop=True)
            op.then_inc(S("ada_sum"), 1)

        with pe.Fori(0, N_SC_ITER) as j:
            for gi in range(4):
                group(G_SC + 4 * j + gi, Q_SC + 8 * j + 2 * gi, 8, xs_of, xs_wait(1))
                ada_sum(4 * j + gi)

        def sc_ready(sl):
            if sl % 2 == 0:
                wait(pe, S("sc_lo"), sl // 2 + 1)

        with pe.Fori(0, 4) as i:
            group(G_SCOUT + i, Q_SCOUT + 3 * i, 12, lambda k: hid[:, k, :], sc_ready)
        norm(2)
        norm(3)

        with pe.Fori(0, 2) as i:
            group(G_U + i, Q_U + 2 * i, 8, xs_of, xs_wait(2))

        with pe.Fori(0, SSM_CHUNKS) as j:
            pe.wait_ge(S("m_bs"), j + 1)
            for w in range(2):
                op = nc.tensor.transpose(ps0[:, w * P:(w + 1) * P], bs[:, w, :], ident)
            op.then_inc(S("mp_bt"), 1)
            for g in range(8):
                pe.wait_ge(S("m_lb"), j + 1)
                for w in range(2):
                    op = mm(ps1[:, w * T:(w + 1) * T], lb[:, w, g, :], uT[:, j, :], start=True, stop=True)
                op.then_inc(S("mp_bu"), 1)
                pe.wait_ge(S("m_cp"), j + 1)
                pe.wait_ge(S("m_crs"), 8 * j + g + 2)
                for w in range(2):
                    op = mm(ps2[:, 0:T], cpad[:, w, g * P:(g + 1) * P], crs[:, w, :],
                            start=(g == 0 and w == 0), stop=(g == 7 and w == 1), skip_group_check=True)
                op.then_inc(S("mp_y"), 1)

        def glu_ready(sl):
            wait(pe, S("m_lo"), SSM_CHUNKS)

        for i in range(2):
            group(G_GLU + i, Q_GLU + i, 4, lambda k: hid2[:, 16 + k, :], glu_ready)
        with pe.Fori(0, 6) as i:
            group(G_QKV + i, Q_QKV + 2 * i, 8, xs_of, xs_wait(2))

        pe.wait_ge(loads["second"], 80)
        mm(ps0[0:8, :], rel_sb[:, :], L("onehot")[0:32, :], start=True, stop=True).then_inc(S("tp_set"), 1)
        pe.wait_ge(loads["toep"], 16 * B_HEADS)
        for n in range(4):
            if n >= 1:
                pe.wait_ge(S("t_set"), n + 1)
            mm(ps0[:, :], L("flip"), toep[:, 2 * n:2 * n + 2, :], start=True, stop=True).then_inc(S("tp_set"), 1)
        pe.wait_ge(S("t_set"), 5)
        with pe.Fori(0, B_HEADS) as h:
            pe.wait_ge(S("t_qv"), h + 1)
            mm(ps0[:, 0:P], qvs[:, 0, 0:P], att[:, 3 * h + 1, 0:P], start=True, stop=True)
            mm(ps0[:, P:3 * P], qvs[:, 0, P:T], att[:, 3 * h + 1, :], start=True, stop=True
               ).then_inc(S("tp_s"), 1)
            for c in range(2):
                op = nc.tensor.transpose(ps1[:, c * P:(c + 1) * P], qvs[:, 1, c * P:(c + 1) * P], ident)
            op.then_inc(S("tp_vn"), 1)
            pe.wait_ge(S("t_p"), h + 1)
            for j in range(3):
                op = nc.tensor.transpose(ps2[:, j * P:(j + 1) * P], mSb[:, j * P:(j + 1) * P], ident)
            op.then_inc(S("tp_pt"), 1)
            pe.wait_ge(S("t_pt"), h + 1)
            mm(ps3[:, 0:T], mvn[:, 0:P], mPT[:, 0:T], start=True, stop=False, skip_group_check=True)
            mm(ps3[:, P:T], mvn[:, P:T], mPT[:, T:T + P], start=False, stop=True, skip_group_check=True
               ).then_inc(S("tp_o"), 1)

        def ssm_in(sl):
            wait(pe, S("glu_lo"), 2)

        def att_in(sl):
            wait(pe, S("t_lo"), B_HEADS)

        with pe.Fori(0, 4) as i:
            group(G_MRG + 4 * i, Q_MRG + 6 * i, 8, xs_of, xs_wait(2))
            group(G_MRG + 4 * i + 1, Q_MRG + 6 * i + 2, 4, lambda k: hid2[:, k, :], ssm_in)
            group(G_MRG + 4 * i + 2, Q_MRG + 6 * i + 3, 8, xs_of, xs_wait(2))
            group(G_MRG + 4 * i + 3, Q_MRG + 6 * i + 5, 4, lambda k: hid2[:, 8 + k, :], att_in)

        def mrg_ready(sl):
            if sl % 2 == 0:
                wait(pe, S("mrg_lo"), sl // 2 + 1)

        with pe.Fori(0, 4) as i:
            group(G_WO + i, Q_WO + 2 * i, 8, lambda k: hid2[:, 16 + k, :], mrg_ready)
        norm(4)
        with pe.Fori(0, FF_QUARTERS) as c:
            with pe.Fori(0, 4) as i:
                group(G_FF + 8 * c + i, Q_FF + 16 * c + 2 * i, 8, xs_of, xs_wait(3))

            with pe.Fori(0, 4) as i:
                def ff_ready(sl):
                    if sl % 2 == 0:
                        pe.wait_ge(S("ff_lo"), 4 * c + sl // 2 + 1)
                group(G_FF + 8 * c + 4 + i, Q_FF + 16 * c + 8 + 2 * i, 8, lambda k: hid2[:, k, :], ff_ready)
        norm(5)

    @block.scalar
    def _(act):
        A = nc.scalar.activation
        steps = [0]

        def link(op):
            steps[0] += 1
            op.then_inc(act_step, 1)
            act.wait_ge(act_step, steps[0])

        def restart():
            act.sem_clear(act_step)
            steps[0] = 0

        def split(q, slot):
            act.wait_ge(raw_in[slot], 16 * (q + 1))
            if not (isinstance(q, int) and q == 0):
                act.wait_ge(slab_used, 4 * q + slot - 3)
            A(wh[:, slot, :], raw[:, slot, :], ACT.Copy).then_inc(hi_ready, 1)

        def evac(g, q_end):
            for n in range(SLAB_N):
                if n < SLAB_N - 1:
                    act.wait_ge(bank_ready, 3 * g + n + 1)
                else:
                    act.wait_ge(slab_used, 4 * q_end)
                wait(act, bank_freed, 4 * g + n - 3)
                A(tmp[:, n, :], G[n][:, T:2 * T], ACT.Copy).then_inc(tmp_ready, 1)

        def norm(n, m=None):
            wait(act, x_ready, X_READY[n])
            sq, y = norm_bufs[n]
            for q in range(4):
                wait(act, norm_sum, 4 * n + q)
                A(sq[:, :, :], x[:, 4 * q:4 * q + 4, :], ACT.Square).then_inc(norm_sq, 1)
            if m is None:
                return
            for q in range(4):
                act.wait_ge(norm_y, 4 * m + q + 1)
                o = xs[:, 4 * q:4 * q + 4, 0:T]
                if shift_of(n) is None:
                    A(o, y[:, :, :], ACT.Copy).then_inc(norm_hi, 1)
                else:
                    for j in range(4):
                        k = 4 * q + j
                        op = A(o[:, j, :], y[:, j, :], ACT.Identity, bias=shift_of(n)[:, k:k + 1])
                    op.then_inc(norm_hi, 1)

        for slot in range(AHEAD):
            split(0, slot)
        act.wait_ge(loads["first"], 80)
        norm(0, 0)
        act.wait_ge(loads["first"], 80)
        act.wait_ge(xs_ready, 4)
        A(wabh[:, :, :], wab_at[:, :, :], ACT.Copy).then_inc(S("gate_act"), 1)
        act.wait_ge(S("gate_dve"), 2)
        A(gt[:, 1, :], gt[:, 0, :], ACT.Exp, scale=-1.0).then_inc(S("gate_act"), 1)
        A(gt[:, 3, :], gt[:, 2, :], ACT.Exp, scale=-1.0).then_inc(S("gate_act"), 1)
        A(gt[:, 5, :], V("a_log"), ACT.Exp).then_inc(S("gate_act"), 1)
        act.wait_ge(S("gate_dve"), 3)
        A(gt[:, 3, :], gt[:, 3, :], ACT.Ln).then_inc(S("gate_act"), 1)
        act.wait_ge(S("gate_dve"), 5)
        A(bexp[:, :, :], gcum[:, :, :], ACT.Exp).then_inc(S("gate_act"), 1)
        A(kdecf[:, :, :], kdecf[:, :, :], ACT.Exp).then_inc(S("gate_act"), 1)

        def conv_act(h):
            act.wait_ge(S("d_conv"), h + 1)
            A(th[:, :, :], qkv[:, :, :], ACT.Tanh, scale=0.5).then_inc(S("a_tanh"), 1)
            act.wait_ge(S("d_silu"), h + 1)
            A(sqq[:, 0:2, :], qkv[:, 0:2, :], ACT.Square).then_inc(S("d_sq"), 1)

        def delta(s, it):
            if s == 0:
                act.wait_ge(bank_freed, 12 * it + 8)
                A(th[:, 2:4, :], zz[:, :, :], ACT.Tanh, scale=0.5).then_inc(S("a_z"), 1)
            elif s == 1:
                act.wait_ge(S("d_gm"), it + 1)
                A(eg[:, :, :], ps1[:, :].rearrange("p (v c i) -> p v c i", v=2, c=2)[:, :, 1, :],
                  ACT.Exp).then_inc(S("a_eg"), 1)
                for j in range(4):
                    v, c = j // 2, j % 2
                    A(gA[:, j, :], gA[:, j, :], ACT.Exp, bias=ngcum[:, 2 * it + v, c:c + 1])
                    op = A(gB[:, j, :], gB[:, j, :], ACT.Exp, scale=-1.0, bias=gcum[:, 2 * it + v, c:c + 1])
                op.then_inc(S("a_dec"), 1)
            elif s == 3:
                act.wait_ge(S("p_nat"), it + 1)
                for j in range(4):
                    v, c = j // 2, j % 2
                    A(kb[:, j, :], ps0[:, c * P:(c + 1) * P], ACT.Copy, scale=bexp[:, 2 * it + v, c:c + 1])
                    A(rhsv[:, j, :], ps1[:, j * P:(j + 1) * P], ACT.Copy, scale=bhalf[:, 2 * it + v, c:c + 1])
                for v in range(2):
                    op = A(kd[:, v, :], ps0[:, 0:P], ACT.Copy, scale=kdecf[:, 2 * it + v, 0:1])
                op.then_inc(S("a_nat"), 1)
            elif 5 <= s < 23 and (s - 5) % 3 == 2:
                lv = (s - 5) // 3 + 1
                act.wait_ge(S("p_E"), 6 * it + lv)
                A(Em[:, :, :], ps1[:, :], ACT.Copy).then_inc(S("a_E"), 1)
            elif s == 23:
                act.wait_ge(S("p_v0"), it + 1)
                A(vn0[:, :, :], ps2[:, 0:2 * P], ACT.Copy)
                A(wTn[:, :, :], ps2[:, 2 * P:4 * P], ACT.Copy, scale=-1.0).then_inc(S("a_v0"), 1)
            elif s == 26:
                act.wait_ge(S("p_o"), it + 1)
                A(osb[:, :, :], ps1[:, :], ACT.Copy)
                A(sqo[:, :, :], ps1[:, :], ACT.Square).then_inc(S("a_o"), 1)
            elif s == 28:
                act.wait_ge(S("ya"), it + 1)
                A(hid[:, bass.ds(2 * it, 2), 0:T], yh[:, :, :].rearrange("p j i -> p (j i)"), ACT.Copy
                  ).then_inc(S("ya_hi"), 1)

        def attn(k, it):
            if k == 0:
                act.wait_ge(bank_freed, 12 * it + 12)
                A(bth[:, :], bb[:, 5, :], ACT.Tanh, scale=0.5).then_inc(S("ba_z"), 1)
            elif k == 2:
                act.wait_ge(S("bp_vn"), it + 1)
                A(vnat[:, :], ps3[:, 0:T], ACT.Copy).then_inc(S("b_vn"), 1)
            elif k == 5:
                act.wait_ge(S("b_mx"), it + 1)
                A(Sb[:, :, 0:P], Sb[:, :, 0:P], ACT.Exp, bias=smx[:, 0:1], accum_out=smx[:, 2:3])
                A(Sb[:, :, P:3 * P], Sb[:, :, P:3 * P], ACT.Exp, bias=smx[:, 1:2],
                  accum_out=smx[:, 3:4]).then_inc(S("ba_e"), 1)
            elif k == 6:
                act.wait_ge(S("bp_pt"), it + 1)
                A(PT[:, :], ps3[:, 0:384], ACT.Copy).then_inc(S("b_pt"), 1)
            elif k == 7:
                act.wait_ge(S("yb"), it + 1)
                A(hid[:, 16 + it, 0:T], yb[:, :], ACT.Copy).then_inc(S("yb_hi"), 1)

        def heads(it):
            def hook(slot):
                if slot in DELTA_AT:
                    delta(DELTA_AT[slot], it)
                if slot in ATTN_AT:
                    attn(ATTN_AT[slot], it)
            return hook

        def hyb(h, hook=None):
            for gi in range(3):
                walk(6 * h + 2 * gi, 8, split, hook, 16 * gi)
                evac(3 * h + gi, 6 * h + 2 * gi + 2)
                if gi == 0:
                    conv_act(h)

        hyb(0)
        with act.Fori(1, QK_HEADS) as h:
            hyb(h, heads(h - 1))
        for gi in range(4):
            walk(Q_OUTA + 2 * gi, 8, split, heads(7) if gi < 3 else None, 16 * gi)
            if gi == 3:
                act.wait_ge(S("first_done"), 1)
                act.dma_start(x[:], ins["x"]).then_inc(loads["xback"], 16)
            evac(G_OUTA + gi, Q_OUTA + 2 * gi + 2)
        with act.Fori(0, 4) as i:
            walk(Q_OUTB + i, 4, split)
            evac(G_OUTB + i, Q_OUTB + i + 1)
        A(cth[:, :], V("c"), ACT.Tanh, scale=0.5).then_inc(S("ca_t"), 1)
        norm(1, 1)
        with act.Fori(0, N_SC_ITER) as j:
            for gi in range(4):
                walk(Q_SC + 8 * j + 2 * gi, 8, split)
                evac(G_SC + 4 * j + gi, Q_SC + 8 * j + 2 * gi + 2)
            act.wait_ge(bank_freed, 4 * (G_SC + 4 * j) + 16)
            A(sth[:, :, :], cc[:, :, :], ACT.Tanh, scale=0.5).then_inc(S("sca_t"), 1)
            act.wait_ge(S("sc_y"), j + 1)
            A(hid[:, bass.ds(4 * j, 4), 0:T], yv[:, :, :], ACT.Copy).then_inc(S("sc_hi"), 1)
        with act.Fori(0, 4) as i:
            walk(Q_SCOUT + 3 * i, 12, split)
            evac(G_SCOUT + i, Q_SCOUT + 3 * i + 3)
        norm(2)
        norm(3, 2)
        act.wait_ge(S("first_done"), 2)
        act.dma_start(ltc[:], ins["ltc"]).then_inc(loads["second"], 16)
        act.dma_start(bb1[:], ins["b1"]).then_inc(loads["second"], 16)
        act.dma_start(bb2[:], ins["b2"]).then_inc(loads["second"], 16)
        act.dma_start(sC[:], ins["c12"]).then_inc(loads["second"], 16)
        act.dma_start(rel_sb[:], ins["rel"]).then_inc(loads["second"], 16)
        with act.Fori(0, 2) as i:
            walk(Q_U + 2 * i, 8, split)
            evac(G_U + i, Q_U + 2 * i + 2)

        A(trg[:, 0, :], V("log_dt"), ACT.Exp).then_inc(S("s_act"), 1)
        act.wait_ge(S("s_dve"), 1)
        A(trg[:, 2, :], trg[:, 2, :], ACT.Exp).then_inc(S("s_act"), 1)
        A(trg[:, 3, :], trg[:, 3, :], ACT.Sin).then_inc(S("s_act"), 1)
        A(trg[:, 4, :], trg[:, 4, :], ACT.Sin).then_inc(S("s_act"), 1)
        with act.Fori(0, SSM_CHUNKS) as j:
            act.wait_ge(S("s_dve"), 2)
            A(bs[:, 0, :], bb1[:, bass.ds(j * P, P)], ACT.Copy)
            A(bs[:, 1, :], bb2[:, bass.ds(j * P, P)], ACT.Copy).then_inc(S("m_bs"), 1)
            for w in range(2):
                op = A(cpad[:, w, :].rearrange("p (g s) -> p g s", s=144)[:, :, 0:16],
                       sC[:, w, bass.ds(8 * j, 8), :], ACT.Copy)
            op.then_inc(S("m_cp"), 1)
            act.wait_ge(S("m_in"), j + 1)
            A(yg[:, :], yg[:, :], ACT.Tanh, scale=math.sqrt(2 / math.pi)).then_inc(S("m_t"), 1)
            act.wait_ge(S("m_yg"), j + 1)
            A(hid2[:, 16 + j, 0:T], uT[:, j, :], ACT.Copy).then_inc(S("m_hi"), 1)
        for i in range(2):
            walk(Q_GLU + i, 4, split)
            evac(G_GLU + i, Q_GLU + i + 1)
            act.wait_ge(bank_freed, 4 * (G_GLU + i) + 4)
            for n in range(4):
                op = A(fxg[:, n, :], fxg[:, n, :], ACT.Tanh, scale=0.5, bias=bgh[:, 4 * i + n:4 * i + n + 1])
            op.then_inc(S("glu_t"), 1)
            act.wait_ge(S("glu_y"), i + 1)
            A(hid2[:, 4 * i:4 * i + 4, 0:T], uT[:, 4 * i:4 * i + 4, :], ACT.Copy).then_inc(S("glu_hi"), 1)
        with act.Fori(0, 6) as i:
            walk(Q_QKV + 2 * i, 8, split)
            evac(G_QKV + i, Q_QKV + 2 * i + 2)
        act.wait_ge(S("t_set"), 1)
        act.dma_start(bias_dram, bvec[:]).then_inc(loads["bias"], 16)
        act.wait_ge(loads["bias"], 16)
        for h in range(B_HEADS):
            act.dma_start(toep[:, h, :], bass.AP(tensor=bias_dram.tensor, offset=512 * h, ap=[[1, P], [1, 256]])
                          ).then_inc(loads["toep"], 16)
        with act.Fori(0, B_HEADS) as h:
            act.wait_ge(bank_freed, 4 * (G_QKV + 6))
            A(qvs[:, 0, :], att[:, 3 * h, :], ACT.Copy, scale=DK_SCALE)
            A(qvs[:, 1, :], att[:, 3 * h + 2, :], ACT.Copy).then_inc(S("t_qv"), 1)
            act.wait_ge(S("tp_vn"), h + 1)
            A(mvn[:, :], ps1[:, 0:T], ACT.Copy)
            act.wait_ge(S("t_mx"), h + 1)
            A(mSb[:, 0:P], mSb[:, 0:P], ACT.Exp, bias=msm[:, 0:1], accum_out=msm[:, 2:3])
            A(mSb[:, P:3 * P], mSb[:, P:3 * P], ACT.Exp, bias=msm[:, 1:2], accum_out=msm[:, 3:4]
              ).then_inc(S("ta_e"), 1)
            act.wait_ge(S("tp_pt"), h + 1)
            A(mPT[:, :], ps2[:, 0:384], ACT.Copy).then_inc(S("t_pt"), 1)
            act.wait_ge(S("t_y"), h + 1)
            A(hid2[:, 8 + h, 0:T], my[:, :], ACT.Copy).then_inc(S("t_hi"), 1)
        with act.Fori(0, 4) as i:
            for gi, n, q in ((0, 8, 0), (1, 4, 2), (2, 8, 3), (3, 4, 5)):
                walk(Q_MRG + 6 * i + q, n, split)
                evac(G_MRG + 4 * i + gi, Q_MRG + 6 * i + q + n // 4)
                if gi % 2 == 0:
                    act.wait_ge(bank_freed, 4 * (G_MRG + 4 * i + gi) + 4)
                    A(sg[:, :, :], sg[:, :, :], ACT.Tanh, scale=0.5).then_inc(S("mg_t"), 1)
            act.wait_ge(S("mrg"), i + 1)
            A(hid2[:, bass.ds(16 + 4 * i, 4), 0:T], macc[:, :, :], ACT.Copy).then_inc(S("mrg_hi"), 1)
        with act.Fori(0, 4) as i:
            walk(Q_WO + 2 * i, 8, split)
            evac(G_WO + i, Q_WO + 2 * i + 2)
        norm(4, 3)
        with act.Fori(0, FF_QUARTERS) as c:
            with act.Fori(0, 4) as i:
                walk(Q_FF + 16 * c + 2 * i, 8, split)
                evac(G_FF + 8 * c + i, Q_FF + 16 * c + 2 * i + 2)
                act.wait_ge(S("ff"), 4 * c + i + 1)
                A(hid2[:, bass.ds(4 * i, 4), 0:T], mt[:, :, :], ACT.Copy).then_inc(S("ff_hi"), 1)
            with act.Fori(0, 4) as i:
                walk(Q_FF + 16 * c + 8 + 2 * i, 8, split)
                evac(G_FF + 8 * c + 4 + i, Q_FF + 16 * c + 8 + 2 * i + 2)
        norm(5)

    @block.gpsimd
    def _(pool):
        def split(q, slot):
            if slot not in POOL_SLOTS:
                return
            pool.wait_ge(hi_ready, 4 * q + slot + 1)
            if not (isinstance(q, int) and q == 0):
                pool.wait_ge(slab_used, 4 * q + slot - 3)
            nc.gpsimd.tensor_tensor(wl[:, slot, :], raw[:, slot, :], wh[:, slot, :].bitcast(F32),
                                    ALU.subtract).then_inc(lo_pool, 1)

        def norm(n):
            pool.wait_ge(norm_var, n + 1)
            nc.gpsimd.tensor_tensor(rn[:, 0:2], nrm[:, 0:2], mhalf[:, 0:2], ALU.pow).then_inc(norm_rn, 1)

        def heads(it):
            def hook(slot):
                s = DELTA_AT.get(slot)
                if s == 0:
                    nc.gpsimd.tensor_copy(gsel[:, :], gcum_g(it))
                    pool.wait_ge(S("d_nrm"), it + 1)
                    nc.gpsimd.tensor_tensor(rn[:, 0:4], nrm[:, 0:4], mhalf[:, 0:4], ALU.pow
                                            ).then_inc(S("l_rn"), 1)
                elif s == 27:
                    pool.wait_ge(S("d_onrm"), it + 1)
                    nc.gpsimd.tensor_tensor(rn[:, 4:8], nrm[:, 4:8], mhalf[:, 4:8], ALU.pow
                                            ).then_inc(S("l_orn"), 1)
            return hook

        def gcum_g(it):
            return gnat[:, bass.ds(2 * it, 2), :]

        nc.gpsimd.memset(mhalf[:, :], -0.5).then_inc(S("l_half"), 1)
        pool.wait_ge(S("l_half"), 1)
        for slot in range(AHEAD):
            split(0, slot)
        norm(0)
        pool.wait_ge(S("gate_pe"), 2)
        for gi in range(3):
            walk(2 * gi, 8, split)
        with pool.Fori(1, QK_HEADS) as h:
            for gi in range(3):
                walk(6 * h + 2 * gi, 8, split, heads(h - 1), 16 * gi)
        for gi in range(4):
            walk(Q_OUTA + 2 * gi, 8, split, heads(7) if gi < 3 else None, 16 * gi)
        with pool.Fori(0, 4) as i:
            walk(Q_OUTB + i, 4, split)
        norm(1)
        with pool.Fori(0, 48) as i:
            walk(Q_SC + i, 4, split)
        with pool.Fori(0, 12) as i:
            walk(Q_SCOUT + i, 4, split)
        norm(2)
        norm(3)
        with pool.Fori(0, 4) as i:
            walk(Q_U + i, 4, split)
        pool.wait_ge(S("s_dve"), 3)
        with pool.Fori(0, SSM_CHUNKS) as j:
            for g in range(8):
                def big(t):
                    return t[:, bass.ds(8 * j + g, 1), :].rearrange("p o a -> p (o a)").unsqueeze(2).to_broadcast([P, 16, 16])

                def small(t):
                    return t[:, bass.ds(8 * j + g, 1), :].to_broadcast([P, 16, 16])
                v = [t[:, :].rearrange("p (a b) -> p a b", a=16) for t in (t2[:, 0, :], t2[:, 1, :])]
                cv = Ct[:, :].rearrange("p (a b) -> p a b", a=16)
                sv = St[:, :].rearrange("p (a b) -> p a b", a=16)
                pool.wait_ge(S("m_crs"), 8 * j + g + 1)
                nc.gpsimd.tensor_tensor(cv, big(cA), small(cB), ALU.mult)
                nc.gpsimd.tensor_tensor(v[0], big(sA), small(sB), ALU.mult)
                nc.gpsimd.tensor_tensor(sv, big(sA), small(cB), ALU.mult)
                nc.gpsimd.tensor_tensor(v[1], big(cA), small(sB), ALU.mult).then_inc(S("m_prod"), 1)
                pool.wait_ge(S("m_prod"), 8 * j + g + 1)
                nc.gpsimd.tensor_tensor(Ct[:, :], Ct[:, :], t2[:, 0, :], ALU.subtract)
                nc.gpsimd.tensor_tensor(St[:, :], St[:, :], t2[:, 1, :], ALU.add).then_inc(S("m_tab"), 1)
        for i in range(2):
            walk(Q_GLU + i, 4, split)
        with pool.Fori(0, 12) as i:
            walk(Q_QKV + i, 4, split)
        with pool.Fori(0, 24) as i:
            walk(Q_MRG + i, 4, split)
        with pool.Fori(0, 8) as i:
            walk(Q_WO + i, 4, split)
        norm(4)
        with pool.Fori(0, 64) as i:
            walk(Q_FF + i, 4, split)
        norm(5)

    @block.vector
    def _(dve):
        tt, ts, stt = nc.vector.tensor_tensor, nc.vector.tensor_scalar, nc.vector.scalar_tensor_tensor
        steps = [0]

        def link(op):
            steps[0] += 1
            op.then_inc(dve_step, 1)
            dve.wait_ge(dve_step, steps[0])

        def restart():
            dve.sem_clear(dve_step)
            steps[0] = 0

        def split(q, slot):
            if slot in POOL_SLOTS:
                return
            dve.wait_ge(hi_ready, 4 * q + slot + 1)
            if not (isinstance(q, int) and q == 0):
                dve.wait_ge(slab_used, 4 * q + slot - 3)
            tt(wl[:, slot, :], raw[:, slot, :], wh[:, slot, :].bitcast(F32), ALU.subtract).then_inc(lo_dve, 1)

        def add(g, n, out):
            dve.wait_ge(tmp_ready, 4 * g + n + 1)
            tt(out, G[n][:, 0:T], tmp[:, n, :], ALU.add).then_inc(bank_freed, 1)

        def added(g):
            dve.wait_ge(bank_freed, 4 * g + 4)

        def low(out, y, hi):
            return tt(out, y, hi.bitcast(F32), ALU.subtract)

        def norm(n, m, w, into=None):
            sq, y = norm_bufs[n]
            dve.wait_ge(norm_sum, 4 * n + 4)
            ts(nrm[:, 0:2], ps0[:, 0:2], 1.0 / D, EPS, ALU.mult, ALU.add).then_inc(norm_var, 1)
            dve.wait_ge(norm_bc, n + 1)
            for q in range(4):
                if m is None:
                    for j in range(4):
                        k = 4 * q + j
                        op = stt(x[:, k, :], x[:, k, :], w[:, k:k + 1], ps1[:, 0:T], ALU.mult, ALU.mult)
                    op.then_inc(into, 1)
                    continue
                wait(dve, xs_ready, 4 * m + q)
                for j in range(4):
                    k = 4 * q + j
                    op = stt(y[:, j, :], x[:, k, :], w[:, k:k + 1], ps1[:, 0:T], ALU.mult, ALU.mult)
                op.then_inc(norm_y, 1)
                dve.wait_ge(norm_y, 4 * m + q + 1)
                dve.wait_ge(norm_hi, 4 * m + q + 1)
                hi = xs[:, 4 * q:4 * q + 4, 0:T]
                lo = xs[:, 4 * q:4 * q + 4, T:2 * T]
                if shift_of(n) is None:
                    op = low(lo, y[:, :, :], hi)
                else:
                    for j in range(4):
                        k = 4 * q + j
                        op = stt(lo[:, j, :], y[:, j, :], shift_of(n)[:, k:k + 1], hi[:, j, :].bitcast(F32),
                                 ALU.add, ALU.subtract)
                op.then_inc(xs_ready, 1)

        for slot in range(AHEAD):
            split(0, slot)
        dve.wait_ge(loads["first"], 80)
        ts(dnh[:, 0:1], V("dn_norm"), 0.5, None, ALU.mult).then_inc(setup, 1)
        norm(0, 0, V("norm0"))
        dve.wait_ge(S("gate_act"), 1)
        tt(wabl[:, :, :], wab_at[:, :, :], wabh[:, :, :].bitcast(F32), ALU.subtract).then_inc(S("gate_dve"), 1)
        dve.wait_ge(S("gate_pe"), 1)
        pv = ps0[:, 0:64].rearrange("p (c a h) -> p c a h", c=2, a=2)

        def ch(row):
            return gt[:, row, :].rearrange("p (c h) -> p c h", c=2)

        def hc(t):
            return t[:, :, :].rearrange("p h c -> p c h")
        link(nc.vector.tensor_copy(ch(0), pv[:, :, 0, :]))
        link(tt(ch(4), pv[:, :, 1, :], V("dt_bias").rearrange("p (c h) -> p c h", c=2), ALU.add))
        stt(gt[:, 2, :], gt[:, 4, :], -1.0, gt[:, 4, :], ALU.mult, ALU.max).then_inc(S("gate_dve"), 1)
        dve.wait_ge(S("gate_act"), 4)
        ts(gt[:, 3, :], gt[:, 3, :], 1.0, None, ALU.add).then_inc(S("gate_dve"), 1)
        link(ts(gt[:, 1, :], gt[:, 1, :], 1.0, None, ALU.add))
        link(nc.vector.reciprocal(gt[:, 1, :], gt[:, 1, :]))
        link(nc.vector.tensor_copy(hc(beta), ch(1)))
        ts(bhalf[:, :, :], beta[:, :, :], 0.5, None, ALU.mult)
        dve.wait_ge(S("gate_act"), 5)
        link(stt(gt[:, 4, :], gt[:, 4, :], 0.0, gt[:, 3, :], ALU.max, ALU.add))
        stt(hc(gnat), ch(5), -1.0, ch(4), ALU.mult, ALU.mult).then_inc(S("gate_dve"), 1)
        dve.wait_ge(S("gate_pe"), 2)
        pg = ps1[:, 0:64].rearrange("p (a c h) -> p a c h", a=2, c=2)
        link(nc.vector.tensor_copy(hc(gcum), pg[:, 0]))
        ts(ngcum[:, :, :], gcum[:, :, :], -1.0, None, ALU.mult)
        tt(hc(kdecf), pg[:, 1], hc(gcum), ALU.subtract).then_inc(S("gate_dve"), 1)
        dve.wait_ge(S("gate_act"), 7)
        link(tt(bexp[:, :, :], bexp[:, :, :], beta[:, :, :], ALU.mult))
        link(nc.vector.memset(cb[:, :, :], 0.0))

        def conv_dve(h):
            added(3 * h)
            for tap in range(4):
                for n in range(4):
                    w = V("dn_conv", 16 * h + 4 * n + tap, 1)
                    src = cb[:, n, 1 + tap:1 + tap + T]
                    if tap == 0:
                        op = ts(qkv[:, n, :], src, w, None, ALU.mult)
                    else:
                        op = stt(qkv[:, n, :], src, w, qkv[:, n, :], ALU.mult, ALU.add)
                if tap < 3:
                    link(op)
            op.then_inc(S("d_conv"), 1)
            dve.wait_ge(S("a_tanh"), h + 1)
            stt(qkv[:, :, :], th[:, :, :], 1.0, qkv[:, :, :], ALU.add, ALU.mult).then_inc(S("d_silu"), 1)

        def delta(s, it):
            if s == 0:
                dve.wait_ge(S("p_norm"), it + 1)
                ts(nrm[:, 0:4], ps0[:, 0:4], 4 * EPS, None, ALU.add).then_inc(S("d_nrm"), 1)
                dve.wait_ge(S("a_z"), it + 1)
                stt(zs[:, :, :], th[:, 2:4, :], 1.0, zz[:, :, :], ALU.add, ALU.mult)
            elif s == 1:
                dve.wait_ge(S("p_bc"), it + 1)
                stt(qkv[:, 0, :], qkv[:, 0, :], DK_SCALE, ps0[:, 0:T], ALU.mult, ALU.mult)
                tt(qkv[:, 1, :], qkv[:, 1, :], ps0[:, T:2 * T], ALU.mult).then_inc(S("d_qk"), 1)
                pv = ps1[:, :].rearrange("p (j i) -> p j i", j=4)
                tt(gA[:, :, :], pv, four(H("mask_t")), ALU.add)
                tt(gB[:, :, :], pv, four(H("mask_s")), ALU.add).then_inc(S("d_gm"), 1)
            elif s == 2:
                dve.wait_ge(S("p_kk"), it + 1)
                dve.wait_ge(S("a_dec"), it + 1)
                for j in range(4):
                    v, c = j // 2, j % 2
                    stt(gB[:, j, :], ps2[:, c * P:(c + 1) * P], beta[:, 2 * it + v, c:c + 1], gB[:, j, :],
                        ALU.mult, ALU.mult)
                two = gA[:, :, :].rearrange("p (v c) i -> p v (c i)", v=2)
                tt(two, ps2[:, 2 * P:4 * P].unsqueeze(1).to_broadcast([P, 2, 2 * P]), two, ALU.mult)
                tt(qe[:, :, :], qkv[:, 0, P:T].unsqueeze(1).to_broadcast([P, 2, P]), eg[:, :, :], ALU.mult
                   ).then_inc(S("d_A"), 1)
            elif s == 4:
                dve.wait_ge(S("p_AT"), it + 1)
                pv = ps2[:, :].rearrange("p (j i) -> p j i", j=4)
                nc.vector.tensor_copy(AT[:, :, :], pv)
                tt(Dm[:, :, :], gB[:, :, :], four(H("nm0")), ALU.mult)
                link(tt(Em[:, :, :], pv, four(H("nm0t")), ALU.mult))
                tt(Dm[:, :, :], Dm[:, :, :], four(ident), ALU.add)
                tt(Em[:, :, :], Em[:, :, :], four(ident), ALU.add).then_inc(S("d_D"), 1)
            elif 5 <= s < 23:
                lv, part = (s - 5) // 3 + 1, (s - 5) % 3
                b = 1 << lv
                if part == 0:
                    dve.wait_ge(S("p_X"), 6 * it + lv)
                    mask = H("levels")[:, (lv - 1) * 64:lv * 64]
                    tt(Xm[:, :, :], ps0[:, 0:256].rearrange("p (j i) -> p j i", j=4), four(mask), ALU.mult
                       ).then_inc(S("d_X"), 1)
                elif part == 1:
                    dve.wait_ge(S("p_DX"), 6 * it + lv)
                    left = Dm[:, :, :].rearrange("p j (m two b) -> p j m two b", two=2, b=b)[:, :, :, 0, :]
                    pv = ps0[:, 256:512].rearrange("p (j m b) -> p j m b", j=4, b=b)
                    tt(left, pv, left, ALU.add).then_inc(S("d_D"), 1)
            elif s == 24:
                dve.wait_ge(S("p_S"), it + 1)
                nc.vector.tensor_copy(Sst[:, :, :], ps0[:, 0:2 * P].rearrange("p (v i) -> p v i", v=2)
                                      ).then_inc(S("d_S"), 1)
            elif s == 25:
                dve.wait_ge(S("p_v1"), it + 1)
                nc.vector.tensor_copy(vn1[:, :, :], ps0[:, 2 * P:4 * P].rearrange("p (v i) -> p v i", v=2)
                                      ).then_inc(S("d_v1"), 1)
            elif s == 27:
                dve.wait_ge(S("p_osum"), it + 1)
                ts(nrm[:, 4:8], ps2[:, 0:4], 1.0 / P, EPS, ALU.mult, ALU.add).then_inc(S("d_onrm"), 1)
            elif s == 28:
                dve.wait_ge(S("p_obc"), it + 1)
                yf = yh[:, :, :].rearrange("p j i -> p (j i)")
                link(stt(yf, osb[:, :, :].rearrange("p j i -> p (j i)"), dnh[:, 0:1], ps2[:, :], ALU.mult, ALU.mult))
                tt(yf, yf, zs[:, :, :].rearrange("p v i -> p (v i)"), ALU.mult).then_inc(S("ya"), 1)
                dve.wait_ge(S("ya_hi"), it + 1)
                yv2 = yh[:, :, :].rearrange("p (v c) i -> p v (c i)", v=2)
                low(hid[:, bass.ds(2 * it, 2), T:2 * T], yv2, hid[:, bass.ds(2 * it, 2), 0:T]
                    ).then_inc(S("ya_lo"), 1)

        def attn(k, it):
            if k < 2:
                dve.wait_ge(S("bp_rope"), 2 * it + k + 1)
                two = bb[0:32, 2 * k:2 * k + 2, :]
                cosb, sinb = (H(n)[0:32, :].unsqueeze(1).to_broadcast([32, 2, T]) for n in ("cos", "sin"))
                tt(rb[:, :, :], ps3[0:32, :].rearrange("p (a i) -> p a i", a=2), sinb, ALU.mult)
                tt(two, two, cosb, ALU.mult).then_inc(S("b_cos"), 1)
                dve.wait_ge(S("b_cos"), 2 * it + k + 1)
                tt(two, two, rb[:, :, :], ALU.add).then_inc(S("b_rope"), 1)
                if k == 0:
                    dve.wait_ge(S("ba_z"), it + 1)
                    stt(bzs[:, :], bth[:, :], 1.0, bb[:, 5, :], ALU.add, ALU.mult)
            elif k in (3, 4, 5):
                dve.wait_ge(S("bp_s"), 3 * it + k - 2)
                m = H("att_mask").rearrange("p (a i) -> p a i", a=3)
                if k == 3:
                    sel, pv = (slice(0, 3), slice(0, P)), ps3[:, 0:384].rearrange("p (a i) -> p a i", a=3)
                elif k == 4:
                    sel, pv = (slice(0, 2), slice(P, 3 * P)), ps3[:, :].rearrange("p (a i) -> p a i", a=2)
                else:
                    sel, pv = (slice(2, 3), slice(P, 3 * P)), ps3[:, 0:T].unsqueeze(1)
                stt(Sb[:, sel[0], sel[1]], pv, DK_SCALE, m[:, sel[0], sel[1]], ALU.mult, ALU.add
                    ).then_inc(S("b_s"), 1)
                if k == 5:
                    dve.wait_ge(S("b_s"), 3 * it + 3)
                    nc.vector.tensor_reduce(smx[:, 0:1], Sb[:, :, 0:P], AX.XY, ALU.max, negate=True)
                    nc.vector.tensor_reduce(smx[:, 1:2], Sb[:, :, P:3 * P], AX.XY, ALU.max, negate=True
                                            ).then_inc(S("b_mx"), 1)
                    dve.wait_ge(S("ba_e"), it + 1)
                    nc.vector.reciprocal(smx[:, 4:6], smx[:, 2:4])
                    tt(Pb[:, :], Sb[:, 0, :], Sb[:, 1, :], ALU.add).then_inc(S("b_p2"), 1)
                    dve.wait_ge(S("b_p2"), 2 * it + 1)
                    tt(Pb[:, :], Pb[:, :], Sb[:, 2, :], ALU.add).then_inc(S("b_p2"), 1)
                    dve.wait_ge(S("b_p2"), 2 * it + 2)
                    ts(Pb[:, 0:P], Pb[:, 0:P], smx[:, 4:5], None, ALU.mult)
                    ts(Pb[:, P:3 * P], Pb[:, P:3 * P], smx[:, 5:6], None, ALU.mult).then_inc(S("b_p"), 1)
            elif k == 7:
                dve.wait_ge(S("bp_o"), it + 1)
                stt(yb[:, :], ps3[:, 0:T], 0.5, bzs[:, :], ALU.mult, ALU.mult).then_inc(S("yb"), 1)
                dve.wait_ge(S("yb"), it + 1)
                dve.wait_ge(S("yb_hi"), it + 1)
                low(hid[:, 16 + it, T:2 * T], yb[:, :], hid[:, 16 + it, 0:T]).then_inc(S("yb_lo"), 1)

        def heads(it):
            def hook(slot):
                if slot in DELTA_AT:
                    delta(DELTA_AT[slot], it)
                if slot in ATTN_AT:
                    attn(ATTN_AT[slot], it)
            return hook

        def hyb(h, hook=None):
            for gi in range(3):
                walk(6 * h + 2 * gi, 8, split, hook, 16 * gi)
                g = 3 * h + gi
                for n in range(4):
                    out = (cb[:, n, 4:4 + T] if gi == 0 else
                           (zz[:, n, :] if n < 2 else bb[:, n - 2, :]) if gi == 1 else bb[:, n + 2, :])
                    add(g, n, out)
                if gi == 0:
                    conv_dve(h)

        hyb(0)
        with dve.Fori(1, QK_HEADS) as h:
            restart()
            hyb(h, heads(h - 1))
        restart()
        for gi in range(4):
            walk(Q_OUTA + 2 * gi, 8, split, heads(7) if gi < 3 else None, 16 * gi)
            if gi == 3:
                dve.wait_ge(S("ya_lo"), 8)
                ts(smx[:, 0:1], smx[:, 0:1], 0.0, None, ALU.mult).then_inc(S("first_done"), 1)
            for n in range(4):
                add(G_OUTA + gi, n, xacc[:, 4 * gi + n, :])
        with dve.Fori(0, 4) as i:
            restart()
            walk(Q_OUTB + i, 4, split)
            for n in range(4):
                add(G_OUTB + i, n, uu[:, n, :])
            added(G_OUTB + i)
            dve.wait_ge(loads["xback"], 16)
            k4 = bass.ds(4 * i, 4)
            link(tt(uu[:, :, :], uu[:, :, :], xacc[:, k4, :], ALU.add))
            tt(x[:, k4, :], x[:, k4, :], uu[:, :, :], ALU.add).then_inc(x_ready, 1)
            dve.wait_ge(x_ready, i + 1)
        restart()
        dve.wait_ge(S("ca_t"), 1)
        link(stt(cact[:, :], cth[:, :], 1.0, V("c"), ALU.add, ALU.mult))
        link(ts(cact[:, :], cact[:, :], 0.5, None, ALU.mult))
        norm(1, 1, V("norm1"))
        link(nc.vector.memset(pc[:, :, :], 0.0))

        def ada(g, sl):
            dve.wait_ge(ada_in[sl % 2], 16 * (4 * g + sl // 2 + 1))
            for k in range(2):
                src, w = araw[:, sl % 2, 512 * k:512 * k + 512], cact[:, 2 * sl + k:2 * sl + k + 1]
                if sl == 0 and k == 0:
                    link(ts(aacc[:, :], src, w, None, ALU.mult))
                elif k == 0:
                    link(stt(aacc[:, :], src, w, aacc[:, :], ALU.mult, ALU.add))
                else:
                    stt(aacc[:, :], src, w, aacc[:, :], ALU.mult, ALU.add).then_inc(S("ada_used"), 1)
                    dve.wait_ge(S("ada_used"), 8 * g + sl + 1)

        with dve.Fori(0, N_SC_ITER) as j:
            restart()
            for gi in range(4):
                g = 4 * j + gi
                walk(Q_SC + 2 * g, 8, split, lambda slot: ada(g, slot // 2) if slot % 2 == 0 else None)
                out = (cc, uu, uu, cc)[gi]
                for n in range(4):
                    add(G_SC + g, n, out[:, n, :])
                added(G_SC + g)
                if gi == 1:
                    link(tt(pc[:, :, 2:2 + T], uu[:, :, :], cc[:, :, :], ALU.mult))
                    for tap in range(3):
                        for n in range(4):
                            w, src = V("sc_conv", 12 * j + 3 * n + tap, 1), pc[:, n, tap:tap + T]
                            if tap == 0:
                                op = ts(yv[:, n, :], src, w, None, ALU.mult)
                            else:
                                op = stt(yv[:, n, :], src, w, yv[:, n, :], ALU.mult, ALU.add)
                        link(op)
                elif gi == 2:
                    link(tt(yv[:, :, :], yv[:, :, :], uu[:, :, :], ALU.mult))
                elif gi == 3:
                    dve.wait_ge(S("sca_t"), j + 1)
                    link(stt(cc[:, :, :], sth[:, :, :], 1.0, cc[:, :, :], ALU.add, ALU.mult))
                    stt(yv[:, :, :], yv[:, :, :], 0.5, cc[:, :, :], ALU.mult, ALU.mult).then_inc(S("sc_y"), 1)
                    dve.wait_ge(S("sc_y"), j + 1)
                    dve.wait_ge(S("sc_hi"), j + 1)
                    low(hid[:, bass.ds(4 * j, 4), T:2 * T], yv[:, :, :], hid[:, bass.ds(4 * j, 4), 0:T]
                        ).then_inc(S("sc_lo"), 1)
                dve.wait_ge(S("ada_sum"), g + 1)
                tt(mod[:, bass.ds(4 * g, 4)], ps2[:, 0:4], V("b_ada", 4 * g, 4), ALU.add).then_inc(S("ada_mod"), 1)
        with dve.Fori(0, 4) as i:
            restart()
            walk(Q_SCOUT + 3 * i, 12, split)
            for n in range(4):
                add(G_SCOUT + i, n, uu[:, n, :])
            added(G_SCOUT + i)
            tt(x[:, bass.ds(4 * i, 4), :], x[:, bass.ds(4 * i, 4), :], uu[:, :, :], ALU.add).then_inc(x_ready, 1)
            dve.wait_ge(x_ready, i + 5)
        restart()
        dve.wait_ge(S("ada_mod"), ADA_GROUPS)
        norm(2, None, V("final1"), x_ready)
        dve.wait_ge(x_ready, 12)
        link(stt(norm_g[:, :], mod[:, 16:32], 1.0, V("mix"), ALU.add, ALU.mult))
        norm(3, 2, norm_g)
        link(ts(bgh[:, :], V("b_glu"), 0.5, None, ALU.mult))
        dve.wait_ge(xs_ready, 12)
        ts(mhalf[:, 0:1], mhalf[:, 0:1], 1.0, None, ALU.mult).then_inc(S("first_done"), 1)
        with dve.Fori(0, 2) as i:
            walk(Q_U + 2 * i, 8, split)
            for n in range(4):
                add(G_U + i, n, uT[:, 4 * i + n, :])

        R = [trg[:, r, :] for r in range(8)]
        are, aim = V("a_re"), V("a_im")
        magic = 12582912.0
        two_pi = 2 * math.pi
        c1 = 6.28125
        c2 = float(np.float32(two_pi - c1))
        c3 = two_pi - c1 - c2
        dve.wait_ge(S("s_act"), 1)
        link(tt(R[2], R[0], are, ALU.mult))
        link(tt(R[1], R[0], aim, ALU.mult))
        link(ts(R[5], R[1], 1 / two_pi, magic, ALU.mult, ALU.add))
        link(ts(R[5], R[5], -magic, None, ALU.add))
        for cw in (c1, c2, c3):
            link(stt(R[1], R[5], -cw, R[1], ALU.mult, ALU.add))
        link(ts(R[3], R[1], 3.1415925, -3.1415925, ALU.min, ALU.max))
        ts(R[4], R[3], 0.5, None, ALU.mult).then_inc(S("s_dve"), 1)
        dve.wait_ge(S("s_act"), 4)
        nc.vector.tensor_copy(mag[:, :], R[2])
        link(tt(R[5], R[4], R[4], ALU.mult))
        link(ts(R[6], R[5], -2.0, 1.0, ALU.mult, ALU.add))
        link(tt(R[5], R[5], R[2], ALU.mult))
        link(ts(R[7], R[2], -1.0, None, ALU.add))
        link(stt(R[5], R[5], -2.0, R[7], ALU.mult, ALU.add))
        link(tt(R[7], R[2], R[3], ALU.mult))
        link(tt(R[0], are, are, ALU.mult))
        link(tt(R[1], aim, aim, ALU.mult))
        link(tt(R[0], R[0], R[1], ALU.add))
        link(nc.vector.reciprocal(R[0], R[0]))
        link(tt(R[1], R[5], are, ALU.mult))
        link(tt(R[2], R[7], aim, ALU.mult))
        link(tt(R[1], R[1], R[2], ALU.add))
        link(tt(R[1], R[1], R[0], ALU.mult))
        link(tt(R[2], R[7], are, ALU.mult))
        link(tt(R[5], R[5], aim, ALU.mult))
        link(tt(R[2], R[2], R[5], ALU.subtract))
        link(tt(R[2], R[2], R[0], ALU.mult))
        dve.wait_ge(loads["second"], 80)

        def wide(r):
            return r.unsqueeze(2).to_broadcast([P, SSM_GROUPS, SSM_P])
        b1v, b2v = (t[:, :].rearrange("p (g q) -> p g q", q=SSM_P) for t in (bb1, bb2))
        T0, T1 = (lb[:, w, :, :].rearrange("p a b -> p (a b)").rearrange("p (g q) -> p g q", q=SSM_P)
                  for w in range(2))
        sgn, nsgn = L("sgn"), L("nsgn")
        link(ts(R[5], R[2], sgn, None, ALU.mult))
        link(ts(R[7], R[1], nsgn, None, ALU.mult))
        link(tt(T0, b1v, wide(R[1]), ALU.mult))
        link(tt(T1, b2v, wide(R[5]), ALU.mult))
        link(tt(T0, T0, T1, ALU.add))
        link(tt(T1, b2v, wide(R[7]), ALU.mult))
        link(tt(b2v, b1v, wide(R[2]), ALU.mult))
        link(tt(b2v, b2v, T1, ALU.add))
        link(nc.vector.tensor_copy(b1v, T0))
        link(ts(sC[:, 0, :, :], sC[:, 0, :, :], nsgn, None, ALU.mult))
        link(ts(sC[:, 1, :, :], sC[:, 1, :, :], -1.0, None, ALU.mult))
        nc.vector.memset(cpad[:, :, :], 0.0).then_inc(S("s_dve"), 1)
        ec, es, e3 = R[6], R[3], R[4]
        u1 = t1[:, :, :].rearrange("p a (g q) -> p (a g) q", q=8)
        u2 = t2[:, :, :].rearrange("p a (g q) -> p (a g) q", q=8)
        for cP, sP in ((cB, sB), (cA, sA)):
            link(nc.vector.memset(cP[:, :, 0:1], 1.0))
            link(nc.vector.memset(sP[:, :, 0:1], 0.0))
            for n in (1, 2, 4, 8):
                def e(r):
                    return r.unsqueeze(2).to_broadcast([P, SSM_GROUPS, n])
                link(tt(u1[:, :, 0:n], cP[:, :, 0:n], e(ec), ALU.mult))
                link(tt(u2[:, :, 0:n], sP[:, :, 0:n], e(es), ALU.mult))
                link(tt(cP[:, :, n:2 * n], u1[:, :, 0:n], u2[:, :, 0:n], ALU.subtract))
                link(tt(u1[:, :, 0:n], sP[:, :, 0:n], e(ec), ALU.mult))
                link(tt(u2[:, :, 0:n], cP[:, :, 0:n], e(es), ALU.mult))
                link(tt(sP[:, :, n:2 * n], u1[:, :, 0:n], u2[:, :, 0:n], ALU.add))
                link(tt(e3, ec, es, ALU.mult))
                link(tt(ec, ec, ec, ALU.mult))
                link(tt(es, es, es, ALU.mult))
                link(tt(ec, ec, es, ALU.subtract))
                link(ts(es, e3, 2.0, None, ALU.mult))
        nc.vector.memset(crs[:, :, :], 0.0).then_inc(S("m_crs"), 1)
        nc.vector.memset(rr[:, :], 0.0).then_inc(S("s_dve"), 1)
        with dve.Fori(0, SSM_CHUNKS) as j:
            restart()
            dve.wait_ge(S("mp_bt"), j + 1)
            for w in range(2):
                op = tt(lb[:, w, :, :], ps0[:, w * P:(w + 1) * P].unsqueeze(1).to_broadcast([P, 8, P]),
                        L("emask").unsqueeze(2).to_broadcast([P, 8, P]), ALU.mult)
            op.then_inc(S("m_lb"), 1)
            for g in range(8):
                dve.wait_ge(S("mp_bu"), 8 * j + g + 1)
                dve.wait_ge(S("m_tab"), 8 * j + g + 1)
                tt(t1[:, 0, :], ps1[:, 0:T], Ct[:, :], ALU.mult)
                tt(t1[:, 1, :], ps1[:, T:2 * T], St[:, :], ALU.mult).then_inc(S("m_x"), 1)
                dve.wait_ge(S("m_x"), 8 * j + g + 1)
                link(tt(xr[:, :], t1[:, 0, :], t1[:, 1, :], ALU.add))
                link(nc.vector.tensor_tensor_scan(rr[:, :], mag[:, bass.ds(8 * j + g, 1)].to_broadcast([P, T]),
                                                  xr[:, :], 0.0, ALU.mult, ALU.add))
                tt(crs[:, 0, :], rr[:, :], Ct[:, :], ALU.mult)
                tt(crs[:, 1, :], rr[:, :], St[:, :], ALU.mult).then_inc(S("m_crs"), 1)
            dve.wait_ge(S("mp_y"), 8 * j + 8)
            stt(yt[:, :], uT[:, j, :], V("ssm_d", j, 1), ps2[:, 0:T], ALU.mult, ALU.add).then_inc(S("m_y"), 1)
            dve.wait_ge(S("m_y"), j + 1)
            link(tt(yg[:, :], yt[:, :], yt[:, :], ALU.mult))
            link(ts(yg[:, :], yg[:, :], 0.044715, 1.0, ALU.mult, ALU.add))
            tt(yg[:, :], yg[:, :], yt[:, :], ALU.mult).then_inc(S("m_in"), 1)
            dve.wait_ge(S("m_t"), j + 1)
            link(stt(yt[:, :], yg[:, :], 1.0, yt[:, :], ALU.add, ALU.mult))
            ts(uT[:, j, :], yt[:, :], 0.5, None, ALU.mult).then_inc(S("m_yg"), 1)
            dve.wait_ge(S("m_yg"), j + 1)
            dve.wait_ge(S("m_hi"), j + 1)
            low(hid2[:, 16 + j, T:2 * T], uT[:, j, :], hid2[:, 16 + j, 0:T]).then_inc(S("m_lo"), 1)
        restart()
        for i in range(2):
            walk(Q_GLU + i, 4, split)
            for n in range(4):
                add(G_GLU + i, n, fxg[:, n, :])
            dve.wait_ge(S("glu_t"), i + 1)
            y4 = uT[:, 4 * i:4 * i + 4, :]
            link(ts(fxg[:, :, :], fxg[:, :, :], 1.0, 0.5, ALU.add, ALU.mult))
            tt(y4, y4, fxg[:, :, :], ALU.mult).then_inc(S("glu_y"), 1)
            dve.wait_ge(S("glu_y"), i + 1)
            dve.wait_ge(S("glu_hi"), i + 1)
            low(hid2[:, 4 * i:4 * i + 4, T:2 * T], y4, hid2[:, 4 * i:4 * i + 4, 0:T]).then_inc(S("glu_lo"), 1)
        with dve.Fori(0, 6) as i:
            walk(Q_QKV + 2 * i, 8, split)
            for n in range(4):
                add(G_QKV + i, n, att[:, 4 * i + n, :])
        dve.wait_ge(S("tp_set"), 1)
        tt(bvec[:, :], ps0[0:8, :], L("negrow")[0:8, :], ALU.add).then_inc(S("t_set"), 1)
        for n in range(4):
            dve.wait_ge(S("tp_set"), n + 2)
            nc.vector.tensor_copy(btab[:, 2 * n:2 * n + 2, :], ps0[:, :].rearrange("p (a i) -> p a i", a=2)
                                  ).then_inc(S("t_set"), 1)
        with dve.Fori(0, B_HEADS) as h:
            restart()
            dve.wait_ge(S("tp_s"), h + 1)
            tt(mSb[:, 0:P], ps0[:, 0:P], btab[:, h, P:2 * P], ALU.add)
            link(tt(mSb[:, P:3 * P], ps0[:, P:3 * P], btab[:, h, :], ALU.add))
            nc.vector.tensor_reduce(msm[:, 0:1], mSb[:, 0:P], AX.X, ALU.max, negate=True)
            nc.vector.tensor_reduce(msm[:, 1:2], mSb[:, P:3 * P], AX.X, ALU.max, negate=True
                                    ).then_inc(S("t_mx"), 1)
            dve.wait_ge(S("ta_e"), h + 1)
            link(nc.vector.reciprocal(msm[:, 4:6], msm[:, 2:4]))
            ts(mSb[:, 0:P], mSb[:, 0:P], msm[:, 4:5], None, ALU.mult)
            ts(mSb[:, P:3 * P], mSb[:, P:3 * P], msm[:, 5:6], None, ALU.mult).then_inc(S("t_p"), 1)
            dve.wait_ge(S("tp_o"), h + 1)
            nc.vector.tensor_copy(my[:, :], ps3[:, 0:T]).then_inc(S("t_y"), 1)
            dve.wait_ge(S("t_y"), h + 1)
            dve.wait_ge(S("t_hi"), h + 1)
            low(hid2[:, 8 + h, T:2 * T], my[:, :], hid2[:, 8 + h, 0:T]).then_inc(S("t_lo"), 1)
        with dve.Fori(0, 4) as i:
            restart()
            for gi, n, q in ((0, 8, 0), (1, 4, 2), (2, 8, 3), (3, 4, 5)):
                g = G_MRG + 4 * i + gi
                walk(Q_MRG + 6 * i + q, n, split)
                for c in range(4):
                    add(g, c, (sg if gi % 2 == 0 else mt)[:, c, :])
                added(g)
                if gi % 2 == 0:
                    dve.wait_ge(S("mg_t"), 2 * i + gi // 2 + 1)
                    link(ts(sg[:, :, :], sg[:, :, :], 1.0, 0.5, ALU.add, ALU.mult))
                elif gi == 1:
                    link(tt(macc[:, :, :], mt[:, :, :], sg[:, :, :], ALU.mult))
                else:
                    link(tt(mt[:, :, :], mt[:, :, :], sg[:, :, :], ALU.mult))
                    tt(macc[:, :, :], macc[:, :, :], mt[:, :, :], ALU.add).then_inc(S("mrg"), 1)
                    dve.wait_ge(S("mrg"), i + 1)
                    dve.wait_ge(S("mrg_hi"), i + 1)
                    o = hid2[:, bass.ds(16 + 4 * i, 4), :]
                    low(o[:, :, T:2 * T], macc[:, :, :], o[:, :, 0:T]).then_inc(S("mrg_lo"), 1)

        def gated_add(g, i, gate, before):
            for n in range(4):
                add(g, n, fx[:, n, :])
            added(g)
            for n in range(4):
                xk = x[:, 4 * i + n, :]
                op = stt(xk, fx[:, n, :], mod[:, bass.ds(gate + 4 * i + n, 1)], xk, ALU.mult, ALU.add)
            op.then_inc(x_ready, 1)
            dve.wait_ge(x_ready, before + 1)

        with dve.Fori(0, 4) as i:
            walk(Q_WO + 2 * i, 8, split)
            gated_add(G_WO + i, i, 32, X_READY[3] + i)
        restart()
        link(stt(norm_g[:, :], mod[:, 64:80], 1.0, V("mlp"), ALU.add, ALU.mult))
        norm(4, 3, norm_g)
        with dve.Fori(0, FF_QUARTERS) as c:
            with dve.Fori(0, 4) as i:
                walk(Q_FF + 16 * c + 2 * i, 8, split)
                g = G_FF + 8 * c + i
                for n in range(4):
                    add(g, n, fx[:, n, :])
                added(g)
                stt(mt[:, :, :], fx[:, :, :], 0.0, fx[:, :, :], ALU.max, ALU.mult).then_inc(S("ff"), 1)
                dve.wait_ge(S("ff"), 4 * c + i + 1)
                dve.wait_ge(S("ff_hi"), 4 * c + i + 1)
                o = hid2[:, bass.ds(4 * i, 4), :]
                low(o[:, :, T:2 * T], mt[:, :, :], o[:, :, 0:T]).then_inc(S("ff_lo"), 1)
            with dve.Fori(0, 4) as i:
                walk(Q_FF + 16 * c + 8 + 2 * i, 8, split)
                gated_add(G_FF + 8 * c + 4 + i, i, 80, X_READY[4] + 4 * c + i)
        norm(5, None, V("final2"), S("out_ready"))


def _pad_cols(a, n=P):
    out = np.zeros((n, a.shape[1]), np.float32)
    out[:a.shape[0]] = a
    return out


def constant_tables():
    i = np.arange(P)
    r, c = i[:, None], i[None, :]
    f = np.float32
    cst = {"ident": np.eye(P, dtype=f), "upper": (r <= c).astype(f), "ones": np.ones((P, P), f)}
    levels = []
    for lv in range(1, 7):
        b = 1 << lv
        left = np.concatenate([np.arange(m, m + b) for m in range(0, P, 2 * b)])
        levels.append(-((r // (2 * b) == left[None, :] // (2 * b)) & (r % (2 * b) >= b)).astype(f))
    nm0 = -((r // 2 == c // 2) & (r == c + 1)).astype(f)
    t = np.arange(2 * P)
    q, k = t[:, None], t[None, :]
    blocks = []
    for window, dil in ((128, 1), (512, 4), (2048, 16)):
        rel = q - k
        ok = (rel >= 0) & (rel % dil == 0) & (rel <= window)
        m = np.where(ok, 0.0, NEG).astype(f)
        blocks += [m[0:P, 0:P], m[P:, 0:P], m[P:, P:]]
    half = 16
    inv = np.power(f(500000.0), -np.arange(half, dtype=f) * f(2.0) / f(32))
    ang = (np.arange(T, dtype=f)[:, None] * inv[None, :]).astype(f)
    cos, sin = np.cos(ang).astype(f).T, np.sin(ang).astype(f).T
    rot = np.zeros((32, 32), f)
    for d in range(half):
        rot[d + half, d] = -1.0
        rot[d, d + half] = 1.0
    hyc = {
        "mask_t": np.where(c >= r, 0.0, NEG).astype(f), "mask_s": np.where(c < r, 0.0, -NEG).astype(f),
        "nm0": nm0, "nm0t": nm0.T, "levels": np.concatenate(levels, 1),
        "att_mask": np.concatenate(blocks, 1), "cos": _pad_cols(np.concatenate([cos, cos])),
        "sin": _pad_cols(np.concatenate([sin, sin])), "rot": _pad_cols(rot),
    }
    rel = 255 - np.arange(512)
    n = np.maximum(rel, 0)
    nf = np.maximum(n, 1).astype(f)
    large = 16 + (np.log(nf / f(16)) / f(math.log(128 / 16)) * f(16)).astype(np.int32)
    bucket = np.where(n < 16, n, np.minimum(large, 31))
    onehot = ((np.arange(32)[:, None] == bucket[None, :]) & (rel >= 0)[None, :]).astype(f)
    negrow = np.tile(np.where(rel >= 0, 0.0, NEG).astype(f)[None, :], (8, 1))
    top = (i < 64)
    ltc = {
        "flip": np.eye(P, dtype=f)[::-1], "onehot": _pad_cols(onehot), "negrow": _pad_cols(negrow),
        "emask": (i[:, None] // 16 == np.arange(8)[None, :]).astype(f),
        "sgn": np.where(top, -1.0, 1.0).astype(f)[:, None], "nsgn": np.where(top, 1.0, -1.0).astype(f)[:, None],
    }
    out = []
    for tabs, widths in ((cst, CONST_WIDTHS), (hyc, HYB_CONST_WIDTHS), (ltc, LATE_CONST_WIDTHS)):
        for name, w in widths:
            assert tabs[name].shape == (P, w), (name, tabs[name].shape)
        out.append(np.ascontiguousarray(np.concatenate([tabs[name] for name, _ in widths], 1), dtype=f))
    return out


def slabs(w, k_chunks, col_chunks):
    kc, nc_ = w.shape[0] // P, w.shape[1] // P
    v = w.reshape(kc, P, nc_, P)[np.asarray(k_chunks)][:, :, np.asarray(col_chunks)]
    v = v.reshape(len(k_chunks) // SLAB_K, SLAB_K, P, len(col_chunks) // SLAB_N, SLAB_N * P)
    return np.ascontiguousarray(v.transpose(3, 0, 2, 1, 4)).reshape(-1, P, SLAB)


def columns(v):
    return v.reshape(-1, P).T


def lay_out(i):
    f = {k: np.asarray(v) for k, v in i.items()}
    hyb = f["hyb_w_in"][0]
    order = []
    conv_order = []
    for h in range(QK_HEADS):
        qkv = [h, 8 + h, 16 + 2 * h, 17 + 2 * h]
        conv_order += qkv
        order += qkv + [32 + 2 * h, 33 + 2 * h] + [48 + h, 56 + h, 64 + h, 72 + h, 80 + h, 88 + h]
    main = np.concatenate([hyb[:, :6144], hyb[:, 6176:]], axis=1)
    k16, k24 = list(range(16)), list(range(24))
    outa = list(range(0, 12)) + list(range(16, 20))
    outb = list(range(12, 16)) + list(range(20, 24))
    sc = f["sc_w_in"][0]
    sc_order = []
    for j in range(N_SC_ITER):
        for part in (1, 2, 0, 3):
            sc_order += [24 * part + 4 * j + n for n in range(4)]
    w2 = f["w_in_2"][0]
    qkv2 = [8 + 8 * a + h for h in range(8) for a in range(3)]
    stream = [slabs(main, k16, order), slabs(f["hyb_w_out"][0], outa, k16), slabs(f["hyb_w_out"][0], outb, k16),
              slabs(sc, k16, sc_order), slabs(f["sc_w_out"][0], k24, k16),
              slabs(w2, k16, list(range(8))), slabs(f["w_glu_2"][0], list(range(8)), list(range(8))),
              slabs(w2, k16, qkv2)]
    for g in range(4):
        cols = list(range(4 * g, 4 * g + 4))
        stream += [slabs(w2, k16, [32 + c for c in cols]), slabs(f["w_proj_ssm_2"][0], list(range(8)), cols),
                   slabs(w2, k16, [48 + c for c in cols]), slabs(f["w_proj_attn_2"][0], list(range(8)), cols)]
    stream.append(slabs(f["w_out_2"][0], k16, k16))
    for c in range(FF_QUARTERS):
        ks = list(range(16 * c, 16 * c + 16))
        stream += [slabs(f["w_ff1_2"][0], k16, ks), slabs(f["w_ff2_2"][0], ks, k16)]
    stream.append(stream[0][:RING])
    stacked = lambda a: np.concatenate([a.T, a.T])
    b_re, b_im = (f[n][0].transpose(1, 0, 2).reshape(64, -1) for n in ("ssm_b_re_2", "ssm_b_im_2"))
    c_re, c_im = (f[n][0].transpose(2, 0, 1) for n in ("ssm_c_re_2", "ssm_c_im_2"))
    row = lambda v: np.broadcast_to(v[None, :], (P, v.shape[0]))
    vecs = {
        "norm0": columns(f["norm_w"][0]), "norm1": columns(f["norm_w"][1]), "final1": columns(f["final_norm_w"]),
        "mix": columns(f["norm_mix_g_2"][0]), "mlp": columns(f["norm_mlp_g_2"][0]),
        "final2": columns(f["norm_final_g_2"]),
        "dn_conv": f["dn_conv_w"][0].reshape(32, P, 4)[np.asarray(conv_order)].transpose(1, 0, 2).reshape(P, -1),
        "sc_conv": f["sc_conv_w"][0].reshape(24, P, 3).transpose(1, 0, 2).reshape(P, -1),
        "dn_norm": f["dn_norm_w"][0][:, None], "ssm_d": columns(f["ssm_d_2"][0]),
        "b_glu": columns(f["b_glu_2"][0]), "c": columns(f["c_2"][0]), "b_ada": columns(f["b_ada_2"][0]),
        "a_log": row(np.concatenate([f["dn_a_log"][0]] * 2)), "dt_bias": row(np.concatenate([f["dn_dt_bias"][0]] * 2)),
        "a_re": stacked(f["ssm_a_re_2"][0]), "a_im": stacked(f["ssm_a_im_2"][0]), "log_dt": row(f["ssm_log_dt_2"][0]),
    }
    cst, hyc, ltc = constant_tables()
    c_ = np.ascontiguousarray
    return {
        "stream": np.concatenate(stream, 0),
        "ada": slabs(f["w_ada_2"][0], k16, list(range(96))),
        "x": c_(f["x"][0].T.reshape(KC, P, T).transpose(1, 0, 2)),
        "vec": c_(np.concatenate([vecs[n] for n, _ in VEC_WIDTHS], 1)),
        "cst": cst, "hyc": hyc, "ltc": ltc,
        "wab": c_(hyb[:, 6144:6176].reshape(KC, P, 32).transpose(1, 0, 2)),
        "b1": c_(np.concatenate([b_re, b_im])), "b2": c_(np.concatenate([b_im, b_re])),
        "c12": c_(np.stack([np.concatenate([c_re, c_im]), np.concatenate([c_im, c_re])], 1)),
        "rel": c_(f["rel_bias_2"]),
    }


def kernel(**inputs):
    from contextlib import ExitStack

    import concourse.bacc as bacc
    from concourse.bass_utils import run_bass_kernel_spmd

    nc = bacc.Bacc("TRN2", target_bir_lowering=False, num_devices=1)
    arrays = lay_out(inputs)
    ins = {n: nc.dram_tensor(f"in_{n}", a.shape, F32, kind="ExternalInput").ap() for n, a in arrays.items()}
    out = nc.dram_tensor("out", (P, KC, T), F32, kind="ExternalOutput").ap()
    with ExitStack() as stack:
        program(nc, stack, ins, out)
    r = run_bass_kernel_spmd(nc, [{f"in_{n}": a for n, a in arrays.items()}], core_ids=[0])
    got = r.results[0]["out"]
    return np.ascontiguousarray(got.transpose(1, 0, 2).reshape(1, D, T).transpose(0, 2, 1))
```

```python
import math

import numpy as np

import concourse.bass as bass
from concourse import mybir

P = 128
T = 256
D = 2048
KC = D // P
EPS = 1e-6
NEG = -1e30

F32 = mybir.dt.float32
F32R = mybir.dt.float32r
ALU = mybir.AluOpType
ACT = mybir.ActivationFunctionType
AX = mybir.AxisListType

QK_HEADS = 8
V_HEADS = 16
B_HEADS = 8
PATTERNS = 3
SC_CHUNKS = 3072 // P
SSM_GROUPS = 64
SSM_P = 16
SSM_CHUNKS = SSM_GROUPS * SSM_P // P
FF_QUARTERS = 4
DK_SCALE = float(P) ** -0.5

SLAB_K = 2
SLAB_N = 4
SLAB = SLAB_K * SLAB_N * P
RING = 4
AHEAD = 3
POOL_ALL = (0, 1, 2, 3)
POOL_REST = (1, 3)
KSLABS = KC // SLAB_K

HYB_GROUPS_PER_HEAD = 3
N_HYB = QK_HEADS * HYB_GROUPS_PER_HEAD
OUT_A_K, OUT_B_K = 16, 8
SC_GROUPS = 4
N_SC_ITER = SC_CHUNKS // SLAB_N
ADA_GROUPS = 24
ADA_RING = 4


VEC_WIDTHS = [
    ("norm0", 16), ("norm1", 16), ("final1", 16), ("mix", 16), ("mlp", 16), ("final2", 16),
    ("dn_conv", 8 * 4 * 4), ("sc_conv", 24 * 3), ("dn_norm", 1), ("ssm_d", 8), ("b_glu", 8),
    ("c", 16), ("b_ada", 96), ("a_log", 32), ("dt_bias", 32),
    ("a_re", 64), ("a_im", 64), ("log_dt", 64),
]
CONST_WIDTHS = [
    ("ident", 128), ("upper", 128), ("ones", 128),
]
HYB_CONST_WIDTHS = [
    ("mask_t", 128), ("mask_s", 128), ("nm0", 128), ("nm0t", 128), ("levels", 6 * 64),
    ("att_mask", 3 * 384), ("cos", 256), ("sin", 256), ("rot", 32),
]
LATE_CONST_WIDTHS = [("flip", 128), ("onehot", 512), ("negrow", 512), ("emask", 8), ("sgn", 1), ("nsgn", 1)]


def offsets(widths):
    at, out = 0, {}
    for name, w in widths:
        out[name] = (at, w)
        at += w
    return out, at


VEC, VEC_N = offsets(VEC_WIDTHS)
CST, CST_N = offsets(CONST_WIDTHS)
HYC, HYC_N = offsets(HYB_CONST_WIDTHS)
LTC, LTC_N = offsets(LATE_CONST_WIDTHS)


def wait(eng, sem, value):
    if isinstance(value, int) and value <= 0:
        return
    eng.wait_ge(sem, value)


def program(nc, stack, ins, out_d):
    base0 = 16512
    top = [base0]
    named = [0]

    def place(name, shape, dt=F32):
        n = 4
        for s in shape[1:]:
            n *= s
        n = (n + 31) // 32 * 32
        t = nc.alloc_sbuf_tensor_at(name, list(shape), dt, offset=top[0])
        top[0] += n
        assert top[0] <= 229368, (name, top[0])
        return t

    raw = place("raw", [P, RING, SLAB])
    wh = place("wh", [P, RING, SLAB], F32R)
    wl = place("wl", [P, RING, SLAB], F32R)
    xs_at = top[0]
    xs = place("xs", [P, KC, 2 * T], F32R)
    tmp = place("tmp", [P, 4, T])
    vec = place("vec", [P, VEC_N])
    cst = place("cst", [P, CST_N])
    mod = place("mod", [P, 96])
    norm_g = place("norm_g", [P, KC])
    cact = place("cact", [P, KC])
    cth = place("cth", [P, KC])
    nrm = place("nrm", [P, 8])
    rn = place("rn", [P, 8])
    mhalf = place("mhalf", [P, 8])
    dnh = place("dnh", [P, 8])
    hid_at = top[0]
    hid = place("hid", [P, 24, 2 * T], F32R)
    arena = top[0]
    hid2 = nc.alloc_sbuf_tensor_at("hid2", [P, 32, 2 * T], F32R, offset=hid_at)
    arena2 = hid_at + 32 * 2 * T * 4
    x_at = 229344 - KC * T * 4
    x_at -= x_at % 32
    x = nc.alloc_sbuf_tensor_at("x", [P, KC, T], F32, offset=x_at)
    xacc = nc.alloc_sbuf_tensor_at("xacc", [P, KC, T], F32, offset=xs_at)

    def V(name, a=0, n=None):
        at, w = VEC[name]
        n = w - a if n is None else n
        if isinstance(a, int):
            return vec[:, at + a:at + a + n]
        return vec[:, bass.ds(at + a, n)]

    def C(name):
        at, w = CST[name]
        return cst[:, at:at + w]

    ident, upper, ones = C("ident"), C("upper"), C("ones")

    top[0] = arena + 16384
    nsq0 = place("nsq0", [P, 4, T])
    nyb0 = place("nyb0", [P, 4, T])
    assert top[0] <= x_at

    top[0] = arena
    hyc = place("hyc", [P, HYC_N])

    def H(name):
        at, w = HYC[name]
        return hyc[:, at:at + w]

    cb = place("cb", [P, 4, 4 + T])
    qkv = place("qkv", [P, 4, T])
    th = place("th", [P, 4, T])
    sqq = th
    zz = place("zz", [P, 2, T])
    zs = place("zs", [P, 2, T])
    gA = place("gA", [P, 4, P])
    gB = place("gB", [P, 4, P])
    eg = place("eg", [P, 2, P])
    kb = place("kb", [P, 4, P])
    kd = place("kd", [P, 2, P])
    rhsv = place("rhsv", [P, 4, P])
    wab_off = top[0]
    AT = place("AT", [P, 4, P])
    Dm = place("Dm", [P, 4, P])
    Em = place("Em", [P, 4, P])
    Xm = place("Xm", [P, 4, 64])
    vn0 = place("vn0", [P, 2, P])
    wTn = place("wTn", [P, 2, P])
    Sst = place("Sst", [P, 2, P])
    vn1 = place("vn1", [P, 2, P])
    qe = place("qe", [P, 2, P])
    gsel = place("gsel", [P, 4])
    gcum = place("gcum", [P, V_HEADS, 2])
    gnat = place("gnat", [P, V_HEADS, 2])
    ngcum = place("ngcum", [P, V_HEADS, 2])
    beta = place("beta", [P, V_HEADS, 2])
    bhalf = place("bhalf", [P, V_HEADS, 2])
    bexp = place("bexp", [P, V_HEADS, 2])
    kdecf = place("kdecf", [P, V_HEADS, 2])
    gt = place("gt", [P, 6, 2 * V_HEADS])
    bb = place("bb", [P, 6, T])
    rb = place("rb", [32, 2, T])
    Sb = place("Sb", [P, PATTERNS, 384])
    Pb = place("Pb", [P, 384])
    PT = place("PT", [P, 384])
    vnat = place("vnat", [P, T])
    bzs = place("bzs", [P, T])
    bth = place("bth", [P, T])
    yb = place("yb", [P, T])
    smx = place("smx", [P, 8])
    osb, sqo = AT, Dm
    yh = kb
    wab_at = nc.alloc_sbuf_tensor_at("wab", [P, KC, 32], F32, offset=wab_off)
    wabh = nc.alloc_sbuf_tensor_at("wabh", [P, KC, 32], F32R, offset=wab_off + 2048)
    wabl = nc.alloc_sbuf_tensor_at("wabl", [P, KC, 32], F32R, offset=wab_off + 4096)

    top[0] = arena
    top[0] = arena
    cc = place("cc", [P, 4, T])
    uu = place("uu", [P, 4, T])
    pc = place("pc", [P, 4, 2 + T])
    yv = place("yv", [P, 4, T])
    sth = place("sth", [P, 4, T])
    sc_end = top[0]
    top[0] = x_at - 4 * (4 * SLAB + 512)
    ada_at = top[0]
    araw = place("araw", [P, ADA_RING, SLAB])
    aacc = place("aacc", [P, 512])
    assert sc_end <= ada_at and top[0] <= x_at

    top[0] = arena2
    ltc = place("ltc", [P, LTC_N])
    rel_sb = place("rel_sb", [32, 8])
    bgh = place("bgh", [P, 8])

    def L(name):
        at, w = LTC[name]
        return ltc[:, at:at + w]
    second = top[0]
    trg = place("trg", [P, 8, SSM_GROUPS])
    mag = place("mag", [P, SSM_GROUPS])
    assert sc_end <= second
    ssm_at = top[0]
    uT = place("uT", [P, SSM_CHUNKS, T])
    cB = place("cB", [P, SSM_GROUPS, 16])
    sB = place("sB", [P, SSM_GROUPS, 16])
    bb1 = place("bb1", [P, SSM_GROUPS * SSM_P])
    bb2 = place("bb2", [P, SSM_GROUPS * SSM_P])
    sC = place("sC", [P, 2, SSM_GROUPS, SSM_P])
    assert top[0] <= x_at, (top[0], x_at)
    top[0] = hid_at
    cA = place("cA", [P, SSM_GROUPS, 16])
    sA = place("sA", [P, SSM_GROUPS, 16])
    lb = place("lb", [P, 2, 8, P])
    cpad = place("cpad", [P, 2, 8 * 144])
    stage = place("stage", [P, 4, T])
    prod0s = place("prod0s", [P, 2, T])
    assert top[0] <= hid_at + 16 * 2 * T * 4, (top[0] - hid_at)
    top[0] = hid_at + 24 * 2 * T * 4
    CS = place("CS", [P, 2, T])
    t1 = place("t1", [P, 2, T])
    prod0c = place("prod0c", [P, 2, T])
    prod1c = place("prod1c", [P, 2, T])
    rr = place("rr", [P, T])
    crs = place("crs", [P, 2, 2, T])
    bs = place("bs", [P, 2, P])
    yt = place("yt", [P, T])
    yg = place("yg", [P, T])
    prod1s = nc.alloc_sbuf_tensor_at("prod1s", [P, 2, T], F32, offset=second)
    prods = ((prod0c, prod0s), (prod1c, prod1s))
    assert top[0] <= hid_at + 32 * 2 * T * 4, (top[0] - hid_at)

    fxg = nc.alloc_sbuf_tensor_at("fxg", [P, 4, T], F32, offset=ssm_at + 8 * T * 4)
    top[0] = second
    att = place("att", [P, 24, T])
    btab = place("btab", [P, 8, 256])
    assert top[0] <= x_at, (top[0], x_at)
    top[0] = hid_at + 24 * 2 * T * 4
    bvec = nc.alloc_sbuf_tensor_at("bvec", [8, 512], F32, offset=top[0])
    qvs = place("qvs", [P, 2, T])
    mSb = place("mSb", [P, 384])
    mPT = place("mPT", [P, 384])
    mvn = place("mvn", [P, T])
    my = place("my", [P, T])
    msm = place("msm", [P, 8])
    toep_at = top[0]
    toep = place("toep", [P, 8, 256])
    assert top[0] <= hid_at + 32 * 2 * T * 4
    top[0] = toep_at
    ATT_BUFS = ((qvs, mSb, mPT, mvn, my, msm), (place("qvs1", [P, 2, T]), place("mSb1", [P, 384]),
                place("mPT1", [P, 384]), place("mvn1", [P, T]), place("my1", [P, T]), place("msm1", [P, 8])))

    top[0] = second
    sg = place("sg", [P, 4, T])
    mt = place("mt", [P, 4, T])
    macc = place("macc", [P, 4, T])
    assert top[0] <= ada_at
    fx = nc.alloc_sbuf_tensor_at("fx", [P, 4, T], F32, offset=second)

    def sem(name):
        return stack.enter_context(nc.semaphore(name))

    G = [stack.enter_context(nc.psum_tensor(f"gemm{n}", [P, 512], F32)) for n in range(4)]
    ps0, ps1, ps2, ps3 = [stack.enter_context(nc.psum_tensor(f"side{n}", [P, 512], F32)) for n in range(4)]
    ATT_BANKS = ((ps0, ps1, ps2, ps3), G)
    stash = nc.dram_tensor("stash", (8, P, 4 * T), F32).ap()
    bias_dram = nc.dram_tensor("bias_scratch", (8, 512), F32).ap()

    raw_in = [sem(f"raw_in{n}") for n in range(RING)]
    ada_in = [sem(f"ada_in{n}") for n in range(ADA_RING)]
    hi_ready = sem("hi_ready")
    lo_ready = [sem(f"lo_ready{n}") for n in range(RING)]
    slab_used = sem("slab_used")
    bank_ready, bank_freed = sem("bank_ready"), sem("bank_freed")
    tmp_ready = sem("tmp_ready")
    loads = {n: sem("in_" + n) for n in ("x", "hyb", "first", "second", "xback", "toep", "bias", "stash", "att", "gate")}
    x_ready = sem("x_ready")
    norm_sq, norm_sum, norm_var, norm_rn, norm_bc = (sem("norm_" + n) for n in ("sq", "sum", "var", "rn", "bc"))
    norm_y, norm_hi, xs_ready = sem("norm_y"), sem("norm_hi"), sem("xs_ready")
    dve_step, act_step, pool_step = sem("dve_step"), sem("act_step"), sem("pool_step")
    setup = sem("setup")
    Z = {}

    def S(name):
        if name not in Z:
            Z[name] = sem(name)
        return Z[name]

    def wait_lo(eng, q, slot):
        wait(eng, lo_ready[slot], q + 1)

    def walk(q0, nslabs, split, hook=None, slot0=0, pool=POOL_REST, after=None):
        for sl in range(nslabs):
            nxt = sl + AHEAD
            split(q0 + nxt // RING, nxt % RING, pool if after is None or nxt < nslabs else after)
            if hook is not None:
                hook(slot0 + 2 * sl)
                hook(slot0 + 2 * sl + 1)

    Q_OUTA = N_HYB * 2
    Q_OUTB = Q_OUTA + 4 * OUT_A_K // 8
    Q_SC = Q_OUTB + 4 * OUT_B_K // 8
    Q_SCOUT = Q_SC + 24 * 2
    Q_U = Q_SCOUT + 4 * 3
    Q_MIX = Q_U + 2 * 2
    Q_GLU = Q_MIX + 8 * 2
    Q_QKV = Q_GLU + 2 * 1
    Q_MRG = Q_QKV + 2 * 2
    Q_WO = Q_MRG + 4 * 4
    Q_FF = Q_WO + 4 * 2
    Q_END = Q_FF + 4 * 16
    G_OUTA = N_HYB
    G_OUTB, G_SC = G_OUTA + 4, G_OUTA + 8
    G_SCOUT = G_SC + 24
    G_U = G_SCOUT + 4
    G_MIX = G_U + 2
    G_GLU, G_QKV = G_MIX + 8, G_MIX + 10
    G_MRG = G_QKV + 2
    G_WO = G_MRG + 12
    G_FF = G_WO + 4
    assert Q_END * 4 == ins["stream"].shape[0] - RING

    DELTA_AT = {1 + int(s * 1.55): s for s in range(29)}
    ATTN_AT = {**{3 + 4 * k: k for k in range(8)}, 25: 8}
    outa_chunks = list(range(0, 12)) + list(range(16, 20))
    outb_chunks = list(range(12, 16)) + list(range(20, 24))

    TAP_AT = {17: 0, 19: 1, 21: 2, 23: 3}
    GATE_PE, GATE_ACT = {33: 0, 39: 1}, {18: 0, 35: 1, 37: 2, 41: 3}
    GATE_DVE = {20: 0, 34: 1, 36: 2, 38: 3, 40: 4, 42: 5}

    TABLE_AT = {s: g for g, s in enumerate((0, 1, 3, 4, 6, 8, 9, 11))}
    SCAN_AT = {s: g for g, s in enumerate((2, 3, 5, 6, 8, 10, 11, 13))}
    SUM_AT = {5: (0,), 6: (1,), 8: (2,), 10: (3,), 11: (4,), 13: (5,), 15: (6, 7)}

    ADA_2 = {2 * m: m for m in range(8)}
    ADA_3 = {3 * (m // 2) + m % 2: m for m in range(8)}
    ADA_1 = {m: m for m in range(8)}
    A_SCOUT = 12
    A_MRG = A_SCOUT + 4
    A_WO = A_MRG + 4

    X_READY = {0: 0, 1: 4, 2: 8, 3: 12, 4: 16, 5: 32}
    SQ_BEFORE = {0: 0, 1: 4, 2: 8, 3: 12, 4: 16, 5: 20 + 4 * (FF_QUARTERS - 1)}
    norm_bufs = {0: (nsq0, nyb0), 1: (cc, sth), 2: (cc, sth), 3: (cc, sth), 4: (macc, mt), 5: (macc, mt)}

    def shift_of(n):
        return {3: mod[:, 0:16], 4: mod[:, 48:64]}.get(n)

    def four(ap):
        return ap.unsqueeze(1).to_broadcast([P, 4, ap.shape[1]])

    block = stack.enter_context(nc.Block())

    @block.sync
    def _(sp):
        sp.dma_start(x[:], ins["x"]).then_inc(loads["x"], 16)
        sp.dma_start(vec[:], ins["vec"]).then_inc(loads["first"], 16)
        sp.dma_start(cst[:], ins["cst"]).then_inc(loads["first"], 16)

        def slab(q, slot):
            if not (isinstance(q, int) and q == 0):
                wait_lo(sp, q - 1, slot)
            sp.dma_start(raw[:, slot, :], ins["stream"][4 * q + slot]).then_inc(raw_in[slot], 16)

        for slot in range(RING):
            slab(0, slot)
        sp.dma_start(hyc[:], ins["hyc"]).then_inc(loads["hyb"], 16)
        sp.dma_start(wab_at[:], ins["wab"]).then_inc(loads["hyb"], 16)
        with sp.Fori(1, Q_SC) as q:
            for slot in range(RING):
                slab(q, slot)
        def ada(g, m):
            if not (isinstance(g, int) and g == 0 and m < ADA_RING):
                sp.wait_ge(S("ada_used"), 8 * g + m - ADA_RING + 1)
            sp.dma_start(araw[:, m % ADA_RING, :], ins["ada"][8 * g + m]).then_inc(ada_in[m % ADA_RING], 16)

        def quads(q0, n, g, at, first=0):
            for sl in range(first, 4 * n):
                slab(q0 + sl // RING, sl % RING)
                if sl in at:
                    ada(g, at[sl])

        sp.wait_ge(S("first_done"), 1)
        quads(Q_SC, 4, 0, ADA_2)
        with sp.Fori(1, 12) as i:
            quads(Q_SC + 4 * i, 4, i, ADA_2)
        with sp.Fori(0, 4) as i:
            quads(Q_SCOUT + 3 * i, 3, A_SCOUT + i, ADA_3)
        with sp.Fori(Q_U, Q_MRG) as q:
            quads(q, 1, 0, {})
        quads(Q_MRG, 1, 0, {})
        sp.wait_ge(S("t_lo"), B_HEADS)
        ada(A_MRG, 0)
        ada(A_MRG, 1)
        quads(Q_MRG, 4, A_MRG, ADA_2, RING)
        with sp.Fori(1, 4) as i:
            quads(Q_MRG + 4 * i, 4, A_MRG + i, ADA_2)
        def late(q0, g, own, before):
            for sl in range(own):
                slab(q0 + sl // RING, sl % RING)
                if sl >= 3:
                    ada(g, sl - 3)
                elif before:
                    ada(g - 1, 5 + sl)

        late(Q_WO, A_WO, 8, False)
        with sp.Fori(1, 4) as i:
            late(Q_WO + 2 * i, A_WO + i, 8, True)
        late(Q_FF, ADA_GROUPS, 3, True)
        slab(Q_FF, 3)
        with sp.Fori(Q_FF + 1, Q_END + 1) as q:
            quads(q, 1, 0, {})
        for slot in range(RING):
            sp.wait_ge(raw_in[slot], 16 * (Q_END + 1))
        for k in range(4):
            sp.wait_ge(S("out_ready"), k + 1)
            sp.dma_start(out_d[:, 4 * k:4 * k + 4, :], x[:, 4 * k:4 * k + 4, :]).then_inc(S("out_stored"), 16)
        sp.wait_ge(S("out_stored"), 64)

    @block.tensor
    def _(pe):
        mm = nc.tensor.matmul

        def group(g, q0, nslabs, rhs, ready, hook=None, slot0=0):
            for sl in range(nslabs):
                q, slot = q0 + sl // RING, sl % RING
                wait(pe, hi_ready, 4 * q + slot + 1)
                wait_lo(pe, q, slot)
                ready(sl)
                for n in range(SLAB_N):
                    if sl == 0:
                        wait(pe, bank_freed, 4 * g + n - 3)
                    for k in range(SLAB_K):
                        xk = rhs(sl * SLAB_K + k)
                        at = (k * SLAB_N + n) * P
                        first = sl == 0 and k == 0
                        last = sl == nslabs - 1 and k == SLAB_K - 1
                        mm(G[n][:, :], wh[:, slot, at:at + P], xk, start=first, stop=False,
                           skip_group_check=True)
                        op = mm(G[n][:, T:2 * T], wl[:, slot, at:at + P], xk[:, 0:T], start=False, stop=last,
                                skip_group_check=True)
                    if n == SLAB_N - 1:
                        op.then_inc(slab_used, 1)
                    elif sl == nslabs - 1:
                        op.then_inc(bank_ready, 1)
                    if hook is not None and n % 2 == 1:
                        hook(slot0 + 2 * sl + n // 2)

        def xs_of(k):
            return xs[:, k, :]

        def xs_wait(m):
            def ready(sl):
                if sl % 2 == 0:
                    wait(pe, xs_ready, 4 * m + sl // 2 + 1)
            return ready

        def norm(n):
            wait(pe, norm_sq, SQ_BEFORE[n] + 4)
            for j in range(4):
                for c in range(2):
                    op = mm(ps0[:, c:c + 1], norm_bufs[n][0][:, j, c * P:(c + 1) * P], ones[:, 0:1],
                            start=(j == 0 and c == 0), stop=(j == 3), skip_group_check=True)
            op.then_inc(norm_sum, 1)
            wait(pe, norm_rn, n + 1)
            for c in range(2):
                op = mm(ps1[:, c * P:(c + 1) * P], rn[:, c:c + 1].to_broadcast([P, P]), ident, start=True, stop=True)
            op.then_inc(norm_bc, 1)

        def gates(step):
            if step == 0:
                pe.wait_ge(S("gate_dve"), 1)
                for c in range(2):
                    for k in range(KC):
                        lh = xs[:, k, c * P:(c + 1) * P]
                        ll = xs[:, k, T + c * P:T + (c + 1) * P]
                        o = ps0[:, 32 * c:32 * c + 32]
                        mm(o, lh, wabh[:, k, :], start=(k == 0), stop=False, skip_group_check=True)
                        mm(o, lh, wabl[:, k, :], start=False, stop=False, skip_group_check=True)
                        op = mm(o, ll, wabh[:, k, :], start=False, stop=(k == KC - 1), skip_group_check=True)
                op.then_inc(S("gate_pe"), 1)
            elif step == 1:
                pe.wait_ge(S("gate_dve"), 4)
                for c in range(2):
                    mm(ps1[:, 16 * c:16 * c + 16], upper, gnat[:, :, c], start=True, stop=True)
                    op = mm(ps1[:, 32 + 16 * c:48 + 16 * c], ones, gnat[:, :, c], start=True, stop=True)
                op.then_inc(S("gate_pe"), 1)

        def delta(s, it):
            if s == 0:
                pe.wait_ge(S("d_sq"), it + 1)
                for a in range(2):
                    for c in range(2):
                        op = mm(ps0[:, 2 * a + c:2 * a + c + 1], sqq[:, a, c * P:(c + 1) * P], ones[:, 0:1],
                                start=True, stop=True)
                op.then_inc(S("p_norm"), 1)
            elif s == 1:
                pe.wait_ge(S("l_rn"), it + 1)
                for j in range(4):
                    mm(ps0[:, j * P:(j + 1) * P], rn[:, j:j + 1].to_broadcast([P, P]), ident, start=True, stop=True)
                for j in range(4):
                    op = mm(ps1[:, j * P:(j + 1) * P], gsel[:, j:j + 1].to_broadcast([P, P]), upper,
                            start=True, stop=True)
                op.then_inc(S("p_bc"), 1)
            elif s == 2:
                pe.wait_ge(S("d_qk"), it + 1)
                for c in range(2):
                    kc_ = qkv[:, 1, c * P:(c + 1) * P]
                    mm(ps2[:, c * P:(c + 1) * P], kc_, kc_, start=True, stop=True)
                    op = mm(ps2[:, (2 + c) * P:(3 + c) * P], kc_, qkv[:, 0, c * P:(c + 1) * P], start=True, stop=True)
                op.then_inc(S("p_kk"), 1)
            elif s == 3:
                pe.wait_ge(S("d_gm"), it + 1)
                pe.wait_ge(S("a_eg"), it + 1)
                for c in range(2):
                    nc.tensor.transpose(ps0[:, c * P:(c + 1) * P], qkv[:, 1, c * P:(c + 1) * P], ident)
                for j in range(4):
                    op = nc.tensor.transpose(ps1[:, j * P:(j + 1) * P],
                                             qkv[:, 2 + j // 2, (j % 2) * P:(j % 2 + 1) * P], ident)
                op.then_inc(S("p_nat"), 1)
            elif s == 4:
                pe.wait_ge(S("d_A"), it + 1)
                for j in range(4):
                    op = nc.tensor.transpose(ps2[:, j * P:(j + 1) * P], gB[:, j, :], ident)
                op.then_inc(S("p_AT"), 1)
            elif s < 23:
                lv, part = (s - 5) // 3 + 1, (s - 5) % 3
                b = 1 << lv
                if part == 0:
                    wait(pe, S("d_D"), 7 * it + lv)
                    if lv == 1:
                        pe.wait_ge(S("a_nat"), it + 1)
                    for j in range(4):
                        left = Dm[:, j, :].rearrange("p (m two b) -> p m two b", two=2, b=b)[:, :, 0, :]
                        op = mm(ps0[:, j * 64:(j + 1) * 64], AT[:, j, :], left, start=True, stop=True)
                    op.then_inc(S("p_X"), 1)
                elif part == 1:
                    wait(pe, S("d_X"), 6 * it + lv)
                    if lv > 1:
                        wait(pe, S("a_E"), 6 * it + lv - 1)
                    for j in range(4):
                        op = mm(ps0[:, 256 + j * 64:256 + (j + 1) * 64], Em[:, j, :], Xm[:, j, :], start=True, stop=True)
                    op.then_inc(S("p_DX"), 1)
                else:
                    wait(pe, S("d_D"), 7 * it + lv + 1)
                    for j in range(4):
                        op = nc.tensor.transpose(ps1[:, j * P:(j + 1) * P], Dm[:, j, :], ident)
                    op.then_inc(S("p_E"), 1)
            elif s == 23:
                wait(pe, S("a_E"), 6 * it + 6)
                for v in range(2):
                    mm(ps2[:, v * P:(v + 1) * P], Em[:, 2 * v, :], rhsv[:, 2 * v, :], start=True, stop=True)
                    op = mm(ps2[:, (2 + v) * P:(3 + v) * P], kb[:, 2 * v + 1, :], Em[:, 2 * v + 1, :],
                            start=True, stop=True)
                op.then_inc(S("p_v0"), 1)
            elif s == 24:
                pe.wait_ge(S("a_v0"), it + 1)
                for v in range(2):
                    op = mm(ps0[:, v * P:(v + 1) * P], kd[:, v, :], vn0[:, v, :], start=True, stop=True)
                op.then_inc(S("p_S"), 1)
            elif s == 25:
                pe.wait_ge(S("d_S"), it + 1)
                for v in range(2):
                    o = ps0[:, (2 + v) * P:(3 + v) * P]
                    mm(o, Em[:, 2 * v + 1, :], rhsv[:, 2 * v + 1, :], start=True, stop=False)
                    op = mm(o, wTn[:, v, :], Sst[:, v, :], start=False, stop=True)
                op.then_inc(S("p_v1"), 1)
            elif s == 26:
                pe.wait_ge(S("d_v1"), it + 1)
                for v in range(2):
                    mm(ps1[:, 2 * v * P:(2 * v + 1) * P], vn0[:, v, :], gA[:, 2 * v, :], start=True, stop=True)
                    o = ps1[:, (2 * v + 1) * P:(2 * v + 2) * P]
                    mm(o, Sst[:, v, :], qe[:, v, :], start=True, stop=False)
                    op = mm(o, vn1[:, v, :], gA[:, 2 * v + 1, :], start=False, stop=True)
                op.then_inc(S("p_o"), 1)
            elif s == 27:
                pe.wait_ge(S("a_o"), it + 1)
                for j in range(4):
                    op = mm(ps2[:, j:j + 1], sqo[:, j, :], ones[:, 0:1], start=True, stop=True)
                op.then_inc(S("p_osum"), 1)
            elif s == 28:
                pe.wait_ge(S("l_orn"), it + 1)
                for j in range(4):
                    op = mm(ps2[:, j * P:(j + 1) * P], rn[:, 4 + j:5 + j].to_broadcast([P, P]), ident,
                            start=True, stop=True)
                op.then_inc(S("p_obc"), 1)

        def attn(k, it):
            if k < 2:
                pe.wait_ge(bank_freed, 12 * it + 12)
                if k == 1:
                    pe.wait_ge(S("b_rope"), 2 * it + 1)
                mm(ps3[0:32, :], H("rot"), bb[:, 2 * k:2 * k + 2, :], start=True, stop=True
                   ).then_inc(S("bp_rope"), 1)
            elif k == 2:
                pe.wait_ge(S("b_rope"), 2 * it + 2)
                for c in range(2):
                    op = nc.tensor.transpose(ps3[:, c * P:(c + 1) * P], bb[:, 4, c * P:(c + 1) * P], ident)
                op.then_inc(S("bp_vn"), 1)
            elif k == 3:
                pe.wait_ge(S("b_vn"), it + 1)
                for a in range(PATTERNS):
                    op = mm(ps3[:, a * P:(a + 1) * P], bb[:, a, 0:P], bb[:, 3, 0:P], start=True, stop=True)
                op.then_inc(S("bp_s"), 1)
            elif k == 4:
                pe.wait_ge(S("b_s"), 3 * it + 1)
                for a in range(2):
                    op = mm(ps3[:, a * T:(a + 1) * T], bb[:, a, P:T], bb[:, 3, :], start=True, stop=True)
                op.then_inc(S("bp_s"), 1)
            elif k == 5:
                pe.wait_ge(S("b_s"), 3 * it + 2)
                mm(ps3[:, 0:T], bb[:, 2, P:T], bb[:, 3, :], start=True, stop=True).then_inc(S("bp_s"), 1)
            elif k == 6:
                pe.wait_ge(S("b_p"), it + 1)
                for j in range(3):
                    op = nc.tensor.transpose(ps3[:, j * P:(j + 1) * P], Pb[:, j * P:(j + 1) * P], ident)
                op.then_inc(S("bp_pt"), 1)
            elif k == 7:
                pe.wait_ge(S("b_pt"), it + 1)
                mm(ps3[:, 0:T], vnat[:, 0:P], PT[:, 0:T], start=True, stop=False, skip_group_check=True)
                mm(ps3[:, P:T], vnat[:, P:T], PT[:, T:T + P], start=False, stop=True,
                   skip_group_check=True).then_inc(S("bp_o"), 1)

        def heads(it):
            def hook(slot):
                if slot in DELTA_AT:
                    delta(DELTA_AT[slot], it)
                if slot in ATTN_AT:
                    attn(ATTN_AT[slot], it)
            return hook

        pe.wait_ge(loads["first"], 32)
        pe.wait_ge(setup, 1)
        norm(0)
        for gi in range(3):
            group(gi, 2 * gi, 8, xs_of, xs_wait(0), lambda slot: gates(GATE_PE.get(slot)), 16 * gi)
        pe.wait_ge(loads["hyb"], 32)
        with pe.Fori(1, QK_HEADS) as h:
            for gi in range(3):
                group(3 * h + gi, 6 * h + 2 * gi, 8, xs_of, lambda sl: None, heads(h - 1), 16 * gi)

        def hid_of(chunks):
            return lambda k: hid[:, chunks[k], :]

        def outa_ready(sl):
            wait(pe, S("ya_lo"), 6)
            wait(pe, S("yb_lo"), 4)

        for gi in range(3):
            group(G_OUTA + gi, Q_OUTA + 2 * gi, 8, hid_of(outa_chunks), outa_ready, heads(7), 16 * gi)
        group(G_OUTA + 3, Q_OUTA + 6, 8, hid_of(outa_chunks), outa_ready)

        def outb_ready(sl):
            wait(pe, S("ya_lo"), 8)
            wait(pe, S("yb_lo"), 8)

        with pe.Fori(0, 4) as i:
            group(G_OUTB + i, Q_OUTB + i, 4, hid_of(outb_chunks), outb_ready)
        norm(1)

        def ada_sum(g):
            pe.wait_ge(S("ada_used"), 8 * g + 8)
            for n in range(4):
                op = mm(ps2[:, n:n + 1], aacc[:, n * P:(n + 1) * P], ones[:, 0:1], start=True, stop=True)
            op.then_inc(S("ada_sum"), 1)

        with pe.Fori(0, N_SC_ITER) as j:
            for gi in range(4):
                group(G_SC + 4 * j + gi, Q_SC + 8 * j + 2 * gi, 8, xs_of, xs_wait(1))
                if gi % 2 == 1:
                    ada_sum(2 * j + gi // 2)

        def sc_ready(sl):
            if sl % 2 == 0:
                wait(pe, S("sc_lo"), sl // 2 + 1)

        with pe.Fori(0, 4) as i:
            group(G_SCOUT + i, Q_SCOUT + 3 * i, 12, lambda k: hid[:, k, :], sc_ready)
            ada_sum(A_SCOUT + i)
        norm(2)
        norm(3)

        with pe.Fori(0, 2) as i:
            group(G_U + i, Q_U + 2 * i, 8, xs_of, xs_wait(2))

        def ssm(j):
            def hook(slot):
                if slot == 0:
                    pe.wait_ge(S("m_bs"), j + 1)
                    for w in range(2):
                        op = nc.tensor.transpose(ps0[:, w * P:(w + 1) * P], bs[:, w, :], ident)
                    op.then_inc(S("mp_bt"), 1)
                for g in SUM_AT.get(slot, ()):
                    pe.wait_ge(S("m_cp"), j + 1)
                    pe.wait_ge(S("m_crs"), 8 * j + g + 1)
                    for w in range(2):
                        op = mm(ps2[:, 0:T], cpad[:, w, g * P:(g + 1) * P], crs[:, g % 2, w, :],
                                start=(g == 0 and w == 0), stop=(g == 7 and w == 1), skip_group_check=True)
                    op.then_inc(S("mp_y"), 1)
                if slot in SCAN_AT:
                    g = SCAN_AT[slot]
                    pe.wait_ge(S("m_lb"), j + 1)
                    for w in range(2):
                        op = mm((ps1, ps3)[g % 2][:, w * T:(w + 1) * T], lb[:, w, g, :], uT[:, j, :], start=True, stop=True)
                    op.then_inc(S("mp_bu"), 1)
            return hook

        with pe.Fori(0, SSM_CHUNKS) as j:
            group(G_MIX + j, Q_MIX + 2 * j, 8, xs_of, lambda sl: None, ssm(j))

        def glu_ready(sl):
            wait(pe, S("m_lo"), SSM_CHUNKS)

        for i in range(2):
            group(G_GLU + i, Q_GLU + i, 4, lambda k: hid2[:, 16 + k, :], glu_ready)
        pe.wait_ge(loads["second"], 64)
        pe.wait_ge(loads["stash"], 16 * 9)
        mm(ps0[0:8, :], rel_sb[:, :], L("onehot")[0:32, :], start=True, stop=True).then_inc(S("tp_set"), 1)
        with pe.Fori(0, 2) as i:
            group(G_QKV + i, Q_QKV + 2 * i, 8, xs_of, lambda sl: None)

        pe.wait_ge(loads["toep"], 16 * B_HEADS)
        for n in range(4):
            if n >= 1:
                pe.wait_ge(S("t_set"), n + 1)
            mm(ps0[:, :], L("flip"), toep[:, 2 * n:2 * n + 2, :], start=True, stop=True).then_inc(S("tp_set"), 1)
        pe.wait_ge(S("t_set"), 5)
        pe.wait_ge(loads["att"], 64)
        with pe.Fori(0, B_HEADS // 2) as pair:
            for s in range(2):
                h, (b0, b1, _, _), (qv, *_) = 2 * pair + s, ATT_BANKS[s], ATT_BUFS[s]
                pe.wait_ge(S("t_qv"), h + 1)
                mm(b0[:, 0:P], qv[:, 0, 0:P], att[:, 3 * h + 1, 0:P], start=True, stop=True)
                mm(b0[:, P:3 * P], qv[:, 0, P:T], att[:, 3 * h + 1, :], start=True, stop=True
                   ).then_inc(S("tp_s"), 1)
                for c in range(2):
                    op = nc.tensor.transpose(b1[:, c * P:(c + 1) * P], qv[:, 1, c * P:(c + 1) * P], ident)
                op.then_inc(S("tp_vn"), 1)
            for s in range(2):
                h, b2, sb = 2 * pair + s, ATT_BANKS[s][2], ATT_BUFS[s][1]
                pe.wait_ge(S("t_p"), h + 1)
                for j in range(3):
                    op = nc.tensor.transpose(b2[:, j * P:(j + 1) * P], sb[:, j * P:(j + 1) * P], ident)
                op.then_inc(S("tp_pt"), 1)
            for s in range(2):
                h, b3, (_, _, pt, vn, _, _) = 2 * pair + s, ATT_BANKS[s][3], ATT_BUFS[s]
                pe.wait_ge(S("t_pt"), h + 1)
                mm(b3[:, 0:T], vn[:, 0:P], pt[:, 0:T], start=True, stop=False, skip_group_check=True)
                mm(b3[:, P:T], vn[:, P:T], pt[:, T:T + P], start=False, stop=True, skip_group_check=True
                   ).then_inc(S("tp_o"), 1)

        def ssm_in(sl):
            wait(pe, S("glu_lo"), 2)

        def att_in(sl):
            wait(pe, S("t_lo"), B_HEADS)

        pe.wait_ge(S("t_y"), B_HEADS)
        with pe.Fori(0, 4) as i:
            group(G_MRG + 3 * i, Q_MRG + 4 * i, 4, lambda k: hid2[:, k, :], ssm_in)
            group(G_MRG + 3 * i + 1, Q_MRG + 4 * i + 1, 8, xs_of, lambda sl: None)
            group(G_MRG + 3 * i + 2, Q_MRG + 4 * i + 3, 4, lambda k: hid2[:, 8 + k, :], att_in)
            ada_sum(A_MRG + i)

        def mrg_ready(sl):
            if sl % 2 == 0:
                wait(pe, S("mrg_lo"), sl // 2 + 1)

        with pe.Fori(0, 4) as i:
            group(G_WO + i, Q_WO + 2 * i, 8, lambda k: hid2[:, 16 + k, :], mrg_ready)
            ada_sum(A_WO + i)
        norm(4)
        with pe.Fori(0, FF_QUARTERS) as c:
            with pe.Fori(0, 4) as i:
                group(G_FF + 8 * c + i, Q_FF + 16 * c + 2 * i, 8, xs_of, xs_wait(3))

            with pe.Fori(0, 4) as i:
                def ff_ready(sl):
                    if sl % 2 == 0:
                        pe.wait_ge(S("ff_lo"), 4 * c + sl // 2 + 1)
                group(G_FF + 8 * c + 4 + i, Q_FF + 16 * c + 8 + 2 * i, 8, lambda k: hid2[:, k, :], ff_ready)
        norm(5)

    @block.scalar
    def _(act):
        A = nc.scalar.activation
        steps = [0]

        def link(op):
            steps[0] += 1
            op.then_inc(act_step, 1)
            act.wait_ge(act_step, steps[0])

        def restart():
            act.sem_clear(act_step)
            steps[0] = 0

        def split(q, slot, _):
            act.wait_ge(raw_in[slot], 16 * (q + 1))
            if not (isinstance(q, int) and q == 0):
                act.wait_ge(slab_used, 4 * q + slot - 3)
            A(wh[:, slot, :], raw[:, slot, :], ACT.Copy).then_inc(hi_ready, 1)

        def evac(g, q_end):
            for n in range(SLAB_N):
                if n < SLAB_N - 1:
                    act.wait_ge(bank_ready, 3 * g + n + 1)
                else:
                    act.wait_ge(slab_used, 4 * q_end)
                wait(act, bank_freed, 4 * g + n - 3)
                A(tmp[:, n, :], G[n][:, T:2 * T], ACT.Copy).then_inc(tmp_ready, 1)

        def norm(n, m=None):
            y = norm_bufs[n][1]
            if n == 3:
                for q in range(4):
                    wait(act, x_ready, X_READY[2] + q + 1)
                    wait(act, norm_sq, SQ_BEFORE[3] + q)
                    A(y[:, :, :], x[:, 4 * q:4 * q + 4, :], ACT.Square).then_inc(S("sq_act"), 1)
            for q in range(4):
                act.wait_ge(norm_y, 4 * m + q + 1)
                o = xs[:, 4 * q:4 * q + 4, 0:T]
                if shift_of(n) is None:
                    A(o, y[:, :, :], ACT.Copy).then_inc(norm_hi, 1)
                else:
                    for j in range(4):
                        k = 4 * q + j
                        op = A(o[:, j, :], y[:, j, :], ACT.Identity, bias=shift_of(n)[:, k:k + 1])
                    op.then_inc(norm_hi, 1)

        for slot in range(AHEAD):
            split(0, slot, POOL_ALL)
        norm(0, 0)

        def gates(step):
            if step == 0:
                act.wait_ge(loads["hyb"], 32)
                A(wabh[:, :, :], wab_at[:, :, :], ACT.Copy).then_inc(S("gate_act"), 1)
            elif step == 1:
                act.wait_ge(S("gate_dve"), 2)
                A(gt[:, 1, :], gt[:, 0, :], ACT.Exp, scale=-1.0).then_inc(S("gate_act"), 1)
                A(gt[:, 3, :], gt[:, 2, :], ACT.Exp, scale=-1.0).then_inc(S("gate_act"), 1)
                A(gt[:, 5, :], V("a_log"), ACT.Exp).then_inc(S("gate_act"), 1)
            elif step == 2:
                act.wait_ge(S("gate_dve"), 3)
                A(gt[:, 3, :], gt[:, 3, :], ACT.Ln).then_inc(S("gate_act"), 1)
            elif step == 3:
                act.wait_ge(S("gate_dve"), 5)
                A(bexp[:, :, :], gcum[:, :, :], ACT.Exp).then_inc(S("gate_act"), 1)
                A(kdecf[:, :, :], kdecf[:, :, :], ACT.Exp).then_inc(S("gate_act"), 1)

        def conv(slot, h):
            if slot == 26:
                act.wait_ge(S("d_conv"), h + 1)
                A(th[:, :, :], qkv[:, :, :], ACT.Tanh, scale=0.5).then_inc(S("a_tanh"), 1)
            elif slot == 30:
                act.wait_ge(S("d_silu"), h + 1)
                A(sqq[:, 0:2, :], qkv[:, 0:2, :], ACT.Square).then_inc(S("d_sq"), 1)

        def delta(s, it):
            if s == 0:
                act.wait_ge(bank_freed, 12 * it + 8)
                A(th[:, 2:4, :], zz[:, :, :], ACT.Tanh, scale=0.5).then_inc(S("a_z"), 1)
            elif s == 1:
                act.wait_ge(S("d_gm"), it + 1)
                A(eg[:, :, :], ps1[:, :].rearrange("p (v c i) -> p v c i", v=2, c=2)[:, :, 1, :],
                  ACT.Exp).then_inc(S("a_eg"), 1)
                for j in range(4):
                    v, c = j // 2, j % 2
                    A(gA[:, j, :], gA[:, j, :], ACT.Exp, bias=ngcum[:, 2 * it + v, c:c + 1])
                    op = A(gB[:, j, :], gB[:, j, :], ACT.Exp, scale=-1.0, bias=gcum[:, 2 * it + v, c:c + 1])
                op.then_inc(S("a_dec"), 1)
            elif s == 3:
                act.wait_ge(S("p_nat"), it + 1)
                for j in range(4):
                    v, c = j // 2, j % 2
                    A(kb[:, j, :], ps0[:, c * P:(c + 1) * P], ACT.Copy, scale=bexp[:, 2 * it + v, c:c + 1])
                    A(rhsv[:, j, :], ps1[:, j * P:(j + 1) * P], ACT.Copy, scale=bhalf[:, 2 * it + v, c:c + 1])
                for v in range(2):
                    op = A(kd[:, v, :], ps0[:, 0:P], ACT.Copy, scale=kdecf[:, 2 * it + v, 0:1])
                op.then_inc(S("a_nat"), 1)
            elif 5 <= s < 23 and (s - 5) % 3 == 2:
                lv = (s - 5) // 3 + 1
                act.wait_ge(S("p_E"), 6 * it + lv)
                A(Em[:, :, :], ps1[:, :], ACT.Copy).then_inc(S("a_E"), 1)
            elif s == 23:
                act.wait_ge(S("p_v0"), it + 1)
                A(vn0[:, :, :], ps2[:, 0:2 * P], ACT.Copy)
                A(wTn[:, :, :], ps2[:, 2 * P:4 * P], ACT.Copy, scale=-1.0).then_inc(S("a_v0"), 1)
            elif s == 26:
                act.wait_ge(S("p_o"), it + 1)
                A(osb[:, :, :], ps1[:, :], ACT.Copy)
                A(sqo[:, :, :], ps1[:, :], ACT.Square).then_inc(S("a_o"), 1)
            elif s == 28:
                act.wait_ge(S("ya"), it + 1)
                A(hid[:, bass.ds(2 * it, 2), 0:T], yh[:, :, :].rearrange("p j i -> p (j i)"), ACT.Copy
                  ).then_inc(S("ya_hi"), 1)

        def attn(k, it):
            if k == 0:
                act.wait_ge(bank_freed, 12 * it + 12)
                A(bth[:, :], bb[:, 5, :], ACT.Tanh, scale=0.5).then_inc(S("ba_z"), 1)
            elif k == 2:
                act.wait_ge(S("bp_vn"), it + 1)
                A(vnat[:, :], ps3[:, 0:T], ACT.Copy).then_inc(S("b_vn"), 1)
            elif k == 5:
                act.wait_ge(S("b_mx"), it + 1)
                A(Sb[:, :, 0:P], Sb[:, :, 0:P], ACT.Exp, bias=smx[:, 0:1], accum_out=smx[:, 2:3])
                A(Sb[:, :, P:3 * P], Sb[:, :, P:3 * P], ACT.Exp, bias=smx[:, 1:2],
                  accum_out=smx[:, 3:4]).then_inc(S("ba_e"), 1)
            elif k == 6:
                act.wait_ge(S("bp_pt"), it + 1)
                A(PT[:, :], ps3[:, 0:384], ACT.Copy).then_inc(S("b_pt"), 1)
            elif k == 7:
                act.wait_ge(S("yb"), it + 1)
                A(hid[:, 16 + it, 0:T], yb[:, :], ACT.Copy).then_inc(S("yb_hi"), 1)

        def heads(it):
            def hook(slot):
                if slot in DELTA_AT:
                    delta(DELTA_AT[slot], it)
                if slot in ATTN_AT:
                    attn(ATTN_AT[slot], it)
            return hook

        def hyb(h, hook=None):
            for gi in range(3):
                walk(6 * h + 2 * gi, 8, split, hook, 16 * gi, POOL_ALL)
                evac(3 * h + gi, 6 * h + 2 * gi + 2)

        def first_head(slot):
            gates(GATE_ACT.get(slot))
            conv(slot, 0)

        def both(h):
            before = heads(h - 1)

            def hook(slot):
                before(slot)
                conv(slot, h)
            return hook

        hyb(0, first_head)
        with act.Fori(1, QK_HEADS) as h:
            hyb(h, both(h))
        for gi in range(4):
            walk(Q_OUTA + 2 * gi, 8, split, heads(7) if gi < 3 else None, 16 * gi, POOL_ALL,
                 None if gi < 3 else POOL_REST)
            if gi == 3:
                act.wait_ge(S("first_done"), 1)
                act.dma_start(x[:], ins["x"]).then_inc(loads["xback"], 16)
            evac(G_OUTA + gi, Q_OUTA + 2 * gi + 2)
        with act.Fori(0, 4) as i:
            walk(Q_OUTB + i, 4, split)
            evac(G_OUTB + i, Q_OUTB + i + 1)
        A(cth[:, :], V("c"), ACT.Tanh, scale=0.5).then_inc(S("ca_t"), 1)
        norm(1, 1)
        with act.Fori(0, N_SC_ITER) as j:
            for gi in range(4):
                walk(Q_SC + 8 * j + 2 * gi, 8, split)
                evac(G_SC + 4 * j + gi, Q_SC + 8 * j + 2 * gi + 2)
            act.wait_ge(bank_freed, 4 * (G_SC + 4 * j) + 16)
            A(sth[:, :, :], cc[:, :, :], ACT.Tanh, scale=0.5).then_inc(S("sca_t"), 1)
            act.wait_ge(S("sc_y"), j + 1)
            A(hid[:, bass.ds(4 * j, 4), 0:T], yv[:, :, :], ACT.Copy).then_inc(S("sc_hi"), 1)
        A(trg[:, 0, :], V("log_dt"), ACT.Exp).then_inc(S("s_act"), 1)
        act.wait_ge(S("s_dve"), 1)
        A(trg[:, 2, :], trg[:, 2, :], ACT.Exp).then_inc(S("s_act"), 1)
        A(trg[:, 3, :], trg[:, 3, :], ACT.Sin).then_inc(S("s_act"), 1)
        A(trg[:, 4, :], trg[:, 4, :], ACT.Sin).then_inc(S("s_act"), 1)
        with act.Fori(0, 4) as i:
            walk(Q_SCOUT + 3 * i, 12, split)
            evac(G_SCOUT + i, Q_SCOUT + 3 * i + 3)
        norm(3, 2)
        act.wait_ge(S("first_done"), 2)
        act.dma_start(ltc[:], ins["ltc"]).then_inc(loads["second"], 16)
        act.dma_start(bb1[:], ins["b1"]).then_inc(loads["second"], 16)
        act.dma_start(bb2[:], ins["b2"]).then_inc(loads["second"], 16)
        act.dma_start(sC[:], ins["c12"]).then_inc(loads["second"], 16)
        act.dma_start(rel_sb[:], ins["rel"]).then_inc(loads["stash"], 16)
        with act.Fori(0, 2) as i:
            walk(Q_U + 2 * i, 8, split)
            evac(G_U + i, Q_U + 2 * i + 2)

        def ssm(j):
            def hook(slot):
                if slot == 0:
                    A(bs[:, 0, :], bb1[:, bass.ds(j * P, P)], ACT.Copy)
                    A(bs[:, 1, :], bb2[:, bass.ds(j * P, P)], ACT.Copy).then_inc(S("m_bs"), 1)
                elif slot == 1:
                    for w in range(2):
                        op = A(cpad[:, w, :].rearrange("p (g s) -> p g s", s=144)[:, :, 0:16],
                               sC[:, w, bass.ds(8 * j, 8), :], ACT.Copy)
                    op.then_inc(S("m_cp"), 1)
            return hook

        act.wait_ge(S("s_dve"), 2)
        with act.Fori(0, SSM_CHUNKS) as j:
            walk(Q_MIX + 2 * j, 8, split, ssm(j))
            evac(G_MIX + j, Q_MIX + 2 * j + 2)
            act.wait_ge(bank_freed, 4 * (G_MIX + j) + 4)
            act.dma_start(stash[j], stage[:, :, :]).then_inc(loads["stash"], 16)
            act.wait_ge(S("m_in"), j + 1)
            A(yg[:, :], yg[:, :], ACT.Tanh, scale=math.sqrt(2 / math.pi)).then_inc(S("m_t"), 1)
            act.wait_ge(S("m_yg"), j + 1)
            A(hid2[:, 16 + j, 0:T], uT[:, j, :], ACT.Copy).then_inc(S("m_hi"), 1)
        for i in range(2):
            walk(Q_GLU + i, 4, split)
            evac(G_GLU + i, Q_GLU + i + 1)
            act.wait_ge(bank_freed, 4 * (G_GLU + i) + 4)
            for n in range(4):
                op = A(fxg[:, n, :], fxg[:, n, :], ACT.Tanh, scale=0.5, bias=bgh[:, 4 * i + n:4 * i + n + 1])
            op.then_inc(S("glu_t"), 1)
            act.wait_ge(S("glu_y"), i + 1)
            A(hid2[:, 4 * i:4 * i + 4, 0:T], uT[:, 4 * i:4 * i + 4, :], ACT.Copy).then_inc(S("glu_hi"), 1)
        act.wait_ge(loads["stash"], 16 * 9)
        act.wait_ge(S("glu_lo"), 2)
        for n in range(4):
            act.dma_start(att[:, 4 * n:4 * n + 4, :], stash[n]).then_inc(loads["att"], 16)
        def bias(slot):
            if slot == 4:
                act.wait_ge(S("t_set"), 1)
                act.dma_start(bias_dram, bvec[:]).then_inc(loads["bias"], 16)
            elif slot == 12:
                act.wait_ge(loads["bias"], 16)
                for h in range(B_HEADS):
                    act.dma_start(toep[:, h, :], bass.AP(tensor=bias_dram.tensor, offset=512 * h, ap=[[1, P], [1, 256]])
                                  ).then_inc(loads["toep"], 16)

        for i in range(2):
            walk(Q_QKV + 2 * i, 8, split, bias if i == 0 else None)
            evac(G_QKV + i, Q_QKV + 2 * i + 2)
        act.wait_ge(bank_freed, 4 * (G_QKV + 2))
        act.wait_ge(loads["att"], 64)
        act.wait_ge(S("t_set"), 5)
        with act.Fori(0, B_HEADS // 2) as pair:
            for s in range(2):
                h, qv = 2 * pair + s, ATT_BUFS[s][0]
                A(qv[:, 0, :], att[:, 3 * h, :], ACT.Copy, scale=DK_SCALE)
                A(qv[:, 1, :], att[:, 3 * h + 2, :], ACT.Copy).then_inc(S("t_qv"), 1)
            for s in range(2):
                h, (_, sb, _, vn, _, sm) = 2 * pair + s, ATT_BUFS[s]
                act.wait_ge(S("tp_vn"), h + 1)
                A(vn[:, :], ATT_BANKS[s][1][:, 0:T], ACT.Copy)
                act.wait_ge(S("t_mx"), h + 1)
                A(sb[:, 0:P], sb[:, 0:P], ACT.Exp, bias=sm[:, 0:1], accum_out=sm[:, 2:3])
                A(sb[:, P:3 * P], sb[:, P:3 * P], ACT.Exp, bias=sm[:, 1:2], accum_out=sm[:, 3:4]
                  ).then_inc(S("ta_e"), 1)
            for s in range(2):
                h, pt = 2 * pair + s, ATT_BUFS[s][2]
                act.wait_ge(S("tp_pt"), h + 1)
                A(pt[:, :], ATT_BANKS[s][2][:, 0:384], ACT.Copy).then_inc(S("t_pt"), 1)
            for s in range(2):
                h, yh_ = 2 * pair + s, ATT_BUFS[s][4]
                act.wait_ge(S("t_y"), h + 1)
                A(hid2[:, 8 + h, 0:T], yh_[:, :], ACT.Copy).then_inc(S("t_hi"), 1)
        with act.Fori(0, 4) as i:
            for gi, n, q in ((0, 4, 0), (1, 8, 1), (2, 4, 3)):
                def first_gate(slot):
                    if gi == 1 and slot == 2:
                        act.dma_start(macc[:, :, :], stash[4 + i]).then_inc(loads["gate"], 16)
                walk(Q_MRG + 4 * i + q, n, split, first_gate)
                evac(G_MRG + 3 * i + gi, Q_MRG + 4 * i + q + n // 4)
                if gi == 1:
                    act.wait_ge(bank_freed, 4 * (G_MRG + 3 * i + gi) + 4)
                    A(sg[:, :, :], sg[:, :, :], ACT.Tanh, scale=0.5)
                    act.wait_ge(loads["gate"], 16 * i + 16)
                    A(macc[:, :, :], macc[:, :, :], ACT.Tanh, scale=0.5).then_inc(S("mg_t"), 1)
            act.wait_ge(S("mrg"), i + 1)
            A(hid2[:, bass.ds(16 + 4 * i, 4), 0:T], macc[:, :, :], ACT.Copy).then_inc(S("mrg_hi"), 1)
        with act.Fori(0, 4) as i:
            walk(Q_WO + 2 * i, 8, split)
            evac(G_WO + i, Q_WO + 2 * i + 2)
        norm(4, 3)
        with act.Fori(0, FF_QUARTERS) as c:
            with act.Fori(0, 4) as i:
                walk(Q_FF + 16 * c + 2 * i, 8, split)
                evac(G_FF + 8 * c + i, Q_FF + 16 * c + 2 * i + 2)
                act.wait_ge(S("ff"), 4 * c + i + 1)
                A(hid2[:, bass.ds(4 * i, 4), 0:T], mt[:, :, :], ACT.Copy).then_inc(S("ff_hi"), 1)
            with act.Fori(0, 4) as i:
                walk(Q_FF + 16 * c + 8 + 2 * i, 8, split)
                evac(G_FF + 8 * c + 4 + i, Q_FF + 16 * c + 8 + 2 * i + 2)

    @block.gpsimd
    def _(pool):
        def split(q, slot, mine):
            if slot not in mine:
                return
            pool.wait_ge(hi_ready, 4 * q + slot + 1)
            if not (isinstance(q, int) and q == 0):
                pool.wait_ge(slab_used, 4 * q + slot - 3)
            nc.gpsimd.tensor_tensor(wl[:, slot, :], raw[:, slot, :], wh[:, slot, :].bitcast(F32),
                                    ALU.subtract).then_inc(lo_ready[slot], 1)

        def norm(n):
            pool.wait_ge(norm_var, n + 1)
            nc.gpsimd.tensor_tensor(rn[:, 0:2], nrm[:, 0:2], mhalf[:, 0:2], ALU.pow).then_inc(norm_rn, 1)

        def heads(it):
            def hook(slot):
                s = DELTA_AT.get(slot)
                if s == 0:
                    nc.gpsimd.tensor_copy(gsel[:, :], gcum_g(it))
                    pool.wait_ge(S("d_nrm"), it + 1)
                    nc.gpsimd.tensor_tensor(rn[:, 0:4], nrm[:, 0:4], mhalf[:, 0:4], ALU.pow
                                            ).then_inc(S("l_rn"), 1)
                elif s == 27:
                    pool.wait_ge(S("d_onrm"), it + 1)
                    nc.gpsimd.tensor_tensor(rn[:, 4:8], nrm[:, 4:8], mhalf[:, 4:8], ALU.pow
                                            ).then_inc(S("l_orn"), 1)
            return hook

        def gcum_g(it):
            return gnat[:, bass.ds(2 * it, 2), :]

        nc.gpsimd.memset(mhalf[:, :], -0.5).then_inc(S("l_half"), 1)
        pool.wait_ge(S("l_half"), 1)
        for slot in range(AHEAD):
            split(0, slot, POOL_ALL)
        norm(0)
        for gi in range(3):
            walk(2 * gi, 8, split, pool=POOL_ALL)
        pool.wait_ge(S("gate_pe"), 2)
        with pool.Fori(1, QK_HEADS) as h:
            for gi in range(3):
                walk(6 * h + 2 * gi, 8, split, heads(h - 1), 16 * gi, POOL_ALL)
        for gi in range(4):
            walk(Q_OUTA + 2 * gi, 8, split, heads(7) if gi < 3 else None, 16 * gi, POOL_ALL,
                 None if gi < 3 else POOL_REST)
        with pool.Fori(0, 4) as i:
            walk(Q_OUTB + i, 4, split)
        norm(1)
        with pool.Fori(0, 48) as i:
            walk(Q_SC + i, 4, split)
        with pool.Fori(0, 12) as i:
            walk(Q_SCOUT + i, 4, split)
        norm(2)
        norm(3)
        for i in range(2):
            walk(Q_U + 2 * i, 8, split, pool=POOL_ALL)
        def tables(j):
            def hook(slot):
                if slot not in TABLE_AT:
                    return
                g = TABLE_AT[slot]
                bc, bsn = (t[:, bass.ds(8 * j + g, 1), :].rearrange("p o a -> p (o a)").unsqueeze(2)
                           .to_broadcast([P, 16, 16]) for t in (cA, sA))
                sc_, ssn = (t[:, bass.ds(8 * j + g, 1), :].to_broadcast([P, 16, 16]) for t in (cB, sB))
                pc_, ps_ = prods[g % 2]
                v = [t[:, n, :].rearrange("p (a b) -> p a b", a=16) for t in (pc_, ps_) for n in range(2)]
                pool.wait_ge(S("m_tab"), 8 * j + g + 1)
                nc.gpsimd.tensor_tensor(v[0], bc, sc_, ALU.mult)
                nc.gpsimd.tensor_tensor(v[1], bsn, ssn, ALU.mult)
                nc.gpsimd.tensor_tensor(v[2], bsn, sc_, ALU.mult)
                nc.gpsimd.tensor_tensor(v[3], bc, ssn, ALU.mult).then_inc(S("m_prod"), 1)
            return hook

        pool.wait_ge(S("s_dve"), 3)
        with pool.Fori(0, SSM_CHUNKS) as j:
            walk(Q_MIX + 2 * j, 8, split, tables(j))
        for i in range(2):
            walk(Q_GLU + i, 4, split)
        with pool.Fori(0, 4) as i:
            walk(Q_QKV + i, 4, split)
        with pool.Fori(0, 16) as i:
            walk(Q_MRG + i, 4, split)
        with pool.Fori(0, 8) as i:
            walk(Q_WO + i, 4, split)
        norm(4)
        with pool.Fori(0, 64) as i:
            walk(Q_FF + i, 4, split)
        norm(5)

    @block.vector
    def _(dve):
        tt, ts, stt = nc.vector.tensor_tensor, nc.vector.tensor_scalar, nc.vector.scalar_tensor_tensor
        steps = [0]

        def link(op):
            steps[0] += 1
            op.then_inc(dve_step, 1)
            dve.wait_ge(dve_step, steps[0])

        def restart():
            dve.sem_clear(dve_step)
            steps[0] = 0

        def split(q, slot, pools):
            if slot in pools:
                return
            dve.wait_ge(hi_ready, 4 * q + slot + 1)
            if not (isinstance(q, int) and q == 0):
                dve.wait_ge(slab_used, 4 * q + slot - 3)
            tt(wl[:, slot, :], raw[:, slot, :], wh[:, slot, :].bitcast(F32), ALU.subtract).then_inc(lo_ready[slot], 1)

        def add(g, n, out):
            dve.wait_ge(tmp_ready, 4 * g + n + 1)
            tt(out, G[n][:, 0:T], tmp[:, n, :], ALU.add).then_inc(bank_freed, 1)

        def added(g):
            dve.wait_ge(bank_freed, 4 * g + 4)

        def low(out, y, hi):
            return tt(out, y, hi.bitcast(F32), ALU.subtract)

        def square_in(n, x4, count):
            acc, sq = norm_bufs[n]
            link(tt(sq[:, :, :], x4, x4, ALU.mult))
            tt(acc[:, :, :], acc[:, :, :], sq[:, :, :], ALU.add).then_inc(norm_sq, 1)
            dve.wait_ge(norm_sq, count)

        def norm(n, m, w, into=None):
            acc, y = norm_bufs[n]
            dve.wait_ge(norm_sum, n + 1)
            if n == 2:
                link(nc.vector.memset(acc[:, :, :], 0.0))

            def squares(q):
                dve.wait_ge(S("sq_act"), q + 1)
                tt(acc[:, :, :], acc[:, :, :], y[:, :, :], ALU.add).then_inc(norm_sq, 1)
                dve.wait_ge(norm_sq, SQ_BEFORE[3] + q + 1)

            ts(nrm[:, 0:2], ps0[:, 0:2], 1.0 / D, EPS, ALU.mult, ALU.add).then_inc(norm_var, 1)
            dve.wait_ge(norm_bc, n + 1)
            for q in range(4):
                if m is None:
                    for j in range(4):
                        k = 4 * q + j
                        op = stt(x[:, k, :], x[:, k, :], w[:, k:k + 1], ps1[:, 0:T], ALU.mult, ALU.mult)
                    op.then_inc(into, 1)
                    if n == 2 and q >= 1:
                        squares(q - 1)
                    if n == 2 and q == 3:
                        squares(3)
                    continue
                wait(dve, xs_ready, 4 * m + q)
                for j in range(4):
                    k = 4 * q + j
                    op = stt(y[:, j, :], x[:, k, :], w[:, k:k + 1], ps1[:, 0:T], ALU.mult, ALU.mult)
                op.then_inc(norm_y, 1)
                dve.wait_ge(norm_y, 4 * m + q + 1)
                dve.wait_ge(norm_hi, 4 * m + q + 1)
                hi = xs[:, 4 * q:4 * q + 4, 0:T]
                lo = xs[:, 4 * q:4 * q + 4, T:2 * T]
                if shift_of(n) is None:
                    op = low(lo, y[:, :, :], hi)
                else:
                    for j in range(4):
                        k = 4 * q + j
                        op = stt(lo[:, j, :], y[:, j, :], shift_of(n)[:, k:k + 1], hi[:, j, :].bitcast(F32),
                                 ALU.add, ALU.subtract)
                op.then_inc(xs_ready, 1)

        for slot in range(AHEAD):
            split(0, slot, POOL_ALL)
        link(nc.vector.memset(nsq0[:, :, :], 0.0))
        dve.wait_ge(loads["x"], 16)
        for q in range(4):
            square_in(0, x[:, 4 * q:4 * q + 4, :], q + 1)
        dve.wait_ge(loads["first"], 32)
        ts(dnh[:, 0:1], V("dn_norm"), 0.5, None, ALU.mult).then_inc(setup, 1)
        norm(0, 0, V("norm0"))
        link(nc.vector.memset(cb[:, :, :], 0.0))

        def ch(row):
            return gt[:, row, :].rearrange("p (c h) -> p c h", c=2)

        def hc(t):
            return t[:, :, :].rearrange("p h c -> p c h")

        def gates(step):
            if step == 0:
                dve.wait_ge(S("gate_act"), 1)
                tt(wabl[:, :, :], wab_at[:, :, :], wabh[:, :, :].bitcast(F32), ALU.subtract
                   ).then_inc(S("gate_dve"), 1)
            elif step == 1:
                dve.wait_ge(S("gate_pe"), 1)
                pv = ps0[:, 0:64].rearrange("p (c a h) -> p c a h", c=2, a=2)
                link(nc.vector.tensor_copy(ch(0), pv[:, :, 0, :]))
                link(tt(ch(4), pv[:, :, 1, :], V("dt_bias").rearrange("p (c h) -> p c h", c=2), ALU.add))
                stt(gt[:, 2, :], gt[:, 4, :], -1.0, gt[:, 4, :], ALU.mult, ALU.max).then_inc(S("gate_dve"), 1)
            elif step == 2:
                dve.wait_ge(S("gate_act"), 4)
                ts(gt[:, 3, :], gt[:, 3, :], 1.0, None, ALU.add).then_inc(S("gate_dve"), 1)
                link(ts(gt[:, 1, :], gt[:, 1, :], 1.0, None, ALU.add))
                link(nc.vector.reciprocal(gt[:, 1, :], gt[:, 1, :]))
                link(nc.vector.tensor_copy(hc(beta), ch(1)))
                link(ts(bhalf[:, :, :], beta[:, :, :], 0.5, None, ALU.mult))
            elif step == 3:
                dve.wait_ge(S("gate_act"), 5)
                link(stt(gt[:, 4, :], gt[:, 4, :], 0.0, gt[:, 3, :], ALU.max, ALU.add))
                stt(hc(gnat), ch(5), -1.0, ch(4), ALU.mult, ALU.mult).then_inc(S("gate_dve"), 1)
            elif step == 4:
                dve.wait_ge(S("gate_pe"), 2)
                pg = ps1[:, 0:64].rearrange("p (a c h) -> p a c h", a=2, c=2)
                link(nc.vector.tensor_copy(hc(gcum), pg[:, 0]))
                link(ts(ngcum[:, :, :], gcum[:, :, :], -1.0, None, ALU.mult))
                tt(hc(kdecf), pg[:, 1], hc(gcum), ALU.subtract).then_inc(S("gate_dve"), 1)
            elif step == 5:
                dve.wait_ge(S("gate_act"), 7)
                link(tt(bexp[:, :, :], bexp[:, :, :], beta[:, :, :], ALU.mult))

        def conv(slot, h):
            if slot in TAP_AT:
                tap = TAP_AT[slot]
                if tap == 0:
                    added(3 * h)
                for n in range(4):
                    w = V("dn_conv", 16 * h + 4 * n + tap, 1)
                    src = cb[:, n, 1 + tap:1 + tap + T]
                    if tap == 0:
                        op = ts(qkv[:, n, :], src, w, None, ALU.mult)
                    else:
                        op = stt(qkv[:, n, :], src, w, qkv[:, n, :], ALU.mult, ALU.add)
                if tap < 3:
                    link(op)
                else:
                    op.then_inc(S("d_conv"), 1)
            elif slot == 28:
                dve.wait_ge(S("a_tanh"), h + 1)
                stt(qkv[:, :, :], th[:, :, :], 1.0, qkv[:, :, :], ALU.add, ALU.mult).then_inc(S("d_silu"), 1)

        def delta(s, it):
            if s == 0:
                dve.wait_ge(S("p_norm"), it + 1)
                ts(nrm[:, 0:4], ps0[:, 0:4], 4 * EPS, None, ALU.add).then_inc(S("d_nrm"), 1)
                dve.wait_ge(S("a_z"), it + 1)
                stt(zs[:, :, :], th[:, 2:4, :], 1.0, zz[:, :, :], ALU.add, ALU.mult)
            elif s == 1:
                dve.wait_ge(S("p_bc"), it + 1)
                stt(qkv[:, 0, :], qkv[:, 0, :], DK_SCALE, ps0[:, 0:T], ALU.mult, ALU.mult)
                tt(qkv[:, 1, :], qkv[:, 1, :], ps0[:, T:2 * T], ALU.mult).then_inc(S("d_qk"), 1)
                pv = ps1[:, :].rearrange("p (j i) -> p j i", j=4)
                tt(gA[:, :, :], pv, four(H("mask_t")), ALU.add)
                tt(gB[:, :, :], pv, four(H("mask_s")), ALU.add).then_inc(S("d_gm"), 1)
            elif s == 2:
                dve.wait_ge(S("p_kk"), it + 1)
                dve.wait_ge(S("a_dec"), it + 1)
                for j in range(4):
                    v, c = j // 2, j % 2
                    stt(gB[:, j, :], ps2[:, c * P:(c + 1) * P], beta[:, 2 * it + v, c:c + 1], gB[:, j, :],
                        ALU.mult, ALU.mult)
                two = gA[:, :, :].rearrange("p (v c) i -> p v (c i)", v=2)
                tt(two, ps2[:, 2 * P:4 * P].unsqueeze(1).to_broadcast([P, 2, 2 * P]), two, ALU.mult)
                tt(qe[:, :, :], qkv[:, 0, P:T].unsqueeze(1).to_broadcast([P, 2, P]), eg[:, :, :], ALU.mult
                   ).then_inc(S("d_A"), 1)
            elif s == 4:
                dve.wait_ge(S("p_AT"), it + 1)
                pv = ps2[:, :].rearrange("p (j i) -> p j i", j=4)
                nc.vector.tensor_copy(AT[:, :, :], pv)
                tt(Dm[:, :, :], gB[:, :, :], four(H("nm0")), ALU.mult)
                link(tt(Em[:, :, :], pv, four(H("nm0t")), ALU.mult))
                tt(Dm[:, :, :], Dm[:, :, :], four(ident), ALU.add)
                tt(Em[:, :, :], Em[:, :, :], four(ident), ALU.add).then_inc(S("d_D"), 1)
            elif 5 <= s < 23:
                lv, part = (s - 5) // 3 + 1, (s - 5) % 3
                b = 1 << lv
                if part == 0:
                    dve.wait_ge(S("p_X"), 6 * it + lv)
                    mask = H("levels")[:, (lv - 1) * 64:lv * 64]
                    tt(Xm[:, :, :], ps0[:, 0:256].rearrange("p (j i) -> p j i", j=4), four(mask), ALU.mult
                       ).then_inc(S("d_X"), 1)
                elif part == 1:
                    dve.wait_ge(S("p_DX"), 6 * it + lv)
                    left = Dm[:, :, :].rearrange("p j (m two b) -> p j m two b", two=2, b=b)[:, :, :, 0, :]
                    pv = ps0[:, 256:512].rearrange("p (j m b) -> p j m b", j=4, b=b)
                    tt(left, pv, left, ALU.add).then_inc(S("d_D"), 1)
            elif s == 24:
                dve.wait_ge(S("p_S"), it + 1)
                nc.vector.tensor_copy(Sst[:, :, :], ps0[:, 0:2 * P].rearrange("p (v i) -> p v i", v=2)
                                      ).then_inc(S("d_S"), 1)
            elif s == 25:
                dve.wait_ge(S("p_v1"), it + 1)
                nc.vector.tensor_copy(vn1[:, :, :], ps0[:, 2 * P:4 * P].rearrange("p (v i) -> p v i", v=2)
                                      ).then_inc(S("d_v1"), 1)
            elif s == 27:
                dve.wait_ge(S("p_osum"), it + 1)
                ts(nrm[:, 4:8], ps2[:, 0:4], 1.0 / P, EPS, ALU.mult, ALU.add).then_inc(S("d_onrm"), 1)
            elif s == 28:
                dve.wait_ge(S("p_obc"), it + 1)
                yf = yh[:, :, :].rearrange("p j i -> p (j i)")
                link(stt(yf, osb[:, :, :].rearrange("p j i -> p (j i)"), dnh[:, 0:1], ps2[:, :], ALU.mult, ALU.mult))
                tt(yf, yf, zs[:, :, :].rearrange("p v i -> p (v i)"), ALU.mult).then_inc(S("ya"), 1)
                dve.wait_ge(S("ya_hi"), it + 1)
                yv2 = yh[:, :, :].rearrange("p (v c) i -> p v (c i)", v=2)
                low(hid[:, bass.ds(2 * it, 2), T:2 * T], yv2, hid[:, bass.ds(2 * it, 2), 0:T]
                    ).then_inc(S("ya_lo"), 1)

        def attn(k, it):
            if k < 2:
                dve.wait_ge(S("bp_rope"), 2 * it + k + 1)
                two = bb[0:32, 2 * k:2 * k + 2, :]
                cosb, sinb = (H(n)[0:32, :].unsqueeze(1).to_broadcast([32, 2, T]) for n in ("cos", "sin"))
                tt(rb[:, :, :], ps3[0:32, :].rearrange("p (a i) -> p a i", a=2), sinb, ALU.mult)
                tt(two, two, cosb, ALU.mult).then_inc(S("b_cos"), 1)
                dve.wait_ge(S("b_cos"), 2 * it + k + 1)
                tt(two, two, rb[:, :, :], ALU.add).then_inc(S("b_rope"), 1)
                if k == 0:
                    dve.wait_ge(S("ba_z"), it + 1)
                    stt(bzs[:, :], bth[:, :], 1.0, bb[:, 5, :], ALU.add, ALU.mult)
            elif k in (3, 4, 5):
                dve.wait_ge(S("bp_s"), 3 * it + k - 2)
                m = H("att_mask").rearrange("p (a i) -> p a i", a=3)
                if k == 3:
                    sel, pv = (slice(0, 3), slice(0, P)), ps3[:, 0:384].rearrange("p (a i) -> p a i", a=3)
                elif k == 4:
                    sel, pv = (slice(0, 2), slice(P, 3 * P)), ps3[:, :].rearrange("p (a i) -> p a i", a=2)
                else:
                    sel, pv = (slice(2, 3), slice(P, 3 * P)), ps3[:, 0:T].unsqueeze(1)
                stt(Sb[:, sel[0], sel[1]], pv, DK_SCALE, m[:, sel[0], sel[1]], ALU.mult, ALU.add
                    ).then_inc(S("b_s"), 1)
                if k == 5:
                    dve.wait_ge(S("b_s"), 3 * it + 3)
                    nc.vector.tensor_reduce(smx[:, 0:1], Sb[:, :, 0:P], AX.XY, ALU.max, negate=True)
                    nc.vector.tensor_reduce(smx[:, 1:2], Sb[:, :, P:3 * P], AX.XY, ALU.max, negate=True
                                            ).then_inc(S("b_mx"), 1)
            elif k == 8:
                dve.wait_ge(S("ba_e"), it + 1)
                nc.vector.reciprocal(smx[:, 4:6], smx[:, 2:4])
                tt(Pb[:, :], Sb[:, 0, :], Sb[:, 1, :], ALU.add).then_inc(S("b_p2"), 1)
                dve.wait_ge(S("b_p2"), 2 * it + 1)
                tt(Pb[:, :], Pb[:, :], Sb[:, 2, :], ALU.add).then_inc(S("b_p2"), 1)
                dve.wait_ge(S("b_p2"), 2 * it + 2)
                ts(Pb[:, 0:P], Pb[:, 0:P], smx[:, 4:5], None, ALU.mult)
                ts(Pb[:, P:3 * P], Pb[:, P:3 * P], smx[:, 5:6], None, ALU.mult).then_inc(S("b_p"), 1)
            elif k == 7:
                dve.wait_ge(S("bp_o"), it + 1)
                stt(yb[:, :], ps3[:, 0:T], 0.5, bzs[:, :], ALU.mult, ALU.mult).then_inc(S("yb"), 1)
                dve.wait_ge(S("yb"), it + 1)
                dve.wait_ge(S("yb_hi"), it + 1)
                low(hid[:, 16 + it, T:2 * T], yb[:, :], hid[:, 16 + it, 0:T]).then_inc(S("yb_lo"), 1)

        def heads(it):
            def hook(slot):
                if slot in DELTA_AT:
                    delta(DELTA_AT[slot], it)
                if slot in ATTN_AT:
                    attn(ATTN_AT[slot], it)
            return hook

        def hyb(h, hook=None):
            for gi in range(3):
                walk(6 * h + 2 * gi, 8, split, hook, 16 * gi, POOL_ALL)
                g = 3 * h + gi
                for n in range(4):
                    out = (cb[:, n, 4:4 + T] if gi == 0 else
                           (zz[:, n, :] if n < 2 else bb[:, n - 2, :]) if gi == 1 else bb[:, n + 2, :])
                    add(g, n, out)

        def first_head(slot):
            gates(GATE_DVE.get(slot))
            conv(slot, 0)

        def both(h):
            before = heads(h - 1)

            def hook(slot):
                before(slot)
                conv(slot, h)
            return hook

        hyb(0, first_head)
        dve.wait_ge(loads["hyb"], 32)
        with dve.Fori(1, QK_HEADS) as h:
            restart()
            hyb(h, both(h))
        restart()
        for gi in range(4):
            walk(Q_OUTA + 2 * gi, 8, split, heads(7) if gi < 3 else None, 16 * gi, POOL_ALL,
                 None if gi < 3 else POOL_REST)
            if gi == 3:
                dve.wait_ge(S("ya_lo"), 8)
                ts(smx[:, 0:1], smx[:, 0:1], 0.0, None, ALU.mult).then_inc(S("first_done"), 1)
            for n in range(4):
                add(G_OUTA + gi, n, xacc[:, 4 * gi + n, :])
        link(nc.vector.memset(cc[:, :, :], 0.0))
        with dve.Fori(0, 4) as i:
            restart()
            walk(Q_OUTB + i, 4, split)
            for n in range(4):
                add(G_OUTB + i, n, uu[:, n, :])
            added(G_OUTB + i)
            dve.wait_ge(loads["xback"], 16)
            k4 = bass.ds(4 * i, 4)
            link(tt(uu[:, :, :], uu[:, :, :], xacc[:, k4, :], ALU.add))
            tt(x[:, k4, :], x[:, k4, :], uu[:, :, :], ALU.add).then_inc(x_ready, 1)
            dve.wait_ge(x_ready, i + 1)
            square_in(1, x[:, k4, :], SQ_BEFORE[1] + i + 1)
        restart()
        dve.wait_ge(S("ca_t"), 1)
        link(stt(cact[:, :], cth[:, :], 1.0, V("c"), ALU.add, ALU.mult))
        link(ts(cact[:, :], cact[:, :], 0.5, None, ALU.mult))
        norm(1, 1, V("norm1"))
        link(nc.vector.memset(pc[:, :, :], 0.0))

        def ada(g, m):
            dve.wait_ge(ada_in[m % ADA_RING], 16 * (2 * g + m // ADA_RING + 1))
            for k in range(2):
                src, w = araw[:, m % ADA_RING, 512 * k:512 * k + 512], cact[:, 2 * m + k:2 * m + k + 1]
                if m == 0 and k == 0:
                    link(ts(aacc[:, :], src, w, None, ALU.mult))
                elif k == 0:
                    link(stt(aacc[:, :], src, w, aacc[:, :], ALU.mult, ALU.add))
                else:
                    stt(aacc[:, :], src, w, aacc[:, :], ALU.mult, ALU.add).then_inc(S("ada_used"), 1)
                    dve.wait_ge(S("ada_used"), 8 * g + m + 1)

        def beside(g, at, first=0):
            def hook(slot):
                if slot % 2 == 0 and first + slot // 2 in at:
                    ada(g, at[first + slot // 2])
            return hook

        def ada_out(g):
            dve.wait_ge(S("ada_sum"), g + 1)
            tt(mod[:, bass.ds(4 * g, 4)], ps2[:, 0:4], V("b_ada", 4 * g, 4), ALU.add).then_inc(S("ada_mod"), 1)

        with dve.Fori(0, N_SC_ITER) as j:
            restart()
            for gi in range(4):
                g = 4 * j + gi
                walk(Q_SC + 2 * g, 8, split, beside(2 * j + gi // 2, ADA_2, 8 * (gi % 2)))
                out = (cc, uu, uu, cc)[gi]
                for n in range(4):
                    add(G_SC + g, n, out[:, n, :])
                added(G_SC + g)
                if gi == 1:
                    link(tt(pc[:, :, 2:2 + T], uu[:, :, :], cc[:, :, :], ALU.mult))
                    for tap in range(3):
                        for n in range(4):
                            w, src = V("sc_conv", 12 * j + 3 * n + tap, 1), pc[:, n, tap:tap + T]
                            if tap == 0:
                                op = ts(yv[:, n, :], src, w, None, ALU.mult)
                            else:
                                op = stt(yv[:, n, :], src, w, yv[:, n, :], ALU.mult, ALU.add)
                        link(op)
                elif gi == 2:
                    link(tt(yv[:, :, :], yv[:, :, :], uu[:, :, :], ALU.mult))
                elif gi == 3:
                    dve.wait_ge(S("sca_t"), j + 1)
                    link(stt(cc[:, :, :], sth[:, :, :], 1.0, cc[:, :, :], ALU.add, ALU.mult))
                    stt(yv[:, :, :], yv[:, :, :], 0.5, cc[:, :, :], ALU.mult, ALU.mult).then_inc(S("sc_y"), 1)
                    dve.wait_ge(S("sc_y"), j + 1)
                    dve.wait_ge(S("sc_hi"), j + 1)
                    low(hid[:, bass.ds(4 * j, 4), T:2 * T], yv[:, :, :], hid[:, bass.ds(4 * j, 4), 0:T]
                        ).then_inc(S("sc_lo"), 1)
                if gi % 2 == 1:
                    ada_out(2 * j + gi // 2)
        R = [trg[:, r, :] for r in range(8)]
        are, aim = V("a_re"), V("a_im")
        magic = 12582912.0
        two_pi = 2 * math.pi
        c1 = 6.28125
        c2 = float(np.float32(two_pi - c1))
        c3 = two_pi - c1 - c2
        dve.wait_ge(S("s_act"), 1)
        link(tt(R[2], R[0], are, ALU.mult))
        link(tt(R[1], R[0], aim, ALU.mult))
        link(ts(R[5], R[1], 1 / two_pi, magic, ALU.mult, ALU.add))
        link(ts(R[5], R[5], -magic, None, ALU.add))
        for cw in (c1, c2, c3):
            link(stt(R[1], R[5], -cw, R[1], ALU.mult, ALU.add))
        link(ts(R[3], R[1], 3.1415925, -3.1415925, ALU.min, ALU.max))
        ts(R[4], R[3], 0.5, None, ALU.mult).then_inc(S("s_dve"), 1)
        dve.wait_ge(S("s_act"), 4)
        nc.vector.tensor_copy(mag[:, :], R[2])
        link(tt(R[5], R[4], R[4], ALU.mult))
        link(ts(R[6], R[5], -2.0, 1.0, ALU.mult, ALU.add))
        link(tt(R[5], R[5], R[2], ALU.mult))
        link(ts(R[7], R[2], -1.0, None, ALU.add))
        link(stt(R[5], R[5], -2.0, R[7], ALU.mult, ALU.add))
        link(tt(R[7], R[2], R[3], ALU.mult))
        link(tt(R[0], are, are, ALU.mult))
        link(tt(R[1], aim, aim, ALU.mult))
        link(tt(R[0], R[0], R[1], ALU.add))
        link(nc.vector.reciprocal(R[0], R[0]))
        link(tt(R[1], R[5], are, ALU.mult))
        link(tt(R[2], R[7], aim, ALU.mult))
        link(tt(R[1], R[1], R[2], ALU.add))
        link(tt(R[1], R[1], R[0], ALU.mult))
        link(tt(R[2], R[7], are, ALU.mult))
        link(tt(R[5], R[5], aim, ALU.mult))
        link(tt(R[2], R[2], R[5], ALU.subtract))
        link(tt(R[2], R[2], R[0], ALU.mult))
        restart()
        link(nc.vector.memset(cc[:, :, :], 0.0))
        with dve.Fori(0, 4) as i:
            restart()
            walk(Q_SCOUT + 3 * i, 12, split, beside(A_SCOUT + i, ADA_3))
            for n in range(4):
                add(G_SCOUT + i, n, uu[:, n, :])
            added(G_SCOUT + i)
            tt(x[:, bass.ds(4 * i, 4), :], x[:, bass.ds(4 * i, 4), :], uu[:, :, :], ALU.add).then_inc(x_ready, 1)
            dve.wait_ge(x_ready, i + 5)
            square_in(2, x[:, bass.ds(4 * i, 4), :], SQ_BEFORE[2] + i + 1)
            ada_out(A_SCOUT + i)
        restart()
        dve.wait_ge(S("ada_mod"), A_MRG)
        norm(2, None, V("final1"), x_ready)
        dve.wait_ge(x_ready, 12)
        link(stt(norm_g[:, :], mod[:, 16:32], 1.0, V("mix"), ALU.add, ALU.mult))
        norm(3, 2, norm_g)
        link(ts(bgh[:, :], V("b_glu"), 0.5, None, ALU.mult))
        dve.wait_ge(xs_ready, 12)
        ts(mhalf[:, 0:1], mhalf[:, 0:1], 1.0, None, ALU.mult).then_inc(S("first_done"), 1)

        def wide(r):
            return r.unsqueeze(2).to_broadcast([P, SSM_GROUPS, SSM_P])
        b1v, b2v = (t[:, :].rearrange("p (g q) -> p g q", q=SSM_P) for t in (bb1, bb2))
        T0, T1 = (lb[:, w, :, :].rearrange("p a b -> p (a b)").rearrange("p (g q) -> p g q", q=SSM_P)
                  for w in range(2))
        sgn, nsgn = L("sgn"), L("nsgn")
        ec, es, e3 = R[6], R[3], R[4]
        u1 = t1[:, :, :].rearrange("p a (g q) -> p (a g) q", q=8)
        u2 = prod0c[:, :, :].rearrange("p a (g q) -> p (a g) q", q=8)

        def double(cP, sP, n):
            def e(r):
                return r.unsqueeze(2).to_broadcast([P, SSM_GROUPS, n])
            link(tt(u1[:, :, 0:n], cP[:, :, 0:n], e(ec), ALU.mult))
            link(tt(u2[:, :, 0:n], sP[:, :, 0:n], e(es), ALU.mult))
            link(tt(cP[:, :, n:2 * n], u1[:, :, 0:n], u2[:, :, 0:n], ALU.subtract))
            link(tt(u1[:, :, 0:n], sP[:, :, 0:n], e(ec), ALU.mult))
            link(tt(u2[:, :, 0:n], cP[:, :, 0:n], e(es), ALU.mult))
            link(tt(sP[:, :, n:2 * n], u1[:, :, 0:n], u2[:, :, 0:n], ALU.add))
            link(tt(e3, ec, es, ALU.mult))
            link(tt(ec, ec, ec, ALU.mult))
            link(tt(es, es, es, ALU.mult))
            link(tt(ec, ec, es, ALU.subtract))
            link(ts(es, e3, 2.0, None, ALU.mult))

        def constants(step):
            if step == 0:
                for cP, sP in ((cB, sB), (cA, sA)):
                    nc.vector.memset(cP[:, :, 0:1], 1.0)
                    link(nc.vector.memset(sP[:, :, 0:1], 0.0))
                double(cB, sB, 1)
            elif step < 8:
                double(*((cB, sB) if step < 4 else (cA, sA)), 1 << step % 4)
            elif step == 8:
                dve.wait_ge(loads["second"], 64)
                link(ts(R[5], R[2], sgn, None, ALU.mult))
                link(ts(R[7], R[1], nsgn, None, ALU.mult))
                link(tt(T0, b1v, wide(R[1]), ALU.mult))
            elif step == 9:
                link(tt(T1, b2v, wide(R[5]), ALU.mult))
                link(tt(T0, T0, T1, ALU.add))
            elif step == 10:
                link(tt(T1, b2v, wide(R[7]), ALU.mult))
                link(tt(b2v, b1v, wide(R[2]), ALU.mult))
            elif step == 11:
                link(tt(b2v, b2v, T1, ALU.add))
                link(nc.vector.tensor_copy(b1v, T0))
            elif step == 12:
                link(ts(sC[:, 0, :, :], sC[:, 0, :, :], nsgn, None, ALU.mult))
                link(ts(sC[:, 1, :, :], sC[:, 1, :, :], -1.0, None, ALU.mult))
            elif step == 13:
                nc.vector.memset(cpad[:, :, :], 0.0).then_inc(S("s_dve"), 1)
                nc.vector.memset(rr[:, :], 0.0).then_inc(S("s_dve"), 1)
                nc.vector.memset(crs[:, 0, :, :], 0.0).then_inc(S("m_tab"), 2)
                dve.wait_ge(S("m_tab"), 2)
        for i in range(2):
            walk(Q_U + 2 * i, 8, split, lambda slot: constants(8 * i + slot // 2) if slot % 2 == 0 else None,
                 pool=POOL_ALL)
            for n in range(4):
                add(G_U + i, n, uT[:, 4 * i + n, :])

        def ssm(j):
            def hook(slot):
                if slot == 0:
                    dve.wait_ge(S("mp_bt"), j + 1)
                    for w in range(2):
                        op = tt(lb[:, w, :, :], ps0[:, w * P:(w + 1) * P].unsqueeze(1).to_broadcast([P, 8, P]),
                                L("emask").unsqueeze(2).to_broadcast([P, 8, P]), ALU.mult)
                    op.then_inc(S("m_lb"), 1)
                if slot in SCAN_AT:
                    g = SCAN_AT[slot]
                    pc_, ps_ = prods[g % 2]
                    dve.wait_ge(S("m_prod"), 8 * j + g + 1)
                    tt(CS[:, 0, :], pc_[:, 0, :], pc_[:, 1, :], ALU.subtract)
                    tt(CS[:, 1, :], ps_[:, 0, :], ps_[:, 1, :], ALU.add).then_inc(S("m_tab"), 1)
                    dve.wait_ge(S("m_tab"), 8 * j + g + 3)
                    dve.wait_ge(S("mp_bu"), 8 * j + g + 1)
                    link(tt(t1[:, :, :], (ps1, ps3)[g % 2][:, :].rearrange("p (w i) -> p w i", w=2), CS[:, :, :], ALU.mult))
                    link(tt(t1[:, 0, :], t1[:, 0, :], t1[:, 1, :], ALU.add))
                    link(nc.vector.tensor_tensor_scan(rr[:, :], mag[:, bass.ds(8 * j + g, 1)].to_broadcast([P, T]),
                                                      t1[:, 0, :], 0.0, ALU.mult, ALU.add))
                    tt(crs[:, g % 2, :, :], rr[:, :].unsqueeze(1).to_broadcast([P, 2, T]), CS[:, :, :], ALU.mult
                       ).then_inc(S("m_crs"), 1)
                    dve.wait_ge(S("m_crs"), 8 * j + g + 1)
            return hook

        with dve.Fori(0, SSM_CHUNKS) as j:
            restart()
            walk(Q_MIX + 2 * j, 8, split, ssm(j))
            dve.wait_ge(loads["stash"], 16 * j + 16)
            for n in range(4):
                add(G_MIX + j, n, stage[:, n, :])
            dve.wait_ge(S("mp_y"), 8 * j + 8)
            stt(yt[:, :], uT[:, j, :], V("ssm_d", j, 1), ps2[:, 0:T], ALU.mult, ALU.add).then_inc(S("m_y"), 1)
            dve.wait_ge(S("m_y"), j + 1)
            link(tt(yg[:, :], yt[:, :], yt[:, :], ALU.mult))
            link(ts(yg[:, :], yg[:, :], 0.044715, 1.0, ALU.mult, ALU.add))
            tt(yg[:, :], yg[:, :], yt[:, :], ALU.mult).then_inc(S("m_in"), 1)
            dve.wait_ge(S("m_t"), j + 1)
            link(stt(yt[:, :], yg[:, :], 1.0, yt[:, :], ALU.add, ALU.mult))
            ts(uT[:, j, :], yt[:, :], 0.5, None, ALU.mult).then_inc(S("m_yg"), 1)
            dve.wait_ge(S("m_yg"), j + 1)
            dve.wait_ge(S("m_hi"), j + 1)
            low(hid2[:, 16 + j, T:2 * T], uT[:, j, :], hid2[:, 16 + j, 0:T]).then_inc(S("m_lo"), 1)
        restart()
        for i in range(2):
            walk(Q_GLU + i, 4, split)
            for n in range(4):
                add(G_GLU + i, n, fxg[:, n, :])
            dve.wait_ge(S("glu_t"), i + 1)
            y4 = uT[:, 4 * i:4 * i + 4, :]
            link(ts(fxg[:, :, :], fxg[:, :, :], 1.0, 0.5, ALU.add, ALU.mult))
            tt(y4, y4, fxg[:, :, :], ALU.mult).then_inc(S("glu_y"), 1)
            dve.wait_ge(S("glu_y"), i + 1)
            dve.wait_ge(S("glu_hi"), i + 1)
            low(hid2[:, 4 * i:4 * i + 4, T:2 * T], y4, hid2[:, 4 * i:4 * i + 4, 0:T]).then_inc(S("glu_lo"), 1)
        dve.wait_ge(S("tp_set"), 1)
        tt(bvec[:, :], ps0[0:8, :], L("negrow")[0:8, :], ALU.add).then_inc(S("t_set"), 1)
        with dve.Fori(0, 2) as i:
            walk(Q_QKV + 2 * i, 8, split)
            for n in range(4):
                add(G_QKV + i, n, att[:, 16 + 4 * i + n, :])
        for n in range(4):
            dve.wait_ge(S("tp_set"), n + 2)
            nc.vector.tensor_copy(btab[:, 2 * n:2 * n + 2, :], ps0[:, :].rearrange("p (a i) -> p a i", a=2)
                                  ).then_inc(S("t_set"), 1)
        with dve.Fori(0, B_HEADS // 2) as pair:
            restart()
            for s in range(2):
                h, b0, (_, sb, _, _, _, sm) = 2 * pair + s, ATT_BANKS[s][0], ATT_BUFS[s]
                dve.wait_ge(S("tp_s"), h + 1)
                tt(sb[:, 0:P], b0[:, 0:P], btab[:, h, P:2 * P], ALU.add)
                link(tt(sb[:, P:3 * P], b0[:, P:3 * P], btab[:, h, :], ALU.add))
                nc.vector.tensor_reduce(sm[:, 0:1], sb[:, 0:P], AX.X, ALU.max, negate=True)
                nc.vector.tensor_reduce(sm[:, 1:2], sb[:, P:3 * P], AX.X, ALU.max, negate=True
                                        ).then_inc(S("t_mx"), 1)
            for s in range(2):
                h, (_, sb, _, _, _, sm) = 2 * pair + s, ATT_BUFS[s]
                dve.wait_ge(S("ta_e"), h + 1)
                link(nc.vector.reciprocal(sm[:, 4:6], sm[:, 2:4]))
                ts(sb[:, 0:P], sb[:, 0:P], sm[:, 4:5], None, ALU.mult)
                ts(sb[:, P:3 * P], sb[:, P:3 * P], sm[:, 5:6], None, ALU.mult).then_inc(S("t_p"), 1)
            for s in range(2):
                h, yh_ = 2 * pair + s, ATT_BUFS[s][4]
                dve.wait_ge(S("tp_o"), h + 1)
                nc.vector.tensor_copy(yh_[:, :], ATT_BANKS[s][3][:, 0:T]).then_inc(S("t_y"), 1)
            for s in range(2):
                h, yh_ = 2 * pair + s, ATT_BUFS[s][4]
                dve.wait_ge(S("t_y"), h + 1)
                dve.wait_ge(S("t_hi"), h + 1)
                low(hid2[:, 8 + h, T:2 * T], yh_[:, :], hid2[:, 8 + h, 0:T]).then_inc(S("t_lo"), 1)
        with dve.Fori(0, 4) as i:
            restart()
            for gi, n, q in ((0, 4, 0), (1, 8, 1), (2, 4, 3)):
                g = G_MRG + 3 * i + gi
                walk(Q_MRG + 4 * i + q, n, split, beside(A_MRG + i, ADA_2, 4 * q))
                for c in range(4):
                    add(g, c, (sg if gi == 1 else mt)[:, c, :])
                added(g)
                if gi == 1:
                    dve.wait_ge(S("mg_t"), i + 1)
                    ts(sg[:, :, :], sg[:, :, :], 1.0, 0.5, ALU.add, ALU.mult)
                    link(ts(macc[:, :, :], macc[:, :, :], 1.0, 0.5, ALU.add, ALU.mult))
                    link(tt(macc[:, :, :], mt[:, :, :], macc[:, :, :], ALU.mult))
                elif gi == 2:
                    link(tt(mt[:, :, :], mt[:, :, :], sg[:, :, :], ALU.mult))
                    tt(macc[:, :, :], macc[:, :, :], mt[:, :, :], ALU.add).then_inc(S("mrg"), 1)
                    dve.wait_ge(S("mrg"), i + 1)
                    dve.wait_ge(S("mrg_hi"), i + 1)
                    o = hid2[:, bass.ds(16 + 4 * i, 4), :]
                    low(o[:, :, T:2 * T], macc[:, :, :], o[:, :, 0:T]).then_inc(S("mrg_lo"), 1)
            ada_out(A_MRG + i)

        def gated_add(g, i, gate, before, the_norm, count):
            for n in range(4):
                add(g, n, fx[:, n, :])
            added(g)
            for n in range(4):
                xk = x[:, 4 * i + n, :]
                op = stt(xk, fx[:, n, :], mod[:, bass.ds(gate + 4 * i + n, 1)], xk, ALU.mult, ALU.add)
            op.then_inc(x_ready, 1)
            dve.wait_ge(x_ready, before + 1)
            square_in(the_norm, x[:, bass.ds(4 * i, 4), :], count)

        dve.wait_ge(S("mrg_lo"), 4)
        link(nc.vector.memset(macc[:, :, :], 0.0))
        with dve.Fori(0, 4) as i:
            restart()
            walk(Q_WO + 2 * i, 8, split, beside(A_WO + i, ADA_1))
            gated_add(G_WO + i, i, 32, X_READY[3] + i, 4, SQ_BEFORE[4] + i + 1)
            ada_out(A_WO + i)
        restart()
        dve.wait_ge(S("ada_mod"), ADA_GROUPS)
        link(stt(norm_g[:, :], mod[:, 64:80], 1.0, V("mlp"), ALU.add, ALU.mult))
        norm(4, 3, norm_g)
        with dve.Fori(0, FF_QUARTERS) as c:
            restart()
            link(nc.vector.memset(macc[:, :, :], 0.0))
            with dve.Fori(0, 4) as i:
                walk(Q_FF + 16 * c + 2 * i, 8, split)
                g = G_FF + 8 * c + i
                for n in range(4):
                    add(g, n, fx[:, n, :])
                added(g)
                stt(mt[:, :, :], fx[:, :, :], 0.0, fx[:, :, :], ALU.max, ALU.mult).then_inc(S("ff"), 1)
                dve.wait_ge(S("ff"), 4 * c + i + 1)
                dve.wait_ge(S("ff_hi"), 4 * c + i + 1)
                o = hid2[:, bass.ds(4 * i, 4), :]
                low(o[:, :, T:2 * T], mt[:, :, :], o[:, :, 0:T]).then_inc(S("ff_lo"), 1)
            with dve.Fori(0, 4) as i:
                restart()
                walk(Q_FF + 16 * c + 8 + 2 * i, 8, split)
                gated_add(G_FF + 8 * c + 4 + i, i, 80, X_READY[4] + 4 * c + i, 5, 21 + 4 * c + i)
        norm(5, None, V("final2"), S("out_ready"))


def _pad_cols(a, n=P):
    out = np.zeros((n, a.shape[1]), np.float32)
    out[:a.shape[0]] = a
    return out


def constant_tables():
    i = np.arange(P)
    r, c = i[:, None], i[None, :]
    f = np.float32
    cst = {"ident": np.eye(P, dtype=f), "upper": (r <= c).astype(f), "ones": np.ones((P, P), f)}
    levels = []
    for lv in range(1, 7):
        b = 1 << lv
        left = np.concatenate([np.arange(m, m + b) for m in range(0, P, 2 * b)])
        levels.append(-((r // (2 * b) == left[None, :] // (2 * b)) & (r % (2 * b) >= b)).astype(f))
    nm0 = -((r // 2 == c // 2) & (r == c + 1)).astype(f)
    t = np.arange(2 * P)
    q, k = t[:, None], t[None, :]
    blocks = []
    for window, dil in ((128, 1), (512, 4), (2048, 16)):
        rel = q - k
        ok = (rel >= 0) & (rel % dil == 0) & (rel <= window)
        m = np.where(ok, 0.0, NEG).astype(f)
        blocks += [m[0:P, 0:P], m[P:, 0:P], m[P:, P:]]
    half = 16
    inv = np.power(f(500000.0), -np.arange(half, dtype=f) * f(2.0) / f(32))
    ang = (np.arange(T, dtype=f)[:, None] * inv[None, :]).astype(f)
    cos, sin = np.cos(ang).astype(f).T, np.sin(ang).astype(f).T
    rot = np.zeros((32, 32), f)
    for d in range(half):
        rot[d + half, d] = -1.0
        rot[d, d + half] = 1.0
    hyc = {
        "mask_t": np.where(c >= r, 0.0, NEG).astype(f), "mask_s": np.where(c < r, 0.0, -NEG).astype(f),
        "nm0": nm0, "nm0t": nm0.T, "levels": np.concatenate(levels, 1),
        "att_mask": np.concatenate(blocks, 1), "cos": _pad_cols(np.concatenate([cos, cos])),
        "sin": _pad_cols(np.concatenate([sin, sin])), "rot": _pad_cols(rot),
    }
    rel = 255 - np.arange(512)
    n = np.maximum(rel, 0)
    nf = np.maximum(n, 1).astype(f)
    large = 16 + (np.log(nf / f(16)) / f(math.log(128 / 16)) * f(16)).astype(np.int32)
    bucket = np.where(n < 16, n, np.minimum(large, 31))
    onehot = ((np.arange(32)[:, None] == bucket[None, :]) & (rel >= 0)[None, :]).astype(f)
    negrow = np.tile(np.where(rel >= 0, 0.0, NEG).astype(f)[None, :], (8, 1))
    top = (i < 64)
    ltc = {
        "flip": np.eye(P, dtype=f)[::-1], "onehot": _pad_cols(onehot), "negrow": _pad_cols(negrow),
        "emask": (i[:, None] // 16 == np.arange(8)[None, :]).astype(f),
        "sgn": np.where(top, -1.0, 1.0).astype(f)[:, None], "nsgn": np.where(top, 1.0, -1.0).astype(f)[:, None],
    }
    out = []
    for tabs, widths in ((cst, CONST_WIDTHS), (hyc, HYB_CONST_WIDTHS), (ltc, LATE_CONST_WIDTHS)):
        for name, w in widths:
            assert tabs[name].shape == (P, w), (name, tabs[name].shape)
        out.append(np.ascontiguousarray(np.concatenate([tabs[name] for name, _ in widths], 1), dtype=f))
    return out


def slabs(w, k_chunks, col_chunks):
    kc, nc_ = w.shape[0] // P, w.shape[1] // P
    v = w.reshape(kc, P, nc_, P)[np.asarray(k_chunks)][:, :, np.asarray(col_chunks)]
    v = v.reshape(len(k_chunks) // SLAB_K, SLAB_K, P, len(col_chunks) // SLAB_N, SLAB_N * P)
    return np.ascontiguousarray(v.transpose(3, 0, 2, 1, 4)).reshape(-1, P, SLAB)


def columns(v):
    return v.reshape(-1, P).T


def lay_out(i):
    f = {k: np.asarray(v) for k, v in i.items()}
    hyb = f["hyb_w_in"][0]
    order = []
    conv_order = []
    for h in range(QK_HEADS):
        qkv = [h, 8 + h, 16 + 2 * h, 17 + 2 * h]
        conv_order += qkv
        order += qkv + [32 + 2 * h, 33 + 2 * h] + [48 + h, 56 + h, 64 + h, 72 + h, 80 + h, 88 + h]
    main = np.concatenate([hyb[:, :6144], hyb[:, 6176:]], axis=1)
    k16, k24 = list(range(16)), list(range(24))
    outa = list(range(0, 12)) + list(range(16, 20))
    outb = list(range(12, 16)) + list(range(20, 24))
    sc = f["sc_w_in"][0]
    sc_order = []
    for j in range(N_SC_ITER):
        for part in (1, 2, 0, 3):
            sc_order += [24 * part + 4 * j + n for n in range(4)]
    w2 = f["w_in_2"][0]
    qkv2 = [8 + 8 * a + h for h in range(8) for a in range(3)]
    stream = [slabs(main, k16, order), slabs(f["hyb_w_out"][0], outa, k16), slabs(f["hyb_w_out"][0], outb, k16),
              slabs(sc, k16, sc_order), slabs(f["sc_w_out"][0], k24, k16),
              slabs(w2, k16, list(range(8))), slabs(w2, k16, qkv2[:16] + list(range(32, 48))),
              slabs(f["w_glu_2"][0], list(range(8)), list(range(8))), slabs(w2, k16, qkv2[16:])]
    for g in range(4):
        cols = list(range(4 * g, 4 * g + 4))
        stream += [slabs(f["w_proj_ssm_2"][0], list(range(8)), cols),
                   slabs(w2, k16, [48 + c for c in cols]), slabs(f["w_proj_attn_2"][0], list(range(8)), cols)]
    stream.append(slabs(f["w_out_2"][0], k16, k16))
    for c in range(FF_QUARTERS):
        ks = list(range(16 * c, 16 * c + 16))
        stream += [slabs(f["w_ff1_2"][0], k16, ks), slabs(f["w_ff2_2"][0], ks, k16)]
    stream.append(stream[0][:RING])
    stacked = lambda a: np.concatenate([a.T, a.T])
    b_re, b_im = (f[n][0].transpose(1, 0, 2).reshape(64, -1) for n in ("ssm_b_re_2", "ssm_b_im_2"))
    c_re, c_im = (f[n][0].transpose(2, 0, 1) for n in ("ssm_c_re_2", "ssm_c_im_2"))
    row = lambda v: np.broadcast_to(v[None, :], (P, v.shape[0]))
    vecs = {
        "norm0": columns(f["norm_w"][0]), "norm1": columns(f["norm_w"][1]), "final1": columns(f["final_norm_w"]),
        "mix": columns(f["norm_mix_g_2"][0]), "mlp": columns(f["norm_mlp_g_2"][0]),
        "final2": columns(f["norm_final_g_2"]),
        "dn_conv": f["dn_conv_w"][0].reshape(32, P, 4)[np.asarray(conv_order)].transpose(1, 0, 2).reshape(P, -1),
        "sc_conv": f["sc_conv_w"][0].reshape(24, P, 3).transpose(1, 0, 2).reshape(P, -1),
        "dn_norm": f["dn_norm_w"][0][:, None], "ssm_d": columns(f["ssm_d_2"][0]),
        "b_glu": columns(f["b_glu_2"][0]), "c": columns(f["c_2"][0]), "b_ada": columns(f["b_ada_2"][0]),
        "a_log": row(np.concatenate([f["dn_a_log"][0]] * 2)), "dt_bias": row(np.concatenate([f["dn_dt_bias"][0]] * 2)),
        "a_re": stacked(f["ssm_a_re_2"][0]), "a_im": stacked(f["ssm_a_im_2"][0]), "log_dt": row(f["ssm_log_dt_2"][0]),
    }
    cst, hyc, ltc = constant_tables()
    c_ = np.ascontiguousarray
    return {
        "stream": np.concatenate(stream, 0),
        "ada": slabs(f["w_ada_2"][0], k16, list(range(96))),
        "x": c_(f["x"][0].T.reshape(KC, P, T).transpose(1, 0, 2)),
        "vec": c_(np.concatenate([vecs[n] for n, _ in VEC_WIDTHS], 1)),
        "cst": cst, "hyc": hyc, "ltc": ltc,
        "wab": c_(hyb[:, 6144:6176].reshape(KC, P, 32).transpose(1, 0, 2)),
        "b1": c_(np.concatenate([b_re, b_im])), "b2": c_(np.concatenate([b_im, b_re])),
        "c12": c_(np.stack([np.concatenate([c_re, c_im]), np.concatenate([c_im, c_re])], 1)),
        "rel": c_(f["rel_bias_2"]),
    }


def kernel(**inputs):
    from contextlib import ExitStack

    import concourse.bacc as bacc
    from concourse.bass_utils import run_bass_kernel_spmd

    nc = bacc.Bacc("TRN2", target_bir_lowering=False, num_devices=1)
    arrays = lay_out(inputs)
    ins = {n: nc.dram_tensor(f"in_{n}", a.shape, F32, kind="ExternalInput").ap() for n, a in arrays.items()}
    out = nc.dram_tensor("out", (P, KC, T), F32, kind="ExternalOutput").ap()
    with ExitStack() as stack:
        program(nc, stack, ins, out)
    r = run_bass_kernel_spmd(nc, [{f"in_{n}": a for n, a in arrays.items()}], core_ids=[0])
    got = r.results[0]["out"]
    return np.ascontiguousarray(got.transpose(1, 0, 2).reshape(1, D, T).transpose(0, 2, 1))
```
